# Optimizing a Trainium2 kernel written in Bass

```python
import jax, jax.numpy as jnp
from jax import lax
import numpy as np
import math
import jax
import jax.numpy as jnp

D_MODEL = 1024
BATCH = 1
SEQ = 512
DEPTH = 2

N_MIXERS = 2
RMS_EPS = 1e-6
L2_EPS = 1e-6

GDN_HEADS = 8
GDN_DK = 128
GDN_DV = 128
GDN_CONV = 4
GDN_CHUNK = 64
GDN_QK_WIDTH = GDN_HEADS * GDN_DK
GDN_V_WIDTH = GDN_HEADS * GDN_DV
GDN_IN_WIDTH = 2 * GDN_QK_WIDTH + 2 * GDN_V_WIDTH + 2 * GDN_HEADS

DIL_GROUPS = ((128, 1), (512, 4), (2048, 16))
N_DIL_GROUPS = 3
DIL_HEADS_PER_GROUP = 8
DIL_HEAD_DIM = 64
DIL_TOTAL_HEADS = N_DIL_GROUPS * DIL_HEADS_PER_GROUP
DIL_IN_WIDTH = 3 * DIL_TOTAL_HEADS * DIL_HEAD_DIM
DIL_OUT_WIDTH = DIL_HEADS_PER_GROUP * DIL_HEAD_DIM
ALIBI_MAX_BIAS = 8.0

FFN_HIDDEN = -(-8 * D_MODEL // (3 * 256)) * 256


def _rmsnorm(x, w):
    xf = x.astype(jnp.float32)
    y = xf * lax.rsqrt(jnp.mean(xf * xf, axis=-1, keepdims=True) + RMS_EPS)
    return (y * w.astype(jnp.float32)).astype(x.dtype)

def _l2norm(x):
    xf = x.astype(jnp.float32)
    return xf * lax.rsqrt(jnp.sum(xf * xf, axis=-1, keepdims=True) + L2_EPS)

def _causal_depthwise_conv(x, w):
    c = x.shape[-1]
    return lax.conv_general_dilated(
        x, w[:, None, :].astype(x.dtype), window_strides=(1,),
        padding=[(w.shape[0] - 1, 0)], dimension_numbers=("NWC", "WIO", "NWC"),
        feature_group_count=c)

def _chunk_gated_delta_rule(q, k, v, g, beta):
    b, s, h, dk = q.shape
    dv = v.shape[-1]
    c = GDN_CHUNK
    nc = s // c

    def chunks(t):
        return t.reshape(b, nc, c, h, -1).transpose(0, 3, 1, 2, 4)

    q, k, v = chunks(q), chunks(k), chunks(v)
    g = g.reshape(b, nc, c, h).transpose(0, 3, 1, 2)
    beta = beta.reshape(b, nc, c, h).transpose(0, 3, 1, 2)
    gc = jnp.cumsum(g, axis=-1)
    idx = jnp.arange(c)
    causal = idx[:, None] >= idx[None, :]
    strict = idx[:, None] > idx[None, :]
    decay = jnp.exp(jnp.where(causal, gc[..., :, None] - gc[..., None, :], -jnp.inf))
    kk = jnp.einsum("bhncd,bhnmd->bhncm", k, k)
    a_mat = jnp.where(strict, kk * beta[..., :, None] * decay, 0.0) + jnp.eye(c, dtype=jnp.float32)
    rhs = jnp.concatenate([v * beta[..., None], k * (beta * jnp.exp(gc))[..., None]], axis=-1)
    sol = lax.linalg.triangular_solve(a_mat, rhs, left_side=True, lower=True, unit_diagonal=True)
    u, w = sol[..., :dv], sol[..., dv:]
    qk = jnp.einsum("bhncd,bhnmd->bhncm", q, k) * decay
    q_dec = q * jnp.exp(gc)[..., None]
    k_tail = k * jnp.exp(gc[..., -1:] - gc)[..., None]
    c_dec = jnp.exp(gc[..., -1])
    xs = (jnp.moveaxis(qk, 2, 0), jnp.moveaxis(q_dec, 2, 0), jnp.moveaxis(k_tail, 2, 0),
          jnp.moveaxis(u, 2, 0), jnp.moveaxis(w, 2, 0), jnp.moveaxis(c_dec, 2, 0))

    def step(state, inp):
        qk_c, qd_c, kt_c, u_c, w_c, cd_c = inp
        v_new = u_c - jnp.einsum("bhck,bhkv->bhcv", w_c, state)
        o_c = (jnp.einsum("bhck,bhkv->bhcv", qd_c, state)
               + jnp.einsum("bhcm,bhmv->bhcv", qk_c, v_new))
        state = state * cd_c[..., None, None] + jnp.einsum("bhck,bhcv->bhkv", kt_c, v_new)
        return state, o_c

    s0 = jnp.zeros((b, h, dk, dv), jnp.float32)
    _, o = lax.scan(step, s0, xs)
    return o.transpose(1, 0, 3, 2, 4).reshape(b, s, h, dv)

def _gated_deltanet(h, w_in, conv_w, a_log, dt_bias, norm_w, w_out):
    b, s, _ = h.shape
    proj = h @ w_in
    n_qkv = 2 * GDN_QK_WIDTH + GDN_V_WIDTH
    qkv = jax.nn.silu(_causal_depthwise_conv(proj[..., :n_qkv], conv_w))
    z = proj[..., n_qkv:n_qkv + GDN_V_WIDTH].reshape(b, s, GDN_HEADS, GDN_DV)
    a = proj[..., n_qkv + GDN_V_WIDTH:n_qkv + GDN_V_WIDTH + GDN_HEADS].astype(jnp.float32)
    bb = proj[..., n_qkv + GDN_V_WIDTH + GDN_HEADS:].astype(jnp.float32)
    q = _l2norm(qkv[..., :GDN_QK_WIDTH].reshape(b, s, GDN_HEADS, GDN_DK)) * (GDN_DK ** -0.5)
    k = _l2norm(qkv[..., GDN_QK_WIDTH:2 * GDN_QK_WIDTH].reshape(b, s, GDN_HEADS, GDN_DK))
    v = qkv[..., 2 * GDN_QK_WIDTH:].reshape(b, s, GDN_HEADS, GDN_DV).astype(jnp.float32)
    beta = jax.nn.sigmoid(bb)
    g = -jnp.exp(a_log.astype(jnp.float32)) * jax.nn.softplus(a + dt_bias.astype(jnp.float32))
    o = _chunk_gated_delta_rule(q, k, v, g, beta)
    o = o * lax.rsqrt(jnp.mean(o * o, axis=-1, keepdims=True) + RMS_EPS)
    o = o * norm_w.astype(jnp.float32) * jax.nn.silu(z.astype(jnp.float32))
    return o.astype(h.dtype).reshape(b, s, GDN_V_WIDTH) @ w_out

def _dilated_group_attention(q, k, v, slopes, dilation, span):
    b, s, h, dh = q.shape
    n_sub = -(-s // dilation)
    nb = -(-n_sub // span)
    l_pad = nb * span
    t_pad = l_pad * dilation

    def to_blocks(t):
        t = jnp.pad(t, ((0, 0), (0, t_pad - s), (0, 0), (0, 0)))
        t = t.reshape(b, l_pad, dilation, h, dh).transpose(0, 2, 1, 3, 4)
        return t.reshape(b, dilation, nb, span, h, dh)

    def with_prev(t):
        prev = jnp.pad(t, ((0, 0), (0, 0), (1, 0), (0, 0), (0, 0), (0, 0)))[:, :, :-1]
        return jnp.concatenate([prev, t], axis=3)

    def from_blocks(t):
        e = t.shape[-1]
        t = t.reshape(b, dilation, l_pad, h, e).transpose(0, 2, 1, 3, 4)
        return t.reshape(b, t_pad, h, e)[:, :s]

    qb = to_blocks(q)
    kb = with_prev(to_blocks(k))
    vb = with_prev(to_blocks(v))
    scores = jnp.einsum("brnqhd,brnkhd->brnhqk", qb, kb,
                        preferred_element_type=jnp.float32) * (dh ** -0.5)
    qi = jnp.arange(span)
    kj = jnp.arange(2 * span)
    steps = qi[:, None] + span - kj[None, :]
    key_sub = jnp.arange(nb)[:, None] * span - span + kj[None, :]
    valid = ((steps >= 0) & (steps <= span))[None] & (key_sub >= 0)[:, None, :]
    bias = -slopes.astype(jnp.float32)[:, None, None] * (steps * dilation).astype(jnp.float32)
    logits = jnp.where(valid[:, None], scores + bias, -jnp.inf)
    m = jnp.max(logits, axis=-1, keepdims=True)
    p = jnp.exp(logits - m)
    l = jnp.sum(p, axis=-1)
    o = jnp.einsum("brnhqk,brnkhd->brnqhd", p, vb.astype(jnp.float32))
    o = o / l.transpose(0, 1, 2, 4, 3)[..., None]
    m_out = from_blocks(m[..., 0].transpose(0, 1, 2, 4, 3)[..., None])[..., 0]
    l_out = from_blocks(l.transpose(0, 1, 2, 4, 3)[..., None])[..., 0]
    return from_blocks(o), m_out, l_out

def _dilated_attention(h, w_in, q_norm, k_norm, w_out):
    b, s, _ = h.shape
    qkv = (h @ w_in).reshape(b, s, 3, N_DIL_GROUPS, DIL_HEADS_PER_GROUP, DIL_HEAD_DIM)
    q = _rmsnorm(qkv[:, :, 0], q_norm)
    k = _rmsnorm(qkv[:, :, 1], k_norm)
    v = qkv[:, :, 2]
    slopes = (2.0 ** (-ALIBI_MAX_BIAS * jnp.arange(1, DIL_TOTAL_HEADS + 1, dtype=jnp.float32)
                      / DIL_TOTAL_HEADS)).reshape(N_DIL_GROUPS, DIL_HEADS_PER_GROUP)
    outs, maxes, dens = [], [], []
    for gi, (window, dilation) in enumerate(DIL_GROUPS):
        o_g, m_g, l_g = _dilated_group_attention(q[:, :, gi], k[:, :, gi], v[:, :, gi],
                                                 slopes[gi], dilation, window // dilation)
        outs.append(o_g)
        maxes.append(m_g)
        dens.append(l_g)
    o_all = jnp.stack(outs)
    m_all = jnp.stack(maxes)
    l_all = jnp.stack(dens)
    wts = l_all * jnp.exp(m_all - jnp.max(m_all, axis=0, keepdims=True))
    o = jnp.sum(wts[..., None] * o_all, axis=0) / jnp.sum(wts, axis=0)[..., None]
    return o.astype(h.dtype).reshape(b, s, DIL_OUT_WIDTH) @ w_out

def _swiglu(h, w_in, w_out):
    gu = h @ w_in
    return (jax.nn.silu(gu[..., :FFN_HIDDEN]) * gu[..., FFN_HIDDEN:]) @ w_out

def first_inputs(seed: int = 0) -> dict:
    key = jax.random.key(seed)
    ks = jax.random.split(key, 16)
    f32 = jnp.float32
    n_a = (DEPTH + 1) // 2
    n_b = DEPTH // 2
    out_scale = (2.0 * DEPTH) ** -0.5

    def nrm(k, shape, scale):
        return jax.random.normal(k, shape, f32) * scale

    def gain(k, shape):
        return 1.0 + 0.02 * jax.random.normal(k, shape, f32)

    dt = jnp.exp(jax.random.uniform(ks[6], (n_a, GDN_HEADS), f32, np.log(1e-3), np.log(1e-1)))
    return {
        "x": nrm(ks[0], (BATCH, SEQ, D_MODEL), 1.0),
        "norm_mix": gain(ks[1], (DEPTH, D_MODEL)),
        "norm_ffn": gain(ks[2], (DEPTH, D_MODEL)),
        "gdn_w_in": nrm(ks[3], (n_a, D_MODEL, GDN_IN_WIDTH), D_MODEL ** -0.5),
        "gdn_conv_w": nrm(ks[4], (n_a, GDN_CONV, 2 * GDN_QK_WIDTH + GDN_V_WIDTH), GDN_CONV ** -0.5),
        "gdn_a_log": jnp.log(jax.random.uniform(ks[5], (n_a, GDN_HEADS), f32, 1.0, 16.0)),
        "gdn_dt_bias": dt + jnp.log(-jnp.expm1(-dt)),
        "gdn_norm_w": gain(ks[7], (n_a, GDN_DV)),
        "gdn_w_out": nrm(ks[8], (n_a, GDN_V_WIDTH, D_MODEL), GDN_V_WIDTH ** -0.5 * out_scale),
        "dil_w_in": nrm(ks[9], (n_b, D_MODEL, DIL_IN_WIDTH), D_MODEL ** -0.5),
        "dil_q_norm": gain(ks[10], (n_b, DIL_HEAD_DIM)),
        "dil_k_norm": gain(ks[11], (n_b, DIL_HEAD_DIM)),
        "dil_w_out": nrm(ks[12], (n_b, DIL_OUT_WIDTH, D_MODEL), DIL_OUT_WIDTH ** -0.5 * out_scale),
        "ffn_w_in": nrm(ks[13], (DEPTH, D_MODEL, 2 * FFN_HIDDEN), D_MODEL ** -0.5),
        "ffn_w_out": nrm(ks[14], (DEPTH, FFN_HIDDEN, D_MODEL), FFN_HIDDEN ** -0.5 * out_scale),
    }

def first_block(x, norm_mix, norm_ffn, gdn_w_in, gdn_conv_w, gdn_a_log, gdn_dt_bias, gdn_norm_w,
              gdn_w_out, dil_w_in, dil_q_norm, dil_k_norm, dil_w_out, ffn_w_in, ffn_w_out):
    for i in range(DEPTH):
        j = i // N_MIXERS
        hn = _rmsnorm(x, norm_mix[i])
        if i % N_MIXERS == 0:
            x = x + _gated_deltanet(hn, gdn_w_in[j], gdn_conv_w[j], gdn_a_log[j], gdn_dt_bias[j],
                                    gdn_norm_w[j], gdn_w_out[j])
        else:
            x = x + _dilated_attention(hn, dil_w_in[j], dil_q_norm[j], dil_k_norm[j], dil_w_out[j])
        x = x + _swiglu(_rmsnorm(x, norm_ffn[i]), ffn_w_in[i], ffn_w_out[i])
    return x


GRID_W = 64
CTX_LEN = 256
HEAD_DIM = 64
NA_HEADS = 6
NA_WIN_R = 8
NA_WIN_C = 16
SG_GROUPS = 4
SG_CHUNK = 128
GQA_Q_HEADS = 6
GQA_KV_HEADS = 2
Q_BLOCK = 128
ROPE_THETA = 10000.0

D_A = NA_HEADS * HEAD_DIM
D_B = SG_GROUPS * HEAD_DIM
D_C = GQA_Q_HEADS * HEAD_DIM
D_MIX = D_A + D_B + D_C
D_KV_C = GQA_KV_HEADS * HEAD_DIM
IN_SIZES = (D_A, D_A, D_A, 2 * D_B, D_C, D_KV_C, D_KV_C)
D_IN = 3 * D_A + 2 * D_B + D_C + 2 * D_KV_C
D_FF = int(math.ceil(8 * D_MODEL / 3 / 256)) * 256
N_MOD = 6
ALPHA = (2 * DEPTH) ** 0.25
BETA = (8 * DEPTH) ** -0.25
LN_EPS = 1e-6


def layer_norm(x):
    xf = x.astype(jnp.float32)
    mu = jnp.mean(xf, -1, keepdims=True)
    var = jnp.mean(jnp.square(xf - mu), -1, keepdims=True)
    return ((xf - mu) * lax.rsqrt(var + LN_EPS)).astype(x.dtype)

def rms_norm(x, g):
    xf = x.astype(jnp.float32)
    y = xf * lax.rsqrt(jnp.mean(xf * xf, -1, keepdims=True) + LN_EPS)
    return y.astype(x.dtype) * g

def modulate(x, shift, scale):
    return layer_norm(x) * (1 + scale) + shift

def split_cols(p, sizes):
    out, off = [], 0
    for s in sizes:
        out.append(p[..., off:off + s])
        off += s
    return out

def heads(t, n):
    return t.reshape(t.shape[0], t.shape[1], n, HEAD_DIM)

def axial_rope_tables(n_tokens, dtype):
    t = jnp.arange(n_tokens, dtype=jnp.int32)
    row = (t // GRID_W).astype(jnp.float32)
    col = (t % GRID_W).astype(jnp.float32)
    n_freq = HEAD_DIM // 4
    inv = 1.0 / (ROPE_THETA ** (jnp.arange(n_freq, dtype=jnp.float32) / n_freq))
    ang = jnp.stack([row[:, None] * inv, col[:, None] * inv], axis=1)
    return jnp.cos(ang).astype(dtype), jnp.sin(ang).astype(dtype)

def apply_axial_rope(x, cos, sin):
    n_freq = HEAD_DIM // 4
    xr = x.reshape(*x.shape[:-1], 2, 2, n_freq)
    x1, x2 = xr[..., 0, :], xr[..., 1, :]
    c, s = cos[:, None], sin[:, None]
    out = jnp.stack([x1 * c - x2 * s, x2 * c + x1 * s], axis=-2)
    return out.reshape(x.shape)

def attend(q, k, v):
    scale = q.shape[-1] ** -0.5
    s = jnp.einsum('bqkgd,bskd->bkgqs', q, k) * scale
    p = jax.nn.softmax(s.astype(jnp.float32), axis=-1).astype(v.dtype)
    return jnp.einsum('bkgqs,bskd->bqkgd', p, v)

def neighbourhood_attention(q, k, v, k_ctx, v_ctx, rpb):
    B, S, H, Dh = q.shape
    rows = S // GRID_W
    kr = min(NA_WIN_R, rows)
    kcw = NA_WIN_C
    scale = Dh ** -0.5
    qg = q.reshape(B, rows, GRID_W, H, Dh)
    kg = k.reshape(B, rows, GRID_W, H, Dh)
    vg = v.reshape(B, rows, GRID_W, H, Dh)
    r_idx = jnp.arange(rows, dtype=jnp.int32)
    row_start = jnp.clip(r_idx - kr // 2, 0, rows - kr)
    c_idx = jnp.arange(GRID_W, dtype=jnp.int32)
    col_start = jnp.clip(c_idx - kcw // 2, 0, GRID_W - kcw)
    col_win = col_start[:, None] + jnp.arange(kcw, dtype=jnp.int32)[None, :]
    dc = col_win - c_idx[:, None] + (NA_WIN_C - 1)
    n_loc = kr * kcw

    def one_row(args):
        q_row, rs, r = args
        k_rows = lax.dynamic_slice_in_dim(kg, rs, kr, axis=1)
        v_rows = lax.dynamic_slice_in_dim(vg, rs, kr, axis=1)
        k_win = k_rows[:, :, col_win]
        v_win = v_rows[:, :, col_win]
        s_loc = jnp.einsum('bqhd,brqchd->bhqrc', q_row, k_win) * scale
        dr = rs + jnp.arange(kr, dtype=jnp.int32) - r + (NA_WIN_R - 1)
        bias = rpb[:, dr][:, :, dc]
        s_loc = s_loc + jnp.transpose(bias, (0, 2, 1, 3))[None]
        s_ctx = jnp.einsum('bqhd,blhd->bhql', q_row, k_ctx) * scale
        s = jnp.concatenate([s_loc.reshape(B, H, GRID_W, n_loc), s_ctx], axis=-1)
        p = jax.nn.softmax(s.astype(jnp.float32), axis=-1).astype(v.dtype)
        p_loc = p[..., :n_loc].reshape(B, H, GRID_W, kr, kcw)
        p_ctx = p[..., n_loc:]
        return (jnp.einsum('bhqrc,brqchd->bqhd', p_loc, v_win)
                + jnp.einsum('bhql,blhd->bqhd', p_ctx, v_ctx))

    out = lax.map(one_row, (jnp.transpose(qg, (1, 0, 2, 3, 4)), row_start, r_idx))
    return jnp.transpose(out, (1, 0, 2, 3, 4)).reshape(B, S, H, Dh)

def gqa_latent(q, k, v, k_ctx, v_ctx):
    B, S, Hq, Dh = q.shape
    G = Hq // GQA_KV_HEADS
    nb = S // Q_BLOCK
    qb = jnp.transpose(q.reshape(B, nb, Q_BLOCK, GQA_KV_HEADS, G, Dh), (1, 0, 2, 3, 4, 5))
    k_all = jnp.concatenate([k, k_ctx], axis=1)
    v_all = jnp.concatenate([v, v_ctx], axis=1)
    out = lax.map(lambda qblk: attend(qblk, k_all, v_all), qb)
    return jnp.transpose(out, (1, 0, 2, 3, 4, 5)).reshape(B, S, Hq, Dh)

def spatial_gating(z, w_s, b_s, g_sgu):
    B, N, _ = z.shape
    u, v = z[..., :D_B], z[..., D_B:]
    v = layer_norm(v) * g_sgu
    vc = v.reshape(B, N // SG_CHUNK, SG_CHUNK, SG_GROUPS, HEAD_DIM)
    mixed = jnp.einsum('gpq,bnqgc->bnpgc', w_s, vc) + jnp.transpose(b_s)[None, None, :, :, None]
    return u * mixed.reshape(B, N, D_B)

def merge_groups(o_a, o_b, o_c, g_out):
    B, N = o_b.shape[0], o_b.shape[1]
    return jnp.concatenate([
        rms_norm(o_a.reshape(B, N, D_A), g_out[:D_A]),
        rms_norm(o_b, g_out[D_A:D_A + D_B]),
        rms_norm(o_c.reshape(B, N, D_C), g_out[D_A + D_B:]),
    ], axis=-1)

def mixing_sublayer(h, hc, w_in, rpb, w_s, b_s, g_sgu, g_q, g_k, g_out, w_o, need_ctx_out):
    B, S, _ = h.shape
    qa, ka, va, zb, qc, kc, vc = split_cols(h @ w_in, IN_SIZES)
    qa_x, ka_x, va_x, zb_x, qc_x, kc_x, vc_x = split_cols(hc @ w_in, IN_SIZES)
    cos, sin = axial_rope_tables(S, h.dtype)
    ka_x, va_x = heads(ka_x, NA_HEADS), heads(va_x, NA_HEADS)
    kc_x = rms_norm(heads(kc_x, GQA_KV_HEADS), g_k)
    vc_x = heads(vc_x, GQA_KV_HEADS)
    o_a = neighbourhood_attention(heads(qa, NA_HEADS), heads(ka, NA_HEADS), heads(va, NA_HEADS),
                                  ka_x, va_x, rpb)
    o_b = spatial_gating(jax.nn.gelu(zb), w_s, b_s, g_sgu)
    q_c = apply_axial_rope(rms_norm(heads(qc, GQA_Q_HEADS), g_q), cos, sin)
    k_c = apply_axial_rope(rms_norm(heads(kc, GQA_KV_HEADS), g_k), cos, sin)
    o_c = gqa_latent(q_c, k_c, heads(vc, GQA_KV_HEADS), kc_x, vc_x)
    y = merge_groups(o_a, o_b, o_c, g_out) @ w_o
    if not need_ctx_out:
        return y, None
    L = hc.shape[1]
    o_ax = attend(heads(qa_x, NA_HEADS)[:, :, :, None], ka_x, va_x)
    o_bx = spatial_gating(jax.nn.gelu(zb_x), w_s, b_s, g_sgu)
    q_cx = rms_norm(heads(qc_x, GQA_Q_HEADS), g_q).reshape(
        B, L, GQA_KV_HEADS, GQA_Q_HEADS // GQA_KV_HEADS, HEAD_DIM)
    o_cx = attend(q_cx, kc_x, vc_x)
    yc = merge_groups(o_ax, o_bx, o_cx, g_out) @ w_o
    return y, yc

def swiglu(h, w_in, w_out):
    a, b = h @ w_in[:, :D_FF], h @ w_in[:, D_FF:]
    return (jax.nn.silu(a) * b) @ w_out

def second_inputs(seed: int = 0) -> dict:
    key = jax.random.key(seed)
    ks = jax.random.split(key, 24)
    n = jax.random.normal
    f = jnp.float32
    return {
        "x": n(ks[0], (BATCH, SEQ, D_MODEL), f),
        "c": n(ks[1], (BATCH, D_MODEL), f),
        "ctx": n(ks[2], (BATCH, CTX_LEN, D_MODEL), f),
        "c_ctx": n(ks[3], (D_MODEL,), f),
        "w_mod": n(ks[4], (DEPTH, D_MODEL, N_MOD * D_MODEL), f) * (0.5 * D_MODEL ** -0.5),
        "b_mod": n(ks[5], (DEPTH, N_MOD * D_MODEL), f) * 0.02,
        "w_in": n(ks[6], (DEPTH, D_MODEL, D_IN), f) * D_MODEL ** -0.5,
        "rpb": n(ks[7], (DEPTH, NA_HEADS, 2 * NA_WIN_R - 1, 2 * NA_WIN_C - 1), f) * 0.02,
        "w_s": n(ks[8], (DEPTH, SG_GROUPS, SG_CHUNK, SG_CHUNK), f) * SG_CHUNK ** -0.5,
        "b_s": n(ks[9], (DEPTH, SG_GROUPS, SG_CHUNK), f) * 0.02,
        "g_sgu": 1.0 + 0.02 * n(ks[10], (DEPTH, D_B), f),
        "g_q": 1.0 + 0.02 * n(ks[11], (DEPTH, HEAD_DIM), f),
        "g_k": 1.0 + 0.02 * n(ks[12], (DEPTH, HEAD_DIM), f),
        "g_out": 1.0 + 0.02 * n(ks[13], (DEPTH, D_MIX), f),
        "w_o": n(ks[14], (DEPTH, D_MIX, D_MODEL), f) * (D_MIX ** -0.5 * BETA),
        "ln1_g": 1.0 + 0.02 * n(ks[15], (DEPTH, D_MODEL), f),
        "ln1_b": 0.02 * n(ks[16], (DEPTH, D_MODEL), f),
        "w_ffn_in": n(ks[17], (DEPTH, D_MODEL, 2 * D_FF), f) * D_MODEL ** -0.5,
        "w_ffn_out": n(ks[18], (DEPTH, D_FF, D_MODEL), f) * (D_FF ** -0.5 * BETA),
        "ln2_g": 1.0 + 0.02 * n(ks[19], (DEPTH, D_MODEL), f),
        "ln2_b": 0.02 * n(ks[20], (DEPTH, D_MODEL), f),
    }

def second_block(x, c, ctx, c_ctx, w_mod, b_mod, w_in, rpb, w_s, b_s, g_sgu, g_q, g_k, g_out, w_o,
              ln1_g, ln1_b, w_ffn_in, w_ffn_out, ln2_g, ln2_b):
    sc = jax.nn.silu(c)
    sc_ctx = jax.nn.silu(c_ctx)
    for l in range(DEPTH):
        need_ctx_out = l < DEPTH - 1
        mod = split_cols((sc @ w_mod[l] + b_mod[l])[:, None, :], (D_MODEL,) * N_MOD)
        mod_x = split_cols(sc_ctx @ w_mod[l] + b_mod[l], (D_MODEL,) * N_MOD)
        sh1, sc1, g1, sh2, sc2, g2 = mod
        sh1x, sc1x, g1x, sh2x, sc2x, g2x = mod_x
        h = modulate(x, sh1, sc1)
        hc = modulate(ctx, sh1x, sc1x)
        y, yc = mixing_sublayer(h, hc, w_in[l], rpb[l], w_s[l], b_s[l], g_sgu[l], g_q[l], g_k[l],
                                g_out[l], w_o[l], need_ctx_out)
        x = layer_norm(ALPHA * x + g1 * y) * ln1_g[l] + ln1_b[l]
        x = layer_norm(ALPHA * x + g2 * swiglu(modulate(x, sh2, sc2), w_ffn_in[l], w_ffn_out[l])) \
            * ln2_g[l] + ln2_b[l]
        if need_ctx_out:
            ctx = layer_norm(ALPHA * ctx + g1x * yc) * ln1_g[l] + ln1_b[l]
            ctx = layer_norm(ALPHA * ctx + g2x * swiglu(modulate(ctx, sh2x, sc2x), w_ffn_in[l],
                                                         w_ffn_out[l])) * ln2_g[l] + ln2_b[l]
    return x


def setup_inputs(seed=0):
    out = dict(first_inputs(seed))
    for name, value in second_inputs(seed + 1).items():
        if name != "x":
            out[name + "_2"] = value
    return out


def reference(
    x, norm_mix, norm_ffn, gdn_w_in, gdn_conv_w, gdn_a_log, gdn_dt_bias, gdn_norm_w, gdn_w_out,
    dil_w_in, dil_q_norm, dil_k_norm, dil_w_out, ffn_w_in, ffn_w_out, c_2, ctx_2, c_ctx_2,
    w_mod_2, b_mod_2, w_in_2, rpb_2, w_s_2, b_s_2, g_sgu_2, g_q_2, g_k_2, g_out_2, w_o_2,
    ln1_g_2, ln1_b_2, w_ffn_in_2, w_ffn_out_2, ln2_g_2, ln2_b_2,
):
    x = first_block(
        x, norm_mix, norm_ffn, gdn_w_in, gdn_conv_w, gdn_a_log, gdn_dt_bias, gdn_norm_w,
        gdn_w_out, dil_w_in, dil_q_norm, dil_k_norm, dil_w_out, ffn_w_in, ffn_w_out,
    )
    return second_block(
        x, c_2, ctx_2, c_ctx_2, w_mod_2, b_mod_2, w_in_2, rpb_2, w_s_2, b_s_2, g_sgu_2, g_q_2,
        g_k_2, g_out_2, w_o_2, ln1_g_2, ln1_b_2, w_ffn_in_2, w_ffn_out_2, ln2_g_2, ln2_b_2,
    )


_drawn_inputs = setup_inputs


def setup_inputs(seed=0):
    import zlib

    import numpy as np

    out = dict(_drawn_inputs(seed))
    spreads = {}
    factors = {'norm_mix': 4.924,
     'norm_ffn': 4.906,
     'gdn_norm_w': 8.0,
     'dil_q_norm': 8.0,
     'dil_k_norm': 8.0,
     'b_mod_2': 3.411,
     'rpb_2': 40.598,
     'b_s_2': 31.312,
     'g_sgu_2': 31.084,
     'g_q_2': 8.0,
     'g_k_2': 8.0,
     'g_out_2': 8.0}
    for name, (base, spread) in spreads.items():
        noise = np.random.default_rng([zlib.crc32(name.encode()), seed]).standard_normal(out[name].shape)
        drawn = base * np.exp(spread * noise) if base else spread * noise
        out[name] = jnp.asarray(drawn.astype(out[name].dtype))
    for name, factor in factors.items():
        out[name] = (out[name] * factor).astype(out[name].dtype)
    return out
```

```python
from contextlib import ExitStack

import numpy as np

import concourse.bass as bass
from concourse import mybir

F32 = mybir.dt.float32
ALU = mybir.AluOpType
ACT = mybir.ActivationFunctionType
AX = mybir.AxisListType.X

S, LC, D = 512, 256, 1024
FF = 2816
ALPHA = 4.0 ** 0.25
EPS = 1e-6
BIG = 1e30
NS = 4

C_NMIX, C_NFFN, C_GNW, C_CONV, C_DQ, C_DK, C_ALOG, C_DT = 0, 16, 32, 33, 129, 130, 131, 132
C_C, C_BMOD, C_GQ, C_GK, C_GOUT, C_LN, C_BS = 133, 149, 245, 247, 249, 265, 329
NCOL = 337
K_ID, K_ONE, K_BONE, K_EPS, K_RES = 0, 128, 256, 384, 392
K_GDN = K_RES
N_GDN = 7 * 128 + 128 + 512
K_DIL = K_GDN + N_GDN
N_DIL = 1280
K_NA = K_DIL + N_DIL
N_NA = 64 + 1024 + 128 + 128
NK = K_NA + N_NA


def constants():
    f = np.float32
    k = np.zeros((128, NK), f)
    i = np.arange(128)[:, None]
    j = np.arange(128)[None, :]
    k[:, K_ID:K_ID + 128] = i == j
    k[:, K_ONE:K_ONE + 128] = 1
    k[:, K_BONE:K_BONE + 128] = i // 64 == j // 64
    for n, e in enumerate((EPS, 64 * EPS, ALPHA * ALPHA * EPS, 1.0, 128 * EPS)):
        k[:, K_EPS + n] = e
    g = K_GDN
    for n in range(7):
        b = 1 << n
        k[:, g:g + 128] = (i // (2 * b) == j // (2 * b)) & (i % (2 * b) >= b) & (j % (2 * b) < b)
        g += 128
    k[:, g:g + 128] = i <= j
    g += 128
    k[:, g:g + 512] = np.arange(512) % 128 != 0
    g = K_DIL
    d0 = 128 + i - np.arange(256)[None, :]
    k[:, g:g + 256] = np.where((d0 >= 0) & (d0 <= 128), -d0, -BIG)
    d = 384 + i - np.arange(512)[None, :]
    k[:, g + 256:g + 768] = np.where((d >= 0) & (d % 4 == 0), -d, -BIG)
    k[:, g + 768:g + 1280] = np.where((d >= 0) & (d % 16 == 0), -d, -BIG)
    g = K_NA
    c, cc = i % 64, np.arange(64)[None, :]
    st = np.clip(c - 8, 0, 48)
    k[:, g:g + 64] = np.where((cc >= st) & (cc < st + 16), 0, -BIG)
    g += 64
    t = np.arange(512)
    inv = (f(1.0) / (f(10000.0) ** (np.arange(16, dtype=f) / f(16)))).astype(f)
    p = np.arange(128) % 64
    pos = np.where((p // 32 == 0)[:, None], (t // 64)[None, :], (t % 64)[None, :]).astype(f)
    ang = (pos * inv[p % 16][:, None]).astype(f)
    k[:, g:g + 512] = np.cos(ang)
    k[:, g + 512:g + 1024] = np.sin(ang)
    g += 1024
    first = (np.arange(128) % 32) < 16
    k[:, g:g + 128] = np.where(first[None, :], -1.0 * (i == j + 16), 1.0 * (i == j - 16))
    k[:, g + 128:g + 256] = (i // 64 == j // 64) & (i % 64 == 63 - j % 64)
    return k


class Engine:

    def __init__(self, sem):
        self.sem, self.n, self.queue, self.seen = sem, 0, [], {}

    def wait(self, *after):
        for t in after:
            if t is None:
                continue
            if isinstance(t, list):
                self.wait(*t)
            elif self.seen.get(id(t[0]), 0) < t[1]:
                self.seen[id(t[0])] = t[1]
                self.queue.append((None, t[0], t[1]))

    def __call__(self, fn, *after):
        self.wait(*after)
        self.n += 1
        self.queue.append((fn, self.sem, 1))
        return (self.sem, self.n)

    def quiet(self, fn, *after):
        self.wait(*after)
        self.queue.append((fn, None, 0))

    def dma(self, fn, lane, *after):
        self.wait(*after)
        lane[1] += 16
        self.queue.append((fn, lane[0], 16))
        return (lane[0], lane[1])

    def emit(self, eng):
        for fn, sem, n in self.queue:
            if fn is None:
                eng.wait_ge(sem, n)
            elif sem is None:
                fn(eng)
            else:
                fn(eng).then_inc(sem, n)


class Banks:

    def __init__(self, tiles):
        self.tiles, self.free, self.i = tiles, [None] * len(tiles), 0

    def take(self):
        b = self.i % len(self.tiles)
        self.i += 1
        return b, self.tiles[b], self.free[b]

    def done(self, b, token):
        self.free[b] = token


def build(nc, a, out, stop=None, dump=None):
    ctx = ExitStack()
    with ctx:
        def sb(name, shape):
            return ctx.enter_context(nc.sbuf_tensor(name, shape, F32))

        def sem(name):
            return ctx.enter_context(nc.semaphore(name))

        X = sb("X", [128, 8, S])
        H = sb("H", [128, 8, S])
        ring = [sb(f"ring{i}", [128, 8, 512])[:, :, :] for i in range(NS)]
        KC = sb("KC", [128, K_RES])
        COL = sb("COL", [128, NCOL])
        MOD = sb("MOD", [128, 48, 2])
        SCT = sb("SCT", [128, 8, 2])
        AC = sb("AC", [128, 16])
        SQ = [sb(f"SQ{i}", [128, 512]) for i in range(2)]
        RR = [sb(f"RR{i}", [128, 512]) for i in range(2)]
        AR = sb("AR", [128, 24960])
        psum = [ctx.enter_context(nc.psum_tensor(f"ps{i}", [128, 512], F32))[:, :] for i in range(8)]

        PE, DV, AC_, PO, SP = (Engine(sem(n)) for n in ("s_pe", "s_dve", "s_act", "s_pool", "s_sp"))
        AE = AC_
        wl = [[sem(f"w{i}"), 0] for i in range(NS)]
        misc = {}

        def lane(name):
            if name not in misc:
                misc[name] = [sem("d_" + name), 0]
            return misc[name]

        B = Banks(psum)
        ident = KC[:, K_ID:K_ID + 128]
        ones = KC[:, K_ONE:K_ONE + 128]
        bones = KC[:, K_BONE:K_BONE + 128]
        e1, e64, ea2, one1, e128 = (KC[:, K_EPS + n:K_EPS + n + 1] for n in range(5))

        def col(n):
            return COL[:, n:n + 1]

        def arena(off, *shape):
            n = int(np.prod(shape))
            v = AR[:, off:off + n]
            if len(shape) == 2:
                v = v.rearrange("p (a b) -> p a b", a=shape[0])
            elif len(shape) == 3:
                v = v.rearrange("p (a b c) -> p a b c", a=shape[0], b=shape[1])
            return v

        def last():
            return [(e.sem, e.n) for e in (PE, DV, AE, PO) if e.n]

        def fence():
            t = last()
            for e in (DV, AE, PO):
                e.wait(t)
            return t

        slot_free = [None] * NS
        slot_n = [0]

        def weights(*parts):
            i = slot_n[0] % NS
            slot_n[0] += 1
            SP.wait(slot_free[i])
            for view, src in parts:
                t = SP.dma(lambda e, v=view(ring[i]), s=src: e.dma_start(v, s), wl[i])
            return i, ring[i], t

        def wtile(src, k, n):
            return weights((lambda r: r[:, 0:k, 0:n], src.rearrange("(k p) n -> p k n", p=128)))

        def mm(bank, groups, *after):
            PE.wait(*after)
            n = len(groups)
            t = None
            for g, (o, prs) in enumerate(groups):
                for i, (l, r) in enumerate(prs):
                    f = (lambda e, o=o, l=l, r=r, st=(i == 0), sp=(i == len(prs) - 1):
                         e.matmul(o, l, r, start=st, stop=sp))
                    if g == n - 1 and i == len(prs) - 1:
                        t = PE(f)
                    else:
                        PE.quiet(f)
            return t

        def tp(outs, *after):
            PE.wait(*after)
            t = None
            for o, i in outs:
                k = i.shape[0]
                f = lambda e, o=o, i=i, k=k: e.transpose(o, i, ident[0:k, 0:k])
                t = PE(f) if i is outs[-1][1] else PE.quiet(f)
            return t

        def act(o, i, fn, *after, **kw):
            return AE(lambda e: e.activation(o, i, fn, **kw), *after)

        def tt(o, x, y, op, *after, e=None):
            return (e or DV)(lambda q: q.tensor_tensor(o, x, y, op), *after)

        def ts(o, x, s1, s2, o0, o1, *after, e=None):
            if s2 is None:
                return (e or DV)(lambda q: q.tensor_scalar(o, x, s1, None, o0), *after)
            return (e or DV)(lambda q: q.tensor_scalar(o, x, s1, s2, o0, o1), *after)

        def stt(o, x, s, y, o0, o1, *after):
            return DV(lambda q: q.scalar_tensor_tensor(o, x, s, y, o0, o1), *after)

        def cp(o, x, *after):
            return DV(lambda q: q.tensor_copy(o, x), *after)

        M, A_ = ALU.mult, ALU.add

        sqf, rrf = [None, None], [None, None]
        cnt = {"sq": 0, "rr": 0}

        def sq_of(src, n, *after):
            i = cnt["sq"] % 2
            cnt["sq"] += 1
            t = act(SQ[i][:, 0:n], src, ACT.Square, sqf[i], *after)
            return i, SQ[i][:, 0:n], t

        def rstd(ps, bank, n, scale, eps, t):
            i = cnt["rr"] % 2
            cnt["rr"] += 1
            r = RR[i][:, 0:n]
            t = act(r, ps, ACT.Ln, t, rrf[i], scale=scale, bias=eps)
            B.done(bank, t)
            t = act(r, r, ACT.Exp, t, scale=-0.5)
            return i, r, t

        def sumsq(srcs, n, mat, *after):
            b, ps, fr = B.take()
            PE.wait(fr)
            for k, s in enumerate(srcs):
                i, q, t = sq_of(s, n, *after)
                f = (lambda e, q=q, k=k: e.matmul(ps[:, 0:n], mat, q, start=(k == 0),
                                                  stop=(k == len(srcs) - 1)))
                t = PE(f, t)
                sqf[i] = t
            return b, ps[:, 0:n], t

        def rms(x, h, w, *after):
            b, ps, t = sumsq([x[:, k, :] for k in range(8)], S, ones, *after)
            i, r, t = rstd(ps, b, S, 1.0 / D, e1, t)
            hold = last()
            for k in range(8):
                t = stt(h[:, k, :], x[:, k, :], col(w + k), r, M, M, t, hold)
            rrf[i] = t
            return t

        def layernorm(x, h, n, eps, g, b_, *after):
            hold = last()
            bk, ps, fr = B.take()
            t = mm(bk, [(ps[:, 0:n], [(ones, x[:, k, :]) for k in range(8)])], fr, *after)
            toks = []
            for k in range(8):
                toks.append(stt(h[:, k, :], ps[:, 0:n], -1.0 / D, x[:, k, :], M, A_, t, hold))
            B.done(bk, toks[-1])
            b, ps, fr = B.take()
            PE.wait(fr)
            for k in range(8):
                i, q, tq = sq_of(h[:, k, :], n, toks[k])
                t = PE(lambda e, q=q, k=k: e.matmul(ps[:, 0:n], ones, q, start=(k == 0), stop=(k == 7)), tq)
                sqf[i] = t
            i, r, t = rstd(ps[:, 0:n], b, n, 1.0 / D, eps, t)
            for k in range(8):
                tk = tt(h[:, k, :], h[:, k, :], r, M, t)
                rrf[i] = tk
                to = act(h[:, k, :], h[:, k, :], ACT.Identity, tk, scale=g(k), bias=b_(k))
            return to

        def linear(w, kt, streams, evac, *after):
            n = w.shape[1]
            PE.wait(*after)
            late = []
            for c in range(0, n, 512):
                m = min(512, n - c)
                si, sl, tw = wtile(w[:, c:c + m], kt, m)
                for j in range(m // 128):
                    for s, (h, nt) in enumerate(streams):
                        if h is None:
                            continue
                        b, ps, fr = B.take()
                        t = mm(b, [(ps[:, 0:nt], [(sl[:, k, j * 128:(j + 1) * 128], h[:, k, :])
                                                  for k in range(kt)])], fr, tw)
                        if late:
                            late.pop()()
                        late.append(lambda b=b, j=c // 128 + j, s=s, o=ps[:, 0:nt], t=t: B.done(b, evac(j, s, o, t)))
                slot_free[si] = t
            late.pop()()

        def linear_tok(w, streams, evac, *after):
            n = w.shape[1]
            PE.wait(*after)
            si, sl, tw = wtile(w, 8, n)
            for s, (h, nt) in enumerate(streams):
                for q in range(nt // 128):
                    b, ps, fr = B.take()
                    t = mm(b, [(ps[:, 0:n], [(h[:, k, q * 128:(q + 1) * 128], sl[:, k, 0:n])
                                             for k in range(8)])], fr, tw)
                    B.done(b, evac(q, s, ps[:, 0:n], t))
            slot_free[si] = t

        def ffn(wi, wo, streams, G, evac, *after):
            PE.wait(*after)
            tg = None
            sil = [None, None]
            q = 0
            for c in range(11):
                si, sl, tw = weights(
                    (lambda r: r[:, :, 0:256], wi[:, c * 256:(c + 1) * 256].rearrange("(k p) n -> p k n", p=128)),
                    (lambda r: r[:, :, 256:512],
                     wi[:, FF + c * 256:FF + (c + 1) * 256].rearrange("(k p) n -> p k n", p=128)))
                for j in range(2):
                    for s, (h, n) in enumerate(streams):
                        ba, pa, fa = B.take()
                        ta = mm(ba, [(pa[:, 0:n], [(sl[:, k, j * 128:(j + 1) * 128], h[:, k, :])
                                                   for k in range(8)])], fa, tw)
                        bb, pb, fb = B.take()
                        tb = mm(bb, [(pb[:, 0:n], [(sl[:, k, 256 + j * 128:256 + (j + 1) * 128], h[:, k, :])
                                                   for k in range(8)])], fb)
                        i = q % 2
                        q += 1
                        t = act(SQ[i][:, 0:n], pa[:, 0:n], ACT.Silu, ta, sqf[i])
                        B.done(ba, t)
                        tg = tt(G[s][:, c * 2 + j, :], SQ[i][:, 0:n], pb[:, 0:n], M, t, tb)
                        sqf[i] = tg
                        B.done(bb, tg)
                slot_free[si] = tb
            for half in range(2):
                bk = [[B.take() for _ in range(4)] for _ in streams]
                r0 = 0
                for nr in (8, 8, 6):
                    si, sl, tw = wtile(wo[r0 * 128:(r0 + nr) * 128, half * 512:(half + 1) * 512], nr, 512)
                    PE.wait(tw, tg)
                    for s, (h, n) in enumerate(streams):
                        for m in range(4):
                            b, ps, fr = bk[s][m]
                            if r0 == 0:
                                PE.wait(fr)
                            for k in range(nr):
                                f = (lambda e, ps=ps, sl=sl, k=k, m=m, s=s, r=r0 + k, n=n: e.matmul(
                                    ps[:, 0:n], sl[:, k, m * 128:(m + 1) * 128], G[s][:, r, :],
                                    start=(r == 0), stop=(r == 21)))
                                if k == nr - 1:
                                    t = PE(f)
                                    if r0 + nr == 22:
                                        B.done(b, evac(half * 4 + m, s, ps[:, 0:n], t))
                                else:
                                    PE.quiet(f)
                    slot_free[si] = t
                    r0 += nr

        lfree, pfree = [None, None], [None, None]

        def attention(jobs, Lb, Pb, vtok, ktok, hooks={}):
            state = []

            def scores(n, job):
                segs, vals, o, note = job
                if n in hooks:
                    hooks[n]()
                tn = note() if note else None
                L = Lb[n % 2]
                m = AC[:, 8 * (n % 2):8 * (n % 2) + 8]
                off, ms, info = 0, [], []
                for g, (q, k, bias, tk) in enumerate(segs):
                    w = k.shape[1]
                    b, ps, fr = B.take()
                    t = mm(b, [(ps[:, 0:w], [(q, k)])], fr, tk, ktok)
                    if bias is None:
                        t = DV(lambda e, ps=ps, w=w, g=g: e.reduce_max(m[:, g:g + 1], ps[:, 0:w], AX),
                               t, lfree[n % 2])
                        info.append((ps[:, 0:w], off, w, b))
                    else:
                        t = DV(lambda e, ps=ps, w=w, g=g, off=off, bias=bias: e.tensor_tensor_reduce(
                            L[:, off:off + w], ps[:, 0:w], bias, 1.0, 0.0 - 3e38, A_, ALU.max,
                            m[:, g:g + 1]), t, lfree[n % 2], tn)
                        B.done(b, t)
                        info.append((L[:, off:off + w], off, w, None))
                    off += w
                t = DV(lambda e: e.tensor_reduce(m[:, 3:4], m[:, 0:len(segs)], AX, ALU.max, negate=True), t)
                for g, (src, f, w, b) in enumerate(info):
                    te = act(L[:, f:f + w], src, ACT.Exp, t, lfree[n % 2], bias=m[:, 3:4], accum_out=m[:, 4 + g:5 + g])
                    if b is not None:
                        B.done(b, te)
                t = DV(lambda e: e.reduce_sum(m[:, 3:4], m[:, 4:4 + len(segs)], AX), te)
                t = DV(lambda e: e.reciprocal(m[:, 3:4], m[:, 3:4]), t)
                state.append((te, t, off))

            def values(n, job):
                segs, vals, o, note = job
                te, tr, width = state[n]
                L, P = Lb[n % 2], Pb[n % 2]
                nb = width // 128
                tc = []
                for c in range(0, nb, 4):
                    k = min(4, nb - c)
                    b, ps, fr = B.take()
                    t = tp([(ps[:, i * 128:(i + 1) * 128], L[:, (c + i) * 128:(c + i + 1) * 128])
                            for i in range(k)], fr, te)
                    o_, i_ = P[:, c * 128:(c + k) * 128], ps[:, 0:k * 128]
                    t2 = act(o_, i_, ACT.Copy, t, pfree[n % 2])
                    B.done(b, t2)
                    tc.append(t2)
                lt = t
                b, ps, fr = B.take()
                t = mm(b, [(ps[:, 0:64], [(P[:, i * 128:(i + 1) * 128], vals[i]) for i in range(nb)])],
                       fr, tc, vtok)
                pfree[n % 2] = t
                r = AC[:, 8 * (n % 2) + 3:8 * (n % 2) + 4]
                t = ts(o, ps[:, 0:64], r, None, M, None, t, tr)
                B.done(b, t)
                lfree[n % 2] = [lt, t]
                return t

            t = None
            for n, job in enumerate(jobs):
                scores(n, job)
                if n:
                    t = values(n - 1, jobs[n - 1])
            return values(len(jobs) - 1, jobs[-1])

        def finish(*after, src=None):
            AE.wait(*after)
            t = AE.dma(lambda e: e.dma_start(out, (src or X)[:, :, :]), lane("out"))
            AE.wait(t)

        tk0 = AE.dma(lambda e: e.dma_start(KC[:, :], a["kc"][:, 0:K_RES]), lane("kc"))
        tcol = AE.dma(lambda e: e.dma_start(COL[:, :], a["cols"]), lane("col"))
        tx = AE.dma(lambda e: e.dma_start(X[:, :, :], a["x"]), lane("x"))
        boot = [tk0, tcol, tx]
        for e in (PE, DV, AE, PO):
            e.wait(boot)

        GM = arena(0, 8, 128)
        tgm = AE.dma(lambda e: e.dma_start(arena(0, 1024), a["kc"][:, K_GDN:K_GDN + 1024]), lane("gm"))
        o_ = 1024
        rows = [arena(o_ + 512 * n, 512) for n in range(2)]
        o_ += 2 * 512
        GC = arena(o_, 4, 8); o_ += 32
        BT = arena(o_, 4, 8); o_ += 32
        EG = arena(o_, 4, 8); o_ += 32
        KB = arena(o_, 4, 8); o_ += 32
        GL = arena(o_, 4, 8); o_ += 32
        TL = arena(o_, 4, 8); o_ += 32
        CD = arena(o_, 4, 8); o_ += 32
        NE = arena(o_, 8); o_ += 8
        bufs = [o_ + 2048 * n for n in range(10)]
        SO = o_ + 20480
        assert SO + 2048 <= 24960
        rs, res = (arena(bufs[9] + 512 * n, 512)[0:8, :] for n in range(2))
        tres = AE.dma(lambda e: e.dma_start(res, a["kc"][0:8, K_GDN + 1024:K_GDN + 1536]), lane("res"))
        cv = [arena(bufs[8], 516), arena(bufs[8] + 516, 516)]
        th = rms(X, H, C_NMIX, boot)
        hs = [(H[:, :, :], S)]
        wg = a["gdn_w_in"]
        si, sl, tw = weights((lambda r: r[:, :, 0:16],
                              wg[:, 4096:4112].rearrange("(k p) n -> p k n", p=128)))
        ba, pa, fa = B.take()
        bb, pb, fb = B.take()
        ta = mm(ba, [(pa[0:8, :], [(sl[:, k, 0:8], H[:, k, :]) for k in range(8)])], fa, tw, th)
        tb = mm(bb, [(pb[0:8, :], [(sl[:, k, 8:16], H[:, k, :]) for k in range(8)])], fb)
        slot_free[si] = tb
        rg, rb = (r[0:8, :] for r in rows)
        dt = COL[0:8, C_DT:C_DT + 1]
        t1 = act(NE[0:8, 0:1], COL[0:8, C_ALOG:C_ALOG + 1], ACT.Exp)
        t2 = act(rs, pa[0:8, :], ACT.Abs, ta, bias=dt)
        t3 = ts(rg, pa[0:8, :], dt, 0.0, A_, ALU.max, t2)
        B.done(ba, t3)
        t2 = act(rs, rs, ACT.Exp, t2, scale=-1.0)
        t2 = act(rs, rs, ACT.Ln, t2, bias=one1[0:8, :])
        t3 = tt(rg, rg, rs, A_, t2, t3)
        t3 = ts(rg, rg, NE[0:8, 0:1], -1.0, M, M, t3, t1)
        t3 = DV(lambda e: e.tensor_tensor_scan(rs, res, rg, 0.0, M, A_), t3, tres)
        tgr = cp(rg, rs, t3)
        t2 = act(rb, pb[0:8, :], ACT.Sigmoid, tb)
        B.done(bb, t2)
        b, ps, fr = B.take()
        t = tp([(ps[:, c * 8:c * 8 + 8], rg[:, c * 128:(c + 1) * 128]) for c in range(4)]
               + [(ps[:, 32 + c * 8:40 + c * 8], rb[:, c * 128:(c + 1) * 128]) for c in range(4)],
               fr, tgr, t2)
        t3 = cp(GC.rearrange("p a b -> p (a b)"), ps[:, 0:32], t)
        t4 = cp(BT.rearrange("p a b -> p (a b)"), ps[:, 32:64], t)
        B.done(b, t4)
        teg = act(EG, GC, ACT.Exp, t3)
        tkb = tt(KB, EG, BT, M, teg, t4)
        tsetup = [t4, tkb]

        def conv(j, dst, ps, t):
            i = cnt.setdefault("cv", 0) % 2
            cnt["cv"] += 1
            c = cv[i]
            w = C_CONV + 4 * j
            fr = cvf[i]
            t0 = PO(lambda e, c=c: e.memset(c[:, 0:3], 0.0), fr, tgr, hold)
            tc = act(c[:, 3:515], ps, ACT.Copy, t, fr, tgr, hold)
            tv = ts(dst, c[:, 3:515], col(w + 3), None, M, None, tc, t0, hold)
            for n in (2, 1, 0):
                tv = stt(dst, c[:, n:n + 512], col(w + n), dst, M, A_, tv)
            cvf[i] = tv
            act(dst, dst, ACT.Silu, tv)
            return tc

        cvf = [None, None]
        for hg in range(2):
            hold = last() if hg else None
            bf = [arena(o, 4, 512) for o in bufs]
            q, k, v, vb, kbe, ktl, DT, Xb, AT, qk = bf
            T, TT = v, k
            tp_ = None
            for which, dst in ((0, q), (1, k), (2, v)):
                w = wg[:, which * 1024 + hg * 512:which * 1024 + (hg + 1) * 512]
                linear(w, 8, hs, lambda j, s, ps, t: conv(which * 8 + hg * 4 + j, dst[:, j, :], ps, t), th)
            tsil = (AE.sem, AE.n)
            gl_tok = []
            ends = []
            for h in range(4):
                hh = hg * 4 + h
                for x_, scale, eps in ((q, 128.0, None), (k, 1.0, e1)):
                    b, ps, t = sumsq([x_[:, h, :]], 512, ones, tsil)
                    if eps is None:
                        i, r, t = rstd(ps, b, 512, 128.0, e128, t)
                    else:
                        i, r, t = rstd(ps, b, 512, 1.0, e1, t)
                    t = tt(x_[:, h, :], x_[:, h, :], r, M, t)
                    rrf[i] = t
                tn = t
                b, ps, fr = B.take()
                t = mm(b, [(ps[:, :], [(ident[0:8, hh:hh + 1].broadcast_to([8, 128]), rb)])], fr, tsetup)
                t = tt(Xb[:, h, :], k[:, h, :], ps[:, :], M, t, tn)
                B.done(b, t)
                b, ps, fr = B.take()
                t = mm(b, [(ps[:, :], [(ident[0:8, hh:hh + 1].broadcast_to([8, 128]), rg)])], fr)
                t4 = cp(GL[:, :, hh], ps.rearrange("p (a b) -> p a b", a=4)[:, :, 127], t)
                for c in range(4):
                    t4 = ts(DT[:, h, c * 128:(c + 1) * 128], ps[:, c * 128:(c + 1) * 128], GC[:, c, hh:hh + 1],
                            0.0, ALU.subtract, ALU.min, t)
                i = cnt["rr"] % 2
                cnt["rr"] += 1
                te = act(RR[i][:, :], ps[:, :], ACT.Exp, t4, rrf[i])
                B.done(b, te)
                td = act(DT[:, h, :], DT[:, h, :], ACT.Exp, t4)
                td = tt(DT[:, h, :].rearrange("p (a b) -> p a b", a=4), DT[:, h, :].rearrange("p (a b) -> p a b", a=4),
                        GM[:, 7:8, :].broadcast_to([128, 4, 128]), M, td, tgm)
                b, ps, fr = B.take()
                t = mm(b, [(ps[:, c * 128:(c + 1) * 128], [(k[:, h, c * 128:(c + 1) * 128],
                                                            Xb[:, h, c * 128:(c + 1) * 128])])
                           for c in range(4)], fr, (DV.sem, DV.n))
                ta_ = tt(AT[:, h, :], ps[:, :], DT[:, h, :], M, t, td)
                B.done(b, ta_)
                b, ps, fr = B.take()
                t = mm(b, [(ps[:, c * 128:(c + 1) * 128], [(k[:, h, c * 128:(c + 1) * 128],
                                                            q[:, h, c * 128:(c + 1) * 128])])
                           for c in range(4)], fr)
                t5 = tt(qk[:, h, :], ps[:, :], DT[:, h, :], M, t)
                B.done(b, t5)
                t6 = tt(q[:, h, :], q[:, h, :], RR[i][:, :], M, t, te)
                rrf[i] = t6
                ends += [t5, t6, ta_]
            h0 = hg * 4
            t = tt(TL[:, :, h0:h0 + 4], GL[:, :, h0:h0 + 4], GC[:, :, h0:h0 + 4], ALU.subtract, t4)
            t1 = act(TL[:, :, h0:h0 + 4], TL[:, :, h0:h0 + 4], ACT.Exp, t)
            t2 = act(CD[:, :, h0:h0 + 4], GL[:, :, h0:h0 + 4], ACT.Exp, t)
            kv = []
            for c in range(4):
                b, ps, fr = B.take()
                t = tp([(ps[:, h * 128:(h + 1) * 128], v[:, h, c * 128:(c + 1) * 128]) for h in range(4)], fr)
                p4 = ps[:, :].rearrange("p (a b) -> p a b", a=4)
                view = lambda z: z[:, c, :].rearrange("p (a b) -> p a b", a=4)
                bc = lambda z: z[:, c, h0:h0 + 4].unsqueeze(2).broadcast_to([128, 4, 128])
                t = tt(view(vb), p4, bc(BT), M, t)
                B.done(b, t)
                kv.append(t)
                b, ps, fr = B.take()
                t = tp([(ps[:, h * 128:(h + 1) * 128], k[:, h, c * 128:(c + 1) * 128]) for h in range(4)], fr)
                p4 = ps[:, :].rearrange("p (a b) -> p a b", a=4)
                t_ = tt(view(kbe), p4, bc(KB), M, t)
                t = tt(view(ktl), p4, bc(TL), M, t, t1)
                B.done(b, t)
                kv.append(t)
            free3 = [(PE.sem, PE.n)]
            tT = [kv] * 4
            for n in range(7):
                for h in range(4):
                    c4 = lambda z: z[:, h, :].rearrange("p (a b) -> p a b", a=4)
                    idb = ident.unsqueeze(1).broadcast_to([128, 4, 128])
                    sl4 = lambda z, c: ident if z is None else z[:, h, c * 128:(c + 1) * 128]
                    Tn, TTn = (None, None) if n == 0 else (T, TT)
                    b, ps, fr = B.take()
                    t = mm(b, [(ps[:, c * 128:(c + 1) * 128], [(AT[:, h, c * 128:(c + 1) * 128], sl4(Tn, c))])
                               for c in range(4)], fr, tT[h], ends)
                    tx_ = tt(c4(Xb), ps[:, :].rearrange("p (a b) -> p a b", a=4),
                             GM[:, n:n + 1, :].broadcast_to([128, 4, 128]), M, t, tT[h])
                    B.done(b, tx_)
                    b2, ps2, fr2 = B.take()
                    t = mm(b2, [(ps2[:, c * 128:(c + 1) * 128], [(Xb[:, h, c * 128:(c + 1) * 128], sl4(TTn, c))])
                                for c in range(4)], fr2, tx_)
                    if n < 6:
                        b1, ps1, fr1 = B.take()
                        t_ = mm(b1, [(ps1[:, c * 128:(c + 1) * 128], [(sl4(TTn, c), Xb[:, h, c * 128:(c + 1) * 128])])
                                     for c in range(4)], fr1)
                        t1_ = tt(c4(T), idb if n == 0 else c4(T), ps1[:, :].rearrange("p (a b) -> p a b", a=4),
                                 ALU.subtract, t_, free3)
                        B.done(b1, t1_)
                    else:
                        t_ = t
                    t2_ = tt(c4(TT), idb if n == 0 else c4(TT), ps2[:, :].rearrange("p (a b) -> p a b", a=4),
                             ALU.subtract, t_, free3)
                    B.done(b2, t2_)
                    tT[h] = [t1_, t2_]
            W = DT
            tw_ = []
            for h in range(4):
                b, ps, fr = B.take()
                t = mm(b, [(ps[:, c * 128:(c + 1) * 128], [(kbe[:, c, h * 128:(h + 1) * 128],
                                                            TT[:, h, c * 128:(c + 1) * 128])])
                           for c in range(4)], fr, tT[h])
                t = act(W[:, h, :], ps[:, :], ACT.Copy, t, scale=-1.0)
                B.done(b, t)
                tw_.append(t)
            SS = [Xb[:, 0, :], Xb[:, 1, :]]
            VN = [Xb[:, 2, :], Xb[:, 3, :]]
            oraw = T
            ts_, tvn = None, None
            for c in range(4):
                Sc, Sn, vn = SS[c % 2], SS[(c + 1) % 2], VN[c % 2]
                hs4 = lambda z, h: z[:, h * 128:(h + 1) * 128]
                b, ps, fr = B.take()
                t = mm(b, [(hs4(ps, h), [(TT[:, h, c * 128:(c + 1) * 128], hs4(vb[:, c, :], h))]
                            + ([(W[:, h, c * 128:(c + 1) * 128], hs4(Sc, h))] if c else []))
                           for h in range(4)], fr, tw_, ts_, tT)
                tvn = act(vn, ps[:, :], ACT.Copy, t)
                B.done(b, tvn)
                if c < 3:
                    b, ps, fr = B.take()
                    t = mm(b, [(hs4(ps, h), [(hs4(ktl[:, c, :], h), hs4(vn, h))]) for h in range(4)], fr, tvn)
                    if c == 0:
                        ts_ = cp(Sn, ps, t)
                    else:
                        for h in range(4):
                            ts_ = stt(hs4(Sn, h), hs4(Sc, h), CD[:, c, h0 + h:h0 + h + 1], hs4(ps, h), M, A_, t, t2)
                    B.done(b, ts_)
                b, ps, fr = B.take()
                t = mm(b, [(hs4(ps, h), ([(hs4(Sc, h), q[:, h, c * 128:(c + 1) * 128])] if c else [])
                            + [(hs4(vn, h), qk[:, h, c * 128:(c + 1) * 128])])
                           for h in range(4)], fr, tvn)
                t = act(oraw[:, :, c * 128:(c + 1) * 128], ps[:, :].rearrange("p (a b) -> p a b", a=4), ACT.Copy, t)
                B.done(b, t)
            Z = AT

            def zev(j, s, ps, t):
                return act(Z[:, j, :], ps, ACT.Silu, t)
            linear(wg[:, 3072 + hg * 512:3072 + (hg + 1) * 512], 8, hs, zev)
            tz = (AE.sem, AE.n)
            O = arena(SO if hg == 0 else bufs[0], 4, 512) if hg == 0 else bf[0]
            for h in range(4):
                b, ps, t = sumsq([oraw[:, h, :]], 512, ones, tz)
                i, r, t = rstd(ps, b, 512, 1.0 / 128, e1, t)
                t = tt(oraw[:, h, :], oraw[:, h, :], r, M, t)
                rrf[i] = t
                t = stt(O[:, h, :], oraw[:, h, :], col(C_GNW), Z[:, h, :], M, M, t)
            if hg == 0:
                O0 = O
        O1 = O

        def add_x(j, s, ps, t):
            return tt(X[:, j, :], X[:, j, :], ps, A_, t)

        for c in range(2):
            si, sl, tw = wtile(a["gdn_w_out"][:, c * 512:(c + 1) * 512], 8, 512)
            for j in range(4):
                b, ps, fr = B.take()
                tm = mm(b, [(ps[:, :], [(sl[:, k, j * 128:(j + 1) * 128], (O0 if k < 4 else O1)[:, k % 4, :])
                                        for k in range(8)])], fr, tw, t)
                t9 = add_x(c * 4 + j, 0, ps[:, :], tm)
                B.done(b, t9)
            slot_free[si] = tm
        txx = t9
        if stop == "gdn":
            finish(txx)
            return emit(nc, ctx, PE, DV, AE, PO, SP)

        def ffn1(l):
            G = arena(0, 22, 512)
            fence()
            th = rms(X, H, C_NFFN + 8 * l, (DV.sem, DV.n))
            ffn(a["ffn_w_in"][l], a["ffn_w_out"][l], hs, [G], add_x, th)

        ffn1(0)
        if stop == "ffn0":
            finish((DV.sem, DV.n))
            return emit(nc, ctx, PE, DV, AE, PO, SP)

        fence()
        tq = last()
        QD, KD, VD = arena(0, 12, 512), arena(6144, 12, 512), arena(12288, 4, 1536)
        DI = arena(18432, 1280)
        PB = [arena(19712, 1280), arena(20992, 1280)]
        BI2 = arena(22272, 1280)
        tdi = AE.dma(lambda e: e.dma_start(DI, a["kc"][:, K_DIL:K_DIL + N_DIL]), lane("di"), tq)
        th = rms(X, H, C_NMIX + 8, (DV.sem, DV.n))
        wd = a["dil_w_in"]

        def headnorm(dst, ps, n, g, scale, eps, t):
            b, p2, t = sumsq([ps], n, bones, t)
            i, r, t = rstd(p2, b, n, scale, eps, t)
            t = stt(dst, ps, g, r, M, M, t)
            rrf[i] = t
            return t

        linear(wd[:, 0:1536], 8, hs, lambda j, s, ps, t: headnorm(QD[:, j, :], ps, 512, col(C_DQ), 1.0, e64, t), th)
        linear(wd[:, 1536:3072], 8, hs,
               lambda j, s, ps, t: headnorm(KD[:, j, :], ps, 512, col(C_DK), 1.0 / 64, e1, t))
        for c in range(3):
            linear_tok(wd[:, 3072 + c * 512:3072 + (c + 1) * 512], hs,
                       lambda qt, s, ps, t: act(VD[:, qt, c * 512:(c + 1) * 512], ps, ACT.Copy, t))
        tv = [(AE.sem, AE.n), (DV.sem, DV.n), (PE.sem, PE.n)]
        HF = H[:, :, :].rearrange("p a b -> p (a b)")
        BI = [HF[:, 0:1280], BI2]
        LB = [HF[:, 1280:2560], HF[:, 2560:3840]]
        OTK = [arena(23552, 512), arena(24064, 512), SQ[0], SQ[1]]
        bt = {}

        def dil_bias(h, *after):
            t = None
            for g, (o0, o1) in enumerate(((0, 256), (256, 768), (768, 1280))):
                slope = float(2.0 ** (-8.0 * (g * 8 + h + 1) / 24))
                t = act(BI[h % 2][:, o0:o1], DI[:, o0:o1], ACT.Copy, tdi, tv, *after, scale=slope)
            bt[h] = t

        jobs, hooks = [], {}
        dil_bias(0)
        for h in range(8):
            if h < 7:
                hooks[4 * h + 1] = lambda h=h: dil_bias(h + 1, (DV.sem, DV.n))
            pb_ = 64 * (h % 2)
            for qt in range(4):
                k0 = max(0, qt - 1)
                segs, vals = [], []
                for g, (lo, full) in enumerate(((k0, 256), (0, 512), (0, 512))):
                    tile = g * 4 + h // 2
                    w = (qt + 1 - lo) * 128
                    base = (0, 256, 768)[g] + full - w
                    segs.append((QD[pb_:pb_ + 64, tile, qt * 128:(qt + 1) * 128],
                                 KD[pb_:pb_ + 64, tile, lo * 128:(qt + 1) * 128],
                                 BI[h % 2][:, base:base + w], None))
                    vals += [VD[:, kt, g * 512 + h * 64:g * 512 + (h + 1) * 64] for kt in range(lo, qt + 1)]
                jobs.append((segs, vals, OTK[qt][:, h * 64:(h + 1) * 64], lambda h=h: bt[h]))
        to = attention(jobs, LB, PB, tv, tv, hooks)
        OF = arena(0, 4, 512)
        tf = None
        fr_ = (PE.sem, PE.n)
        for j in range(4):
            b, ps, fr = B.take()
            t = tp([(ps[:, q * 128:(q + 1) * 128], OTK[q][:, j * 128:(j + 1) * 128]) for q in range(4)], fr, to)
            tf = act(OF[:, j, :], ps[:, :], ACT.Copy, t, fr_)
            sqf[0] = sqf[1] = t
            B.done(b, tf)
        linear(a["dil_w_out"], 4, [(OF, S)], add_x, tf)
        if stop == "dil":
            finish((DV.sem, DV.n))
            return emit(nc, ctx, PE, DV, AE, PO, SP)
        ffn1(1)
        if stop == "ffn1":
            finish((DV.sem, DV.n))
            return emit(nc, ctx, PE, DV, AE, PO, SP)

        fence()
        tq = last()
        XC = arena(24960 - 2048, 8, LC)
        HC = arena(24960 - 4096, 8, LC)
        AMAX = 24960 - 4096
        txc = AE.dma(lambda e: e.dma_start(XC, a["ctx"]), lane("xc"), tq)
        for k in range(8):
            tx1 = act(X[:, k, :], X[:, k, :], ACT.Copy, tq, scale=ALPHA)
        tx2 = act(XC, XC, ACT.Copy, txc, scale=ALPHA)
        tsc = act(SCT[:, :, :], COL[:, C_C:C_C + 16].rearrange("p (k s) -> p k s", s=2), ACT.Silu)
        tX, tXC = [tx1], [tx2]
        CL = AC
        for l in range(2):
            b, ps, fr = B.take()
            hold = last()
            PE.wait(fr, tsc)
            for c in range(12):
                si, sl, tw = wtile(a["w_mod"][l][:, c * 512:(c + 1) * 512], 8, 512)
                PE.wait(tw)
                for j in range(4):
                    m = c * 4 + j
                    for k in range(8):
                        f = (lambda e, ps=ps, m=m, k=k, sl=sl, j=j: e.matmul(
                            ps[:, 2 * m:2 * m + 2], sl[:, k, j * 128:(j + 1) * 128], SCT[:, k, :],
                            start=(k == 0), stop=(k == 7)))
                        t = PE(f) if j == 3 and k == 7 else PE.quiet(f)
                slot_free[si] = t
            t = tt(MOD[:, :, :], ps[:, 0:96].rearrange("p (a b) -> p a b", b=2),
                   COL[:, C_BMOD + 48 * l:C_BMOD + 48 * (l + 1)].unsqueeze(2).broadcast_to([128, 48, 2]), A_, t, hold)
            B.done(b, t)
            for o in (8, 32):
                tmod = ts(MOD[:, o:o + 8, :], MOD[:, o:o + 8, :], 1.0, None, A_, None, t)
            mod = lambda g, s: (lambda k: MOD[:, 8 * g + k, s:s + 1])
            layernorm(X, H, S, ea2, mod(1, 0), mod(0, 0), tX, tmod)
            layernorm(XC, HC, LC, ea2, mod(1, 1), mod(0, 1), tXC, tmod)
            th = (AE.sem, AE.n)
            if stop == "H":
                finish(th, src=H)
                return emit(nc, ctx, PE, DV, AE, PO, SP)
            tq = fence()
            o = 0
            def take(*shape):
                nonlocal o
                v = arena(o, *shape)
                o += int(np.prod(shape))
                assert o <= AMAX, o
                return v
            QA, QAX, KA, KAX = take(3, S), take(3, LC), take(3, S), take(3, LC)
            VA, VAX = take(4, 384), take(2, 384)
            ZB, ZBX = take(4, 512), take(2, 512)
            QC, QCX, KCx, KCX = take(3, S), take(3, LC), take(1, S), take(1, LC)
            VC, VCX = take(4, 128), take(2, 128)
            EB = [take(14, 64), take(14, 64)]
            LB = [take(768), take(768)]
            PB = [take(768), take(768)]
            NM = take(N_NA)
            WS = take(4, 128)
            GS = take(256)
            CO, SI, RM, FL = NM[:, 64:576], NM[:, 576:1088], NM[:, 1088:1216], NM[:, 1216:1344]
            tnm = AE.dma(lambda e: e.dma_start(NM, a["kc"][:, K_NA:K_NA + N_NA]), lane("nm"), tq)
            tws = AE.dma(lambda e, l=l: e.dma_start(WS, a["w_sT"][l]), lane("ws"))
            tgs = AE.dma(lambda e, l=l: e.dma_start(
                GS, a["g_sgu"][l:l + 1, :].broadcast_to([128, 256])), lane("gs"))
            w = a["w_in"][l]
            both = [(H[:, :, :], S), (HC, LC)]
            qs = both if l == 0 else both[:1]
            linear(w[:, 0:384], 8, qs,
                   lambda j, s, ps, t: act((QA, QAX)[s][:, j, :], ps, ACT.Copy, t, scale=0.125), th)
            if stop == "projW0":
                print("slot", slot_n[0]-1)
                finish(*last(), src=ring[(slot_n[0] - 1) % 4])
                return emit(nc, ctx, PE, DV, AE, PO, SP)
            linear(w[:, 384:768], 8, both, lambda j, s, ps, t: act((KA, KAX)[s][:, j, :], ps, ACT.Copy, t))
            linear_tok(w[:, 768:1152], both, lambda q, s, ps, t: act((VA, VAX)[s][:, q, :], ps, ACT.Copy, t))
            linear_tok(w[:, 1152:1664], qs, lambda q, s, ps, t: act((ZB, ZBX)[s][:, q, :], ps, ACT.Gelu_apprx_tanh, t))
            kp = lambda v: v.rearrange("(k p) n -> p k n", p=128)
            si, sl, tw = weights(*[
                (lambda r, j=j, g=g: r[:, :, j * 128 + g * 64:j * 128 + (g + 1) * 64],
                 kp(w[:, 1664 + g * 192 + j * 64:1664 + g * 192 + (j + 1) * 64]))
                for j in range(3) for g in range(2)], (lambda r: r[:, :, 384:512], kp(w[:, 2048:2176])))
            for j in range(4):
                for s, (h_, n) in enumerate(both):
                    if j < 3 and s == 1 and l == 1:
                        continue
                    b, ps, fr = B.take()
                    t = mm(b, [(ps[:, 0:n], [(sl[:, k, j * 128:(j + 1) * 128], h_[:, k, :]) for k in range(8)])],
                           fr, tw)
                    last_pe = t
                    dst = ((QC, QCX)[s][:, j, :] if j < 3 else (KCx, KCX)[s][:, 0, :])
                    g, sc, ep = (C_GQ + l, 1.0, e64) if j < 3 else (C_GK + l, 1.0 / 64, e1)
                    t = headnorm(dst, ps[:, 0:n], n, col(g), sc, ep, t)
                    B.done(b, t)
                    if s == 0:
                        b, ps, fr = B.take()
                        t = mm(b, [(ps[:, :], [(RM, dst)])], fr, t, tnm)
                        i = cnt["rr"] % 2
                        cnt["rr"] += 1
                        t = tt(RR[i][:, :], ps[:, :], SI, M, t, rrf[i])
                        B.done(b, t)
                        t2 = tt(dst, dst, CO, M, t)
                        t = tt(dst, dst, RR[i][:, :], A_, t2)
                        rrf[i] = t
            slot_free[si] = last_pe
            linear_tok(w[:, 2176:2304], both, lambda q, s, ps, t: act((VC, VCX)[s][:, q, :], ps, ACT.Copy, t))
            tv = last()
            if stop == "projH":
                finish(tv, src=H)
                return emit(nc, ctx, PE, DV, AE, PO, SP)
            if stop == "projW":
                finish(tv, src=ring[(slot_n[0] - 6) % 4])
                return emit(nc, ctx, PE, DV, AE, PO, SP)
            if stop == "proj":
                finish(tv, src=arena(0, 8, 512))
                return emit(nc, ctx, PE, DV, AE, PO, SP)
            if stop == "proj2":
                finish(tv, src=arena(4608, 8, 512))
                return emit(nc, ctx, PE, DV, AE, PO, SP)
            OT = H[:, :, :].rearrange("p a b -> p (a b)").rearrange("p (a b) -> p a b", a=4)
            OTX = HC.rearrange("p a b -> p (a b)").rearrange("p (a b) -> p a b", a=2)
            ST, MV = LB[0][:, 0:16], LB[0][:, 16:24]
            tl = tv
            for s, (zb, ot, nt) in enumerate(((ZB, OT, 4), (ZBX, OTX, 2))):
                if s and l:
                    continue
                for q in range(nt):
                    vv = zb[:, q, 256:512]
                    t = DV(lambda e, vv=vv: e.bn_stats(ST[:, 0:6], vv), tl)
                    t = DV(lambda e: e.bn_aggr(MV[:, 0:2], ST[:, 0:6]), t)
                    t1 = act(MV[:, 2:3], MV[:, 1:2], ACT.Ln, t, bias=e1)
                    t1 = act(MV[:, 2:3], MV[:, 2:3], ACT.Exp, t1, scale=-0.5)
                    t = ts(vv, vv, MV[:, 0:1], MV[:, 2:3], ALU.subtract, M, t1)
                    t = tt(vv, vv, GS, M, t, tgs)
                    b, ps, fr = B.take()
                    t = mm(b, [(ps[:, g * 64:(g + 1) * 64], [(WS[:, g, :], vv[:, g * 64:(g + 1) * 64])])
                               for g in range(4)], fr, t, tws)
                    for g in range(4):
                        t2 = stt(ot[:, q, 384 + g * 64:384 + (g + 1) * 64], ps[:, g * 64:(g + 1) * 64],
                                 col(C_BS + 4 * l + g), zb[:, q, g * 64:(g + 1) * 64], A_, M, t, tv)
                    B.done(b, t2)
                    tl = t2
            bl, bt = {}, {}

            def bias_load(h, fr):
                for r in range(2):
                    base = ((l * 6 + h) * 15 + (1 - r)) * 127
                    src = bass.AP(a["rpb"].tensor, base, [[1, 64], [127, 14], [1, 64]])
                    bl[h] = SP.dma(lambda e, src=src, r=r, h=h: e.dma_start(EB[h % 2][64 * r:64 * r + 64, :, :], src),
                                   lane(f"rpb{h % 2}"), fr)

            def bias_turn(h):
                pair = []
                for c in range(2):
                    b, ps, fr = B.take()
                    t = mm(b, [(ps[:, 0:448], [(FL, EB[h % 2][:, 7 * c:7 * c + 7, :])])], fr, bl[h], tnm)
                    pair.append((b, ps))
                for c, (b, ps) in enumerate(pair):
                    bt[h] = tt(EB[h % 2][:, 7 * c:7 * c + 7, :], ps[:, 0:448].rearrange("p (a b) -> p a b", a=7),
                               NM[:, 0:64].unsqueeze(1).broadcast_to([128, 7, 64]), A_, t)
                    B.done(b, bt[h])
            for h in range(2):
                bias_load(h, tv)
                bias_turn(h)
            jobs, hooks = [], {}
            for h in range(6):
                pb_, tile = 64 * (h % 2), h // 2
                E = EB[h % 2].rearrange("p a b -> p (a b)")
                kx = KAX[pb_:pb_ + 64, tile, :]
                hv = slice(h * 64, (h + 1) * 64)
                if 1 <= h < 5:
                    hooks[len(jobs) + 1] = lambda h=h: bias_load(h + 1, (DV.sem, DV.n))
                    hooks[len(jobs) + 3] = lambda h=h: bias_turn(h + 1)
                for q in range(4):
                    qv = QA[pb_:pb_ + 64, tile, q * 128:(q + 1) * 128]
                    jobs.append(([(qv, KA[pb_:pb_ + 64, tile, :], E[:, (6 - 2 * q) * 64:(14 - 2 * q) * 64], None),
                                  (qv, kx, None, None)],
                                 [VA[:, t_, hv] for t_ in range(4)] + [VAX[:, t_, hv] for t_ in range(2)],
                                 OT[:, q, hv], lambda h=h: bt[h]))
                if l == 0:
                    for q in range(2):
                        jobs.append(([(QAX[pb_:pb_ + 64, tile, q * 128:(q + 1) * 128], kx, None, None)],
                                     [VAX[:, t_, hv] for t_ in range(2)], OTX[:, q, hv], None))
            for h in range(6):
                g, tile = h // 3, h % 3
                pb_ = 64 * g
                hv = slice(g * 64, (g + 1) * 64)
                ov = slice(640 + h * 64, 640 + (h + 1) * 64)
                kk, kx = KCx[pb_:pb_ + 64, 0, :], KCX[pb_:pb_ + 64, 0, :]
                for q in range(4):
                    qv = QC[pb_:pb_ + 64, tile, q * 128:(q + 1) * 128]
                    jobs.append(([(qv, kk, None, None), (qv, kx, None, None)],
                                 [VC[:, t_, hv] for t_ in range(4)] + [VCX[:, t_, hv] for t_ in range(2)],
                                 OT[:, q, ov], None))
                if l == 0:
                    for q in range(2):
                        jobs.append(([(QCX[pb_:pb_ + 64, tile, q * 128:(q + 1) * 128], kx, None, None)],
                                     [VCX[:, t_, hv] for t_ in range(2)], OTX[:, q, ov], None))
            to = attention(jobs, LB, PB, tv, tv, hooks)
            if stop == "OT":
                finish(to, src=H)
                return emit(nc, ctx, PE, DV, AE, PO, SP)
            MG, MGX = arena(0, 8, S), arena(4096, 8, LC)
            tq = fence()
            SG = LB[0][:, 0:64]
            SCR = LB[1]
            groups = ((0, 384), (384, 640), (640, 1024))
            jj = 0
            tr = to
            for s, (ot, nt) in enumerate(((OT, 4), (OTX, 2))):
                if s and l:
                    continue
                for q in range(nt):
                    for g, (lo, hi) in enumerate(groups):
                        c_ = SG[:, jj:jj + 1]
                        jj += 1
                        t1 = act(SCR[:, 0:hi - lo], ot[:, q, lo:hi], ACT.Square, tr, (AE.sem, AE.n), accum_out=c_)
                        t1 = act(c_, c_, ACT.Ln, t1, scale=1.0 / (hi - lo), bias=e1)
                        t1 = act(c_, c_, ACT.Exp, t1, scale=-0.5)
                        tr_ = ts(ot[:, q, lo:hi], ot[:, q, lo:hi], c_, None, M, None, t1)
            for s, (ot, mg, nt) in enumerate(((OT, MG, 4), (OTX, MGX, 2))):
                if s and l:
                    continue
                for k in range(8):
                    b, ps, fr = B.take()
                    t = tp([(ps[:, q * 128:(q + 1) * 128], ot[:, q, k * 128:(k + 1) * 128]) for q in range(nt)],
                           fr, tr_)
                    t = act(mg[:, k, :], ps[:, 0:nt * 128], ACT.Copy, t, tq, scale=col(C_GOUT + 8 * l + k))
                    B.done(b, t)
            def gated(g):
                def evac(j, s, ps, t):
                    x = (X, XC)[s][:, j, :]
                    return stt(x, ps, MOD[:, 8 * g + j, s:s + 1], x, M, A_, t)
                return evac
            ms = [(MG, S), (MGX, LC)][:2 - l]
            linear(a["w_o"][l], 8, ms, gated(2), t)

            if stop == f"mix{l}":
                break

            def post(n_, fin=False):
                c0 = C_LN + 32 * l + 16 * n_
                tq = (DV.sem, DV.n)
                r = []
                for s, (x, n) in enumerate(((X, S), (XC, LC))):
                    if s and l:
                        continue
                    t = layernorm(x, x, n, e1, lambda k: col(c0 + k), lambda k: col(c0 + 8 + k), tq)
                    r.append(t)
                    if not fin:
                        for k in range(8):
                            t = ts(x[:, k, :], x[:, k, :], ALPHA, 1.0, M, M, (AE.sem, AE.n), e=PO)
                        r[-1] = t
                return r
            tt_ = post(0)
            if stop == f"post{l}":
                break
            layernorm(X, H, S, ea2, mod(4, 0), mod(3, 0), tt_)
            if l == 0:
                layernorm(XC, HC, LC, ea2, mod(4, 1), mod(3, 1), tt_)
            th = (AE.sem, AE.n)
            G, GX = arena(0, 22, S), arena(22 * 512, 22, LC)
            assert 22 * 768 <= AMAX
            fence()
            ffn(a["w_ffn_in"][l], a["w_ffn_out"][l], [(H[:, :, :], S), (HC, LC)][:2 - l], [G, GX], gated(5), th)
            tt_ = post(1, fin=(l == 1))
            tX, tXC = [tt_], [tt_]
            if stop == f"b2_{l}":
                break
        finish((AE.sem, AE.n), (PO.sem, PO.n), (DV.sem, DV.n))
        return emit(nc, ctx, PE, DV, AE, PO, SP)


def emit(nc, ctx, PE, DV, AE, PO, SP):
    block = ctx.enter_context(nc.Block())

    @block.sync
    def _(eng):
        SP.emit(eng)

    @block.tensor
    def _(eng):
        PE.emit(eng)

    @block.vector
    def _(eng):
        DV.emit(eng)

    @block.scalar
    def _(eng):
        AE.emit(eng)

    @block.gpsimd
    def _(eng):
        PO.emit(eng)


def layout(i):
    f = np.float32
    A = {k: np.ascontiguousarray(v) for k, v in i.items()}

    def feat(v, n=8):
        return v.reshape(n, 128).T

    c = np.zeros((128, NCOL), f)
    for l in range(2):
        c[:, C_NMIX + 8 * l:C_NMIX + 8 * l + 8] = feat(A["norm_mix"][l])
        c[:, C_NFFN + 8 * l:C_NFFN + 8 * l + 8] = feat(A["norm_ffn"][l])
        c[:, C_BMOD + 48 * l:C_BMOD + 48 * l + 48] = feat(A["b_mod_2"][l], 48)
        for h in range(2):
            c[64 * h:64 * h + 64, C_GQ + l] = A["g_q_2"][l]
            c[64 * h:64 * h + 64, C_GK + l] = A["g_k_2"][l]
        c[:, C_GOUT + 8 * l:C_GOUT + 8 * l + 8] = feat(A["g_out_2"][l])
        for n, k in enumerate(("ln1_g_2", "ln1_b_2", "ln2_g_2", "ln2_b_2")):
            o = C_LN + 32 * l + 8 * n
            c[:, o:o + 8] = feat(A[k][l])
        c[:, C_BS + 4 * l:C_BS + 4 * l + 4] = A["b_s_2"][l].T
    c[:, C_GNW] = A["gdn_norm_w"][0]
    c[:, C_CONV:C_CONV + 96] = A["gdn_conv_w"][0].reshape(4, 24, 128).transpose(2, 1, 0).reshape(128, 96)
    for h in range(2):
        c[64 * h:64 * h + 64, C_DQ] = A["dil_q_norm"][0]
        c[64 * h:64 * h + 64, C_DK] = A["dil_k_norm"][0]
    c[0:8, C_ALOG] = A["gdn_a_log"][0]
    c[0:8, C_DT] = A["gdn_dt_bias"][0]
    cc = np.stack([feat(A["c_2"][0]), feat(A["c_ctx_2"])], axis=2)
    c[:, C_C:C_C + 16] = cc.reshape(128, 16)
    rpb = np.zeros((2, 6, 15, 127), f)
    rpb[:, :, :, 48:79] = A["rpb_2"]
    return {
        "x": np.ascontiguousarray(A["x"][0].T.reshape(8, 128, S).transpose(1, 0, 2)),
        "ctx": np.ascontiguousarray(A["ctx_2"][0].T.reshape(8, 128, LC).transpose(1, 0, 2)),
        "cols": c, "kc": constants(), "rpb": rpb,
        "gdn_w_in": A["gdn_w_in"][0], "gdn_w_out": A["gdn_w_out"][0],
        "dil_w_in": A["dil_w_in"][0], "dil_w_out": A["dil_w_out"][0],
        "ffn_w_in": A["ffn_w_in"], "ffn_w_out": A["ffn_w_out"],
        "w_mod": A["w_mod_2"], "w_in": A["w_in_2"], "w_o": A["w_o_2"],
        "w_ffn_in": A["w_ffn_in_2"], "w_ffn_out": A["w_ffn_out_2"],
        "w_sT": np.ascontiguousarray(A["w_s_2"].transpose(0, 3, 1, 2)),
        "g_sgu": A["g_sgu_2"],
    }


def kernel(**inputs):
    import concourse.bacc as bacc
    from concourse.bass_utils import run_bass_kernel_spmd

    arrays = layout({k: np.asarray(v) for k, v in inputs.items()})
    nc = bacc.Bacc("TRN2", target_bir_lowering=False, num_devices=1)
    aps = {k: nc.dram_tensor("in_" + k, v.shape, F32, kind="ExternalInput").ap() for k, v in arrays.items()}
    out = nc.dram_tensor("out_0", (128, 8, S), F32, kind="ExternalOutput").ap()
    build(nc, aps, out)
    r = run_bass_kernel_spmd(nc, [{"in_" + k: v for k, v in arrays.items()}], core_ids=[0])
    y = np.asarray(r.results[0]["out_0"])
    return y.transpose(2, 1, 0).reshape(1, S, D)
```

```python
from contextlib import ExitStack

import numpy as np

import concourse.bass as bass
from concourse import mybir

F32 = mybir.dt.float32
F32R = mybir.dt.float32r
ALU = mybir.AluOpType
ACT = mybir.ActivationFunctionType
AX = mybir.AxisListType.X

S, LC, D = 512, 256, 1024
FF = 2816
ALPHA = 4.0 ** 0.25
EPS = 1e-6
BIG = 1e30
NS = 3
UN = 33792

C_NMIX, C_NFFN, C_GNW, C_CONV, C_DQ, C_DK, C_ALOG, C_DT = 0, 16, 32, 33, 129, 130, 131, 132
C_C, C_BMOD, C_GQ, C_GK, C_GOUT, C_LN, C_BS = 133, 149, 245, 247, 249, 265, 329
NCOL = 337
K_ID, K_ONE, K_BONE, K_EPS, K_RES = 0, 128, 256, 384, 392
K_GDN = K_RES
N_GDN = 7 * 128 + 128 + 512
K_DIL = K_GDN + N_GDN
N_DIL = 1280
K_NA = K_DIL + N_DIL
N_NA = 64 + 1024 + 128 + 128
NK = K_NA + N_NA


def constants():
    f = np.float32
    k = np.zeros((128, NK), f)
    i = np.arange(128)[:, None]
    j = np.arange(128)[None, :]
    k[:, K_ID:K_ID + 128] = i == j
    k[:, K_ONE:K_ONE + 128] = 1
    k[:, K_BONE:K_BONE + 128] = i // 64 == j // 64
    for n, e in enumerate((EPS, 64 * EPS, ALPHA * ALPHA * EPS, 1.0, 128 * EPS)):
        k[:, K_EPS + n] = e
    g = K_GDN
    for n in range(7):
        b = 1 << n
        k[:, g:g + 128] = (i // (2 * b) == j // (2 * b)) & (i % (2 * b) >= b) & (j % (2 * b) < b)
        g += 128
    k[:, g:g + 128] = i <= j
    g += 128
    k[:, g:g + 512] = np.arange(512) % 128 != 0
    g = K_DIL
    d0 = 128 + i - np.arange(256)[None, :]
    k[:, g:g + 256] = np.where((d0 >= 0) & (d0 <= 128), -d0, -BIG)
    d = 384 + i - np.arange(512)[None, :]
    k[:, g + 256:g + 768] = np.where((d >= 0) & (d % 4 == 0), -d, -BIG)
    k[:, g + 768:g + 1280] = np.where((d >= 0) & (d % 16 == 0), -d, -BIG)
    g = K_NA
    c, cc = i % 64, np.arange(64)[None, :]
    st = np.clip(c - 8, 0, 48)
    k[:, g:g + 64] = np.where((cc >= st) & (cc < st + 16), 0, -BIG)
    g += 64
    t = np.arange(512)
    inv = (f(1.0) / (f(10000.0) ** (np.arange(16, dtype=f) / f(16)))).astype(f)
    p = np.arange(128) % 64
    pos = np.where((p // 32 == 0)[:, None], (t // 64)[None, :], (t % 64)[None, :]).astype(f)
    ang = (pos * inv[p % 16][:, None]).astype(f)
    k[:, g:g + 512] = np.cos(ang)
    k[:, g + 512:g + 1024] = np.sin(ang)
    g += 1024
    first = (np.arange(128) % 32) < 16
    k[:, g:g + 128] = np.where(first[None, :], -1.0 * (i == j + 16), 1.0 * (i == j - 16))
    k[:, g + 128:g + 256] = (i // 64 == j // 64) & (i % 64 == 63 - j % 64)
    return k


class Engine:

    def __init__(self, sem):
        self.sem, self.n, self.queue, self.seen = sem, 0, [], {}

    def wait(self, *after):
        for t in after:
            if t is None:
                continue
            if isinstance(t, list):
                self.wait(*t)
            elif self.seen.get(id(t[0]), 0) < t[1]:
                self.seen[id(t[0])] = t[1]
                self.queue.append((None, t[0], t[1]))

    def __call__(self, fn, *after):
        self.wait(*after)
        self.n += 1
        self.queue.append((fn, self.sem, 1))
        return (self.sem, self.n)

    def quiet(self, fn, *after):
        self.wait(*after)
        self.queue.append((fn, None, 0))

    def dma(self, fn, lane, *after):
        self.wait(*after)
        lane[1] += 16
        self.queue.append((fn, lane[0], 16))
        return (lane[0], lane[1])

    def emit(self, eng):
        for fn, sem, n in self.queue:
            if fn is None:
                eng.wait_ge(sem, n)
            elif sem is None:
                fn(eng)
            else:
                fn(eng).then_inc(sem, n)


class Banks:

    def __init__(self, tiles):
        self.tiles, self.free, self.i = tiles, [None] * len(tiles), 0

    def take(self):
        b = self.i % len(self.tiles)
        self.i += 1
        return b, self.tiles[b], self.free[b]

    def done(self, b, token):
        self.free[b] = token


def build(nc, a, out, stop=None, dump=None):
    ctx = ExitStack()
    with ctx:
        def sb(name, shape):
            return ctx.enter_context(nc.sbuf_tensor(name, shape, F32))

        def sem(name):
            return ctx.enter_context(nc.semaphore(name))

        X = sb("X", [128, 8, S])
        ring = [sb(f"ring{i}", [128, 8, 512])[:, :, :] for i in range(NS)]
        KC = sb("KC", [128, K_RES])
        COL = sb("COL", [128, NCOL])
        MODS = [sb(f"MOD{l}", [128, 48, 2]) for l in range(2)]
        SCT = sb("SCT", [128, 8, 2])
        AC = sb("AC", [128, 32])
        SQ = [sb(f"SQ{i}", [128, 512]) for i in range(2)]
        RR = [sb(f"RR{i}", [128, 512]) for i in range(2)]
        at = -(-nc.sbuf_base // 64) * 64
        U = nc.alloc_sbuf_tensor_at("U", [128, UN], F32, offset=at)
        H = U[:, 0:4096].rearrange("p (a b) -> p a b", a=8)
        psum = [ctx.enter_context(nc.psum_tensor(f"ps{i}", [128, 512], F32))[:, :] for i in range(8)]

        PE, DV, AC_, PO, SP = (Engine(sem(n)) for n in ("s_pe", "s_dve", "s_act", "s_pool", "s_sp"))
        AE = AC_
        wl = [[sem(f"w{i}"), 0] for i in range(NS)]
        misc = {}

        def lane(name):
            if name not in misc:
                misc[name] = [sem("d_" + name), 0]
            return misc[name]

        B = Banks(psum)
        ident = KC[:, K_ID:K_ID + 128]
        ones = KC[:, K_ONE:K_ONE + 128]
        bones = KC[:, K_BONE:K_BONE + 128]
        e1, e64, ea2, one1, e128 = (KC[:, K_EPS + n:K_EPS + n + 1] for n in range(5))

        def col(n):
            return COL[:, n:n + 1]

        def view(v, shape):
            if len(shape) == 2:
                v = v.rearrange("p (a b) -> p a b", a=shape[0])
            elif len(shape) == 3:
                v = v.rearrange("p (a b c) -> p a b c", a=shape[0], b=shape[1])
            return v

        def arena(off, *shape):
            off += 4096
            assert off + int(np.prod(shape)) <= UN
            return view(U[:, off:off + int(np.prod(shape))], shape)

        def last():
            return [(e.sem, e.n) for e in (PE, DV, AE, PO) if e.n]

        def fence():
            t = last()
            for e in (DV, AE, PO):
                e.wait(t)
            return t

        slot_free = [None] * NS
        slot_n = [0]

        def weights(*parts):
            i = slot_n[0] % NS
            slot_n[0] += 1
            SP.wait(slot_free[i])
            for view, src in parts:
                t = SP.dma(lambda e, v=view(ring[i]), s=src: e.dma_start(v, s), wl[i])
            return i, ring[i], t

        def wtile(src, k, n):
            return weights((lambda r: r[:, 0:k, 0:n], src.rearrange("(k p) n -> p k n", p=128)))

        def mm(bank, groups, *after):
            PE.wait(*after)
            n = len(groups)
            t = None
            for g, (o, prs) in enumerate(groups):
                for i, (l, r) in enumerate(prs):
                    f = (lambda e, o=o, l=l, r=r, st=(i == 0), sp=(i == len(prs) - 1):
                         e.matmul(o, l, r, start=st, stop=sp))
                    if g == n - 1 and i == len(prs) - 1:
                        t = PE(f)
                    else:
                        PE.quiet(f)
            return t

        def tp(outs, *after):
            PE.wait(*after)
            t = None
            for o, i in outs:
                k = i.shape[0]
                f = lambda e, o=o, i=i, k=k: e.transpose(o, i, ident[0:k, 0:k])
                t = PE(f) if i is outs[-1][1] else PE.quiet(f)
            return t

        table = [None]

        def act(o, i, fn, *after, **kw):
            if fn in (ACT.Exp, ACT.Ln) and table[0] != "log":
                AE.quiet(lambda e: e.preload_act_table_set("natural_log_exp_and_others"))
                table[0] = "log"
            elif fn in (ACT.Silu, ACT.Gelu_apprx_tanh, ACT.Sigmoid):
                table[0] = "other"
            return AE(lambda e: e.activation(o, i, fn, **kw), *after)

        def tt(o, x, y, op, *after, e=None):
            return (e or DV)(lambda q: q.tensor_tensor(o, x, y, op), *after)

        def ts(o, x, s1, s2, o0, o1, *after, e=None):
            if s2 is None:
                return (e or DV)(lambda q: q.tensor_scalar(o, x, s1, None, o0), *after)
            return (e or DV)(lambda q: q.tensor_scalar(o, x, s1, s2, o0, o1), *after)

        def stt(o, x, s, y, o0, o1, *after):
            return DV(lambda q: q.scalar_tensor_tensor(o, x, s, y, o0, o1), *after)

        def cp(o, x, *after):
            return DV(lambda q: q.tensor_copy(o, x), *after)

        M, A_ = ALU.mult, ALU.add

        sqf, rrf = [None, None], [None, None]
        cnt = {"sq": 0, "rr": 0}

        def sq_of(src, n, *after):
            i = cnt["sq"] % 2
            cnt["sq"] += 1
            t = act(SQ[i][:, 0:n], src, ACT.Square, sqf[i], *after)
            return i, SQ[i][:, 0:n], t

        def rstd(ps, bank, n, scale, eps, t):
            i = cnt["rr"] % 2
            cnt["rr"] += 1
            r = RR[i][:, 0:n]
            t = act(r, ps, ACT.Ln, t, rrf[i], scale=scale, bias=eps)
            B.done(bank, t)
            t = act(r, r, ACT.Exp, t, scale=-0.5)
            return i, r, t

        def sumsq(srcs, n, mat, *after):
            b, ps, fr = B.take()
            PE.wait(fr)
            for k, s in enumerate(srcs):
                i, q, t = sq_of(s, n, *after)
                f = (lambda e, q=q, k=k: e.matmul(ps[:, 0:n], mat, q, start=(k == 0),
                                                  stop=(k == len(srcs) - 1)))
                t = PE(f, t)
                sqf[i] = t
            return b, ps[:, 0:n], t

        def rms(x, h, w, *after):
            b, ps, t = sumsq([x[:, k, :] for k in range(8)], S, ones, *after)
            i, r, t = rstd(ps, b, S, 1.0 / D, e1, t)
            hold = last()
            for k in range(8):
                t = stt(h[:, k, :], x[:, k, :], col(w + k), r, M, M, t, hold)
            rrf[i] = t
            return t

        def layernorm(x, h, n, eps, g, b_, *after):
            hold = last()
            bk, ps, fr = B.take()
            t = mm(bk, [(ps[:, 0:n], [(ones, x[:, k, :]) for k in range(8)])], fr, *after)
            toks = []
            for k in range(8):
                toks.append(stt(h[:, k, :], ps[:, 0:n], -1.0 / D, x[:, k, :], M, A_, t, hold))
            B.done(bk, toks[-1])
            b, ps, fr = B.take()
            PE.wait(fr)
            for k in range(8):
                i, q, tq = sq_of(h[:, k, :], n, toks[k])
                t = PE(lambda e, q=q, k=k: e.matmul(ps[:, 0:n], ones, q, start=(k == 0), stop=(k == 7)), tq)
                sqf[i] = t
            i, r, t = rstd(ps[:, 0:n], b, n, 1.0 / D, eps, t)
            for k in range(8):
                tk = tt(h[:, k, :], h[:, k, :], r, M, t)
                rrf[i] = tk
                to = act(h[:, k, :], h[:, k, :], ACT.Identity, tk, scale=g(k), bias=b_(k))
            return to

        def linear(w, kt, streams, evac, *after):
            n = w.shape[1]
            PE.wait(*after)
            late = []
            for c in range(0, n, 512):
                m = min(512, n - c)
                si, sl, tw = wtile(w[:, c:c + m], kt, m)
                for j in range(m // 128):
                    for s, (h, nt) in enumerate(streams):
                        if h is None:
                            continue
                        b, ps, fr = B.take()
                        t = mm(b, [(ps[:, 0:nt], [(sl[:, k, j * 128:(j + 1) * 128], h[:, k, :])
                                                  for k in range(kt)])], fr, tw)
                        if late:
                            late.pop()()
                        late.append(lambda b=b, j=c // 128 + j, s=s, o=ps[:, 0:nt], t=t: B.done(b, evac(j, s, o, t)))
                slot_free[si] = t
            late.pop()()

        def linear_tok(w, streams, evac, *after):
            n = w.shape[1]
            PE.wait(*after)
            si, sl, tw = wtile(w, 8, n)
            for s, (h, nt) in enumerate(streams):
                for q in range(nt // 128):
                    b, ps, fr = B.take()
                    t = mm(b, [(ps[:, 0:n], [(h[:, k, q * 128:(q + 1) * 128], sl[:, k, 0:n])
                                             for k in range(8)])], fr, tw)
                    B.done(b, evac(q, s, ps[:, 0:n], t))
            slot_free[si] = t

        def ru(off, n):
            return nc.alloc_sbuf_tensor_at(f"R{off}", [128, n], F32R, offset=at + 4 * off)[:, :]

        HR = [[view(ru(o, 4096), (8, S)) for o in (0, 4096)],
              [view(ru(o, 2048), (8, LC)) for o in (8192, 10240)]]
        WR = [[ru(12288 + 4096 * i + 2048 * p, 2048) for p in range(2)] for i in range(3)]
        GR_ = [[[view(ru(24576 + 2048 * b + 1024 * p, 1024), (2, S)) for p in range(2)] for b in range(2)],
               [[view(ru(28672 + 1024 * b + 512 * p, 512), (2, LC)) for p in range(2)] for b in range(2)]]
        HT = [view(U[:, 24576:28672], (8, S)), view(U[:, 28672:30720], (8, LC))]
        TG = [U[:, 30720 + 512 * i:31232 + 512 * i] for i in range(2)]

        def split(hi, lo, src, *after, e=None):
            t = (e or PO)(lambda q: q.tensor_copy(hi, src), *after)
            return tt(lo, src, hi, ALU.subtract, t)

        def split_act(hi, lo, src, *after):
            t = act(hi, src, ACT.Copy, *after)
            return tt(lo, src, hi, ALU.subtract, t)

        def three(ws, xs, ks):
            out = []
            for n, k in enumerate(ks):
                out += [(ws(0, k), xs(0, k)), (ws(0, k), xs(1, k)), (ws(1, k), xs(0, k))]
            return out

        def ffn(wi, wo, ns, evac, *after):
            tw = [None] * 3
            wfree = [None] * 3
            gfree = [[None] * 2, [None] * 2]
            gtok = [[None] * 2, [None] * 2]
            tgf = [None, None]
            qn = [0]
            outs = {}

            def w_in(c):
                si, sl, t = weights(
                    (lambda r: r[:, :, 0:256], wi[:, c * 256:(c + 1) * 256].rearrange("(k p) n -> p k n", p=128)),
                    (lambda r: r[:, :, 256:512],
                     wi[:, FF + c * 256:FF + (c + 1) * 256].rearrange("(k p) n -> p k n", p=128)))
                for p in range(2):
                    hi, lo = (view(z, (8, 256)) for z in WR[p])
                    tw[p] = split_act(hi, lo, sl[:, :, p * 256:(p + 1) * 256], t, wfree[p])
                slot_free[si] = [tw[0], tw[1]]

            def w_out(c):
                if c % 2 == 0:
                    k = min(4, 22 - 2 * c)
                    outs["w"] = weights((lambda r: r.rearrange("p a b -> p (a b)")[:, 0:1024 * k].rearrange(
                        "p (k n) -> p k n", k=k), wo[256 * c:256 * c + 128 * k, :].rearrange("(k p) n -> p k n", p=128)))
                si, sl, t = outs["w"]
                src = sl.rearrange("p a b -> p (a b)")[:, 2048 * (c % 2):2048 * (c % 2) + 2048]
                hi, lo = WR[2]
                tw[2] = split_act(hi, lo, src, t, wfree[2])
                slot_free[si] = tw[2]

            def inner(c):
                late = []
                for j in range(2):
                    for s, n in enumerate(ns):
                        bk = []
                        for p in range(2):
                            b, ps, fr = B.take()
                            w = lambda part, k: view(WR[p][part], (8, 256))[:, k, j * 128:(j + 1) * 128]
                            x = lambda part, k: HR[s][part][:, k, :]
                            t = mm(b, [(ps[:, 0:n], three(w, x, range(8)))], fr, tw[p])
                            bk.append((b, ps, t))
                            if p == 0 and late:
                                late.pop()()
                        wfree[0] = wfree[1] = t

                        def ev(bk=bk, s=s, n=n, j=j):
                            (ba, pa, ta), (bb, pb, tb) = bk
                            i = qn[0] % 2
                            qn[0] += 1
                            t = act(SQ[i][:, 0:n], pa[:, 0:n], ACT.Silu, ta, sqf[i])
                            B.done(ba, t)
                            tg = tt(TG[i][:, 0:n], SQ[i][:, 0:n], pb[:, 0:n], M, t, tb, tgf[i])
                            sqf[i] = tg
                            B.done(bb, tg)
                            hi, lo = (GR_[s][c % 2][p][:, j, :] for p in range(2))
                            t = split(hi, lo, TG[i][:, 0:n], tg, gfree[s][c % 2])
                            tgf[i] = t
                            gtok[s][c % 2] = t
                        late.append(ev)
                return late.pop()

            def outer(c):
                for s, n in enumerate(ns):
                    late = []
                    for m in range(8):
                        b, ps, fr = B.take()
                        w = lambda part, k: view(WR[2][part], (2, 1024))[:, k, m * 128:(m + 1) * 128]
                        x = lambda part, k: GR_[s][c % 2][part][:, k, :]
                        t = mm(b, [(ps[:, 0:n], three(w, x, range(2)))], fr, tw[2], gtok[s][c % 2])
                        if late:
                            late.pop()()
                        late.append(lambda m=m, s=s, o=ps[:, 0:n], t=t, b=b: B.done(b, evac(m, s, o, t)))
                    gfree[s][c % 2] = t
                    late.pop()()
                wfree[2] = t

            w_in(0)
            PE.wait(*after)
            for c in range(12):
                tail = inner(c) if c < 11 else None
                if c == 0:
                    w_out(0)
                if c < 10:
                    w_in(c + 1)
                if c:
                    if tail:
                        tail()
                        tail = None
                    outer(c - 1)
                    if c < 11:
                        w_out(c)
                if tail:
                    tail()

        lfree, pfree, rfree = [None] * 2, [None] * 2, [None] * 4

        def attention(jobs, Lb, Pb, ready, hooks={}):
            state, turned = [], []

            def scores(n):
                segs, _, _, note = jobs[n]
                tn = note() if note else None
                L = Lb[n % 2]
                m = AC[:, 8 * (n % 4):8 * (n % 4) + 8]
                off, info = 0, []
                for g, (q, k, bias) in enumerate(segs):
                    w = k.shape[1]
                    b, ps, fr = B.take()
                    t = mm(b, [(ps[:, 0:w], [(q, k)])], fr, ready)
                    if bias is None:
                        t = DV(lambda e, ps=ps, w=w, g=g: e.reduce_max(m[:, g:g + 1], ps[:, 0:w], AX),
                               t, rfree[n % 4])
                        info.append((ps[:, 0:w], off, w, b))
                    else:
                        t = DV(lambda e, ps=ps, w=w, g=g, off=off, bias=bias: e.tensor_tensor_reduce(
                            L[:, off:off + w], ps[:, 0:w], bias, 1.0, 0.0 - 3e38, A_, ALU.max,
                            m[:, g:g + 1]), t, lfree[n % 2], rfree[n % 4], tn)
                        B.done(b, t)
                        info.append((L[:, off:off + w], off, w, None))
                    off += w
                t = DV(lambda e: e.tensor_reduce(m[:, 3:4], m[:, 0:len(segs)], AX, ALU.max, negate=True), t)
                for g, (src, f, w, b) in enumerate(info):
                    te = act(L[:, f:f + w], src, ACT.Exp, t, lfree[n % 2], bias=m[:, 3:4], accum_out=m[:, 4 + g:5 + g])
                    if b is not None:
                        B.done(b, te)
                t = DV(lambda e: e.reduce_sum(m[:, 3:4], m[:, 4:4 + len(segs)], AX), te)
                t = DV(lambda e: e.reciprocal(m[:, 3:4], m[:, 3:4]), t)
                state.append((te, t, off))

            def turn(n):
                te, tr, width = state[n]
                L, P = Lb[n % 2], Pb[n % 2]
                nb = width // 128
                tc = []
                for c in range(0, nb, 4):
                    k = min(4, nb - c)
                    b, ps, fr = B.take()
                    t = tp([(ps[:, i * 128:(i + 1) * 128], L[:, (c + i) * 128:(c + i + 1) * 128])
                            for i in range(k)], fr, te)
                    o_, i_ = P[:, c * 128:(c + k) * 128], ps[:, 0:k * 128]
                    if (c // 4) % 2:
                        t2 = cp(o_, i_, t, pfree[n % 2])
                    else:
                        t2 = act(o_, i_, ACT.Copy, t, pfree[n % 2])
                    B.done(b, t2)
                    tc.append(t2)
                lfree[n % 2] = t
                turned.append(tc)

            def values(n):
                _, vals, o, _ = jobs[n]
                P = Pb[n % 2]
                b, ps, fr = B.take()
                t = mm(b, [(ps[:, 0:64], [(P[:, i * 128:(i + 1) * 128], v) for i, v in enumerate(vals)])],
                       fr, turned[n])
                pfree[n % 2] = t
                r = AC[:, 8 * (n % 4) + 3:8 * (n % 4) + 4]
                t = ts(o, ps[:, 0:64], r, None, M, None, t, state[n][1])
                B.done(b, t)
                rfree[n % 4] = t
                return t

            t = None
            for n in range(len(jobs) + 2):
                for h in hooks.get(n, ()):
                    h()
                if n < len(jobs):
                    scores(n)
                if 0 <= n - 1 < len(jobs):
                    turn(n - 1)
                if n >= 2:
                    t = values(n - 2)
            return t

        mrf, MR = [None], [None]

        def mod_piece(l, c):
            w = []

            def half(g):
                si, sl, tw = w[0]
                b, ps, fr = B.take()
                t = mm(b, [(ps[0:2, :], [(SCT[:, k, :], sl[:, k, :]) for k in range(4 * g, 4 * g + 4)])], fr, tw, tsc)
                return si, b, ps[0:2, :], t

            def first():
                w.append(wtile(a["w_mod"][l][:, c * 512:(c + 1) * 512], 8, 512))
                si, b, ps, t = half(0)
                B.done(b, cp(MR[0], ps, t, mrf[0]))

            def second():
                si, b, ps, t = half(1)
                slot_free[si] = t
                t = tt(MR[0], MR[0], ps, A_, t)
                B.done(b, t)
                b, ps, fr = B.take()
                t = tp([(ps[:, 2 * j:2 * j + 2], MR[0][:, j * 128:(j + 1) * 128]) for j in range(4)], fr, t)
                mrf[0] = t
                o = C_BMOD + 48 * l + 4 * c
                t = tt(MODS[l][:, 4 * c:4 * c + 4, :], ps[:, 0:8].rearrange("p (a b) -> p a b", b=2),
                       COL[:, o:o + 4].unsqueeze(2).broadcast_to([128, 4, 2]), A_, t)
                B.done(b, t)
                if c in (2, 3, 8, 9):
                    z = MODS[l][:, 4 * c:4 * c + 4, :]
                    t = ts(z, z, 1.0, None, A_, None, t)
            return first, second

        def finish(*after, src=None):
            AE.wait(*after)
            t = AE.dma(lambda e: e.dma_start(out, (src or X)[:, :, :]), lane("out"))
            AE.wait(t)

        tk0 = AE.dma(lambda e: e.dma_start(KC[:, :], a["kc"][:, 0:K_RES]), lane("kc"))
        tcol = AE.dma(lambda e: e.dma_start(COL[:, :], a["cols"]), lane("col"))
        tx = AE.dma(lambda e: e.dma_start(X[:, :, :], a["x"]), lane("x"))
        boot = [tk0, tcol, tx]
        for e in (PE, DV, AE, PO):
            e.wait(boot)

        tsc = act(SCT[:, :, :], COL[:, C_C:C_C + 16].rearrange("p (k s) -> p k s", s=2), ACT.Silu)

        GM = arena(0, 8, 128)
        tgm = AE.dma(lambda e: e.dma_start(arena(0, 1024), a["kc"][:, K_GDN:K_GDN + 1024]), lane("gm"))
        o_ = 1024
        rows = [arena(o_ + 512 * n, 512) for n in range(2)]
        o_ += 2 * 512
        GC = arena(o_, 4, 8); o_ += 32
        BT = arena(o_, 4, 8); o_ += 32
        EG = arena(o_, 4, 8); o_ += 32
        KB = arena(o_, 4, 8); o_ += 32
        GL = arena(o_, 4, 8); o_ += 32
        TL = arena(o_, 4, 8); o_ += 32
        CD = arena(o_, 4, 8); o_ += 32
        NE = arena(o_, 8); o_ += 8
        bufs = [o_ + 2048 * n for n in range(10)]
        SO = o_ + 20480
        assert SO + 2048 <= 24960
        rs, res = (arena(bufs[9] + 512 * n, 512)[0:8, :] for n in range(2))
        tres = AE.dma(lambda e: e.dma_start(res, a["kc"][0:8, K_GDN + 1024:K_GDN + 1536]), lane("res"))
        cv = [arena(bufs[8], 516), arena(bufs[8] + 516, 516)]
        th = rms(X, H, C_NMIX, boot)
        hs = [(H, S)]
        wg = a["gdn_w_in"]
        si, sl, tw = weights((lambda r: r[:, :, 0:16],
                              wg[:, 4096:4112].rearrange("(k p) n -> p k n", p=128)))
        ba, pa, fa = B.take()
        bb, pb, fb = B.take()
        ta = mm(ba, [(pa[0:8, :], [(sl[:, k, 0:8], H[:, k, :]) for k in range(8)])], fa, tw, th)
        tb = mm(bb, [(pb[0:8, :], [(sl[:, k, 8:16], H[:, k, :]) for k in range(8)])], fb)
        slot_free[si] = tb
        rg, rb = (r[0:8, :] for r in rows)
        dt = COL[0:8, C_DT:C_DT + 1]
        t1 = act(NE[0:8, 0:1], COL[0:8, C_ALOG:C_ALOG + 1], ACT.Exp)
        t2 = act(rs, pa[0:8, :], ACT.Abs, ta, bias=dt)
        t3 = ts(rg, pa[0:8, :], dt, 0.0, A_, ALU.max, t2)
        B.done(ba, t3)
        t2 = act(rs, rs, ACT.Exp, t2, scale=-1.0)
        t2 = act(rs, rs, ACT.Ln, t2, bias=one1[0:8, :])
        t3 = tt(rg, rg, rs, A_, t2, t3)
        t3 = ts(rg, rg, NE[0:8, 0:1], -1.0, M, M, t3, t1)
        t3 = DV(lambda e: e.tensor_tensor_scan(rs, res, rg, 0.0, M, A_), t3, tres)
        tgr = cp(rg, rs, t3)
        t2 = act(rb, pb[0:8, :], ACT.Sigmoid, tb)
        B.done(bb, t2)
        b, ps, fr = B.take()
        t = tp([(ps[:, c * 8:c * 8 + 8], rg[:, c * 128:(c + 1) * 128]) for c in range(4)]
               + [(ps[:, 32 + c * 8:40 + c * 8], rb[:, c * 128:(c + 1) * 128]) for c in range(4)],
               fr, tgr, t2)
        t3 = cp(GC.rearrange("p a b -> p (a b)"), ps[:, 0:32], t)
        t4 = cp(BT.rearrange("p a b -> p (a b)"), ps[:, 32:64], t)
        B.done(b, t4)
        teg = act(EG, GC, ACT.Exp, t3)
        tkb = tt(KB, EG, BT, M, teg, t4)
        tsetup = [t4, tkb]

        def conv(j, dst, ps, t):
            i = cnt.setdefault("cv", 0) % 2
            cnt["cv"] += 1
            c = cv[i]
            w = C_CONV + 4 * j
            fr = cvf[i]
            t0 = PO(lambda e, c=c: e.memset(c[:, 0:3], 0.0), fr, tgr, hold)
            tc = act(c[:, 3:515], ps, ACT.Copy, t, fr, tgr, hold)
            tv = ts(dst, c[:, 3:515], col(w + 3), None, M, None, tc, t0, hold)
            for n in (2, 1, 0):
                tv = stt(dst, c[:, n:n + 512], col(w + n), dst, M, A_, tv)
            cvf[i] = tv
            act(dst, dst, ACT.Silu, tv)
            return tc

        cvf = [None, None]
        for hg in range(2):
            hold = last() if hg else None
            bf = [arena(o, 4, 512) for o in bufs]
            q, k, v, vb, kbe, ktl, DT, Xb, AT, qk = bf
            T, TT = v, k
            tp_ = None
            for which, dst in ((0, q), (1, k), (2, v)):
                w = wg[:, which * 1024 + hg * 512:which * 1024 + (hg + 1) * 512]
                linear(w, 8, hs, lambda j, s, ps, t: conv(which * 8 + hg * 4 + j, dst[:, j, :], ps, t), th)
            tsil = (AE.sem, AE.n)
            gl_tok = []
            ends = []
            for h in range(4):
                hh = hg * 4 + h
                for x_, scale, eps in ((q, 128.0, None), (k, 1.0, e1)):
                    b, ps, t = sumsq([x_[:, h, :]], 512, ones, tsil)
                    if eps is None:
                        i, r, t = rstd(ps, b, 512, 128.0, e128, t)
                    else:
                        i, r, t = rstd(ps, b, 512, 1.0, e1, t)
                    t = tt(x_[:, h, :], x_[:, h, :], r, M, t)
                    rrf[i] = t
                tn = t
                b, ps, fr = B.take()
                t = mm(b, [(ps[:, :], [(ident[0:8, hh:hh + 1].broadcast_to([8, 128]), rb)])], fr, tsetup)
                t = tt(Xb[:, h, :], k[:, h, :], ps[:, :], M, t, tn)
                B.done(b, t)
                b, ps, fr = B.take()
                t = mm(b, [(ps[:, :], [(ident[0:8, hh:hh + 1].broadcast_to([8, 128]), rg)])], fr)
                t4 = cp(GL[:, :, hh], ps.rearrange("p (a b) -> p a b", a=4)[:, :, 127], t)
                for c in range(4):
                    t4 = ts(DT[:, h, c * 128:(c + 1) * 128], ps[:, c * 128:(c + 1) * 128], GC[:, c, hh:hh + 1],
                            0.0, ALU.subtract, ALU.min, t)
                i = cnt["rr"] % 2
                cnt["rr"] += 1
                te = act(RR[i][:, :], ps[:, :], ACT.Exp, t4, rrf[i])
                B.done(b, te)
                td = act(DT[:, h, :], DT[:, h, :], ACT.Exp, t4)
                td = tt(DT[:, h, :].rearrange("p (a b) -> p a b", a=4), DT[:, h, :].rearrange("p (a b) -> p a b", a=4),
                        GM[:, 7:8, :].broadcast_to([128, 4, 128]), M, td, tgm)
                b, ps, fr = B.take()
                t = mm(b, [(ps[:, c * 128:(c + 1) * 128], [(k[:, h, c * 128:(c + 1) * 128],
                                                            Xb[:, h, c * 128:(c + 1) * 128])])
                           for c in range(4)], fr, (DV.sem, DV.n))
                ta_ = tt(AT[:, h, :], ps[:, :], DT[:, h, :], M, t, td)
                B.done(b, ta_)
                b, ps, fr = B.take()
                t = mm(b, [(ps[:, c * 128:(c + 1) * 128], [(k[:, h, c * 128:(c + 1) * 128],
                                                            q[:, h, c * 128:(c + 1) * 128])])
                           for c in range(4)], fr)
                t5 = tt(qk[:, h, :], ps[:, :], DT[:, h, :], M, t)
                B.done(b, t5)
                t6 = tt(q[:, h, :], q[:, h, :], RR[i][:, :], M, t, te)
                rrf[i] = t6
                ends += [t5, t6, ta_]
            h0 = hg * 4
            t = tt(TL[:, :, h0:h0 + 4], GL[:, :, h0:h0 + 4], GC[:, :, h0:h0 + 4], ALU.subtract, t4)
            t1 = act(TL[:, :, h0:h0 + 4], TL[:, :, h0:h0 + 4], ACT.Exp, t)
            t2 = act(CD[:, :, h0:h0 + 4], GL[:, :, h0:h0 + 4], ACT.Exp, t)
            kv = []
            for c in range(4):
                b, ps, fr = B.take()
                t = tp([(ps[:, h * 128:(h + 1) * 128], v[:, h, c * 128:(c + 1) * 128]) for h in range(4)], fr)
                p4 = ps[:, :].rearrange("p (a b) -> p a b", a=4)
                as4 = lambda z: z[:, c, :].rearrange("p (a b) -> p a b", a=4)
                bc = lambda z: z[:, c, h0:h0 + 4].unsqueeze(2).broadcast_to([128, 4, 128])
                t = tt(as4(vb), p4, bc(BT), M, t)
                B.done(b, t)
                kv.append(t)
                b, ps, fr = B.take()
                t = tp([(ps[:, h * 128:(h + 1) * 128], k[:, h, c * 128:(c + 1) * 128]) for h in range(4)], fr)
                p4 = ps[:, :].rearrange("p (a b) -> p a b", a=4)
                t_ = tt(as4(kbe), p4, bc(KB), M, t)
                t = tt(as4(ktl), p4, bc(TL), M, t, t1)
                B.done(b, t)
                kv.append(t)
            free3 = [(PE.sem, PE.n)]
            tT = [kv] * 4
            for n in range(7):
                for h in range(4):
                    c4 = lambda z: z[:, h, :].rearrange("p (a b) -> p a b", a=4)
                    idb = ident.unsqueeze(1).broadcast_to([128, 4, 128])
                    sl4 = lambda z, c: ident if z is None else z[:, h, c * 128:(c + 1) * 128]
                    Tn, TTn = (None, None) if n == 0 else (T, TT)
                    b, ps, fr = B.take()
                    t = mm(b, [(ps[:, c * 128:(c + 1) * 128], [(AT[:, h, c * 128:(c + 1) * 128], sl4(Tn, c))])
                               for c in range(4)], fr, tT[h], ends)
                    tx_ = tt(c4(Xb), ps[:, :].rearrange("p (a b) -> p a b", a=4),
                             GM[:, n:n + 1, :].broadcast_to([128, 4, 128]), M, t, tT[h])
                    B.done(b, tx_)
                    b2, ps2, fr2 = B.take()
                    t = mm(b2, [(ps2[:, c * 128:(c + 1) * 128], [(Xb[:, h, c * 128:(c + 1) * 128], sl4(TTn, c))])
                                for c in range(4)], fr2, tx_)
                    if n < 6:
                        b1, ps1, fr1 = B.take()
                        t_ = mm(b1, [(ps1[:, c * 128:(c + 1) * 128], [(sl4(TTn, c), Xb[:, h, c * 128:(c + 1) * 128])])
                                     for c in range(4)], fr1)
                        t1_ = tt(c4(T), idb if n == 0 else c4(T), ps1[:, :].rearrange("p (a b) -> p a b", a=4),
                                 ALU.subtract, t_, free3)
                        B.done(b1, t1_)
                    else:
                        t_ = t
                    t2_ = tt(c4(TT), idb if n == 0 else c4(TT), ps2[:, :].rearrange("p (a b) -> p a b", a=4),
                             ALU.subtract, t_, free3)
                    B.done(b2, t2_)
                    tT[h] = [t1_, t2_]
            W = DT
            tw_ = []
            for h in range(4):
                b, ps, fr = B.take()
                t = mm(b, [(ps[:, c * 128:(c + 1) * 128], [(kbe[:, c, h * 128:(h + 1) * 128],
                                                            TT[:, h, c * 128:(c + 1) * 128])])
                           for c in range(4)], fr, tT[h])
                t = act(W[:, h, :], ps[:, :], ACT.Copy, t, scale=-1.0)
                B.done(b, t)
                tw_.append(t)
            SS = [Xb[:, 0, :], Xb[:, 1, :]]
            VN = [Xb[:, 2, :], Xb[:, 3, :]]
            oraw = T
            ts_, tvn = None, None
            for c in range(4):
                Sc, Sn, vn = SS[c % 2], SS[(c + 1) % 2], VN[c % 2]
                hs4 = lambda z, h: z[:, h * 128:(h + 1) * 128]
                b, ps, fr = B.take()
                t = mm(b, [(hs4(ps, h), [(TT[:, h, c * 128:(c + 1) * 128], hs4(vb[:, c, :], h))]
                            + ([(W[:, h, c * 128:(c + 1) * 128], hs4(Sc, h))] if c else []))
                           for h in range(4)], fr, tw_, ts_, tT)
                tvn = act(vn, ps[:, :], ACT.Copy, t)
                B.done(b, tvn)
                if c < 3:
                    b, ps, fr = B.take()
                    t = mm(b, [(hs4(ps, h), [(hs4(ktl[:, c, :], h), hs4(vn, h))]) for h in range(4)], fr, tvn)
                    if c == 0:
                        ts_ = cp(Sn, ps, t)
                    else:
                        for h in range(4):
                            ts_ = stt(hs4(Sn, h), hs4(Sc, h), CD[:, c, h0 + h:h0 + h + 1], hs4(ps, h), M, A_, t, t2)
                    B.done(b, ts_)
                b, ps, fr = B.take()
                t = mm(b, [(hs4(ps, h), ([(hs4(Sc, h), q[:, h, c * 128:(c + 1) * 128])] if c else [])
                            + [(hs4(vn, h), qk[:, h, c * 128:(c + 1) * 128])])
                           for h in range(4)], fr, tvn)
                t = act(oraw[:, :, c * 128:(c + 1) * 128], ps[:, :].rearrange("p (a b) -> p a b", a=4), ACT.Copy, t)
                B.done(b, t)
            Z = AT

            def zev(j, s, ps, t):
                return act(Z[:, j, :], ps, ACT.Silu, t)
            linear(wg[:, 3072 + hg * 512:3072 + (hg + 1) * 512], 8, hs, zev)
            tz = (AE.sem, AE.n)
            O = arena(SO if hg == 0 else bufs[0], 4, 512) if hg == 0 else bf[0]
            for h in range(4):
                b, ps, t = sumsq([oraw[:, h, :]], 512, ones, tz)
                i, r, t = rstd(ps, b, 512, 1.0 / 128, e1, t)
                t = tt(oraw[:, h, :], oraw[:, h, :], r, M, t)
                rrf[i] = t
                t = stt(O[:, h, :], oraw[:, h, :], col(C_GNW), Z[:, h, :], M, M, t)
            if hg == 0:
                O0 = O
        O1 = O

        def add_x(j, s, ps, t):
            return tt(X[:, j, :], X[:, j, :], ps, A_, t)

        for c in range(2):
            si, sl, tw = wtile(a["gdn_w_out"][:, c * 512:(c + 1) * 512], 8, 512)
            for j in range(4):
                b, ps, fr = B.take()
                tm = mm(b, [(ps[:, :], [(sl[:, k, j * 128:(j + 1) * 128], (O0 if k < 4 else O1)[:, k % 4, :])
                                        for k in range(8)])], fr, tw, t)
                t9 = add_x(c * 4 + j, 0, ps[:, :], tm)
                B.done(b, t9)
            slot_free[si] = tm
        txx = t9
        if stop == "gdn":
            finish(txx)
            return emit(nc, ctx, PE, DV, AE, PO, SP)

        def ffn1(l):
            fence()
            b, ps, t = sumsq([X[:, k, :] for k in range(8)], S, ones, (DV.sem, DV.n))
            i, r, t = rstd(ps, b, S, 1.0 / D, e1, t)
            for k in range(8):
                tk = stt(HT[0][:, k, :], X[:, k, :], col(C_NFFN + 8 * l + k), r, M, M, t)
                th = split(HR[0][0][:, k, :], HR[0][1][:, k, :], HT[0][:, k, :], tk)
            rrf[i] = tk
            ffn(a["ffn_w_in"][l], a["ffn_w_out"][l], [S], add_x, th)

        ffn1(0)
        if stop == "ffn0":
            finish((DV.sem, DV.n))
            return emit(nc, ctx, PE, DV, AE, PO, SP)

        fence()
        tq = last()
        QD, KD, VD = arena(0, 12, 512), arena(6144, 12, 512), arena(12288, 4, 1536)
        DI = arena(18432, 1280)
        PB = [arena(19712, 1280), arena(20992, 1280)]
        BI2 = arena(22272, 1280)
        tdi = AE.dma(lambda e: e.dma_start(DI, a["kc"][:, K_DIL:K_DIL + N_DIL]), lane("di"), tq)
        th = rms(X, H, C_NMIX + 8, (DV.sem, DV.n))
        wd = a["dil_w_in"]

        def headnorm(dst, ps, n, g, scale, eps, t):
            b, p2, t = sumsq([ps], n, bones, t)
            i, r, t = rstd(p2, b, n, scale, eps, t)
            t = stt(dst, ps, g, r, M, M, t)
            rrf[i] = t
            return t

        linear(wd[:, 0:1536], 8, hs, lambda j, s, ps, t: headnorm(QD[:, j, :], ps, 512, col(C_DQ), 1.0, e64, t), th)
        linear(wd[:, 1536:3072], 8, hs,
               lambda j, s, ps, t: headnorm(KD[:, j, :], ps, 512, col(C_DK), 1.0 / 64, e1, t))
        for c in range(3):
            linear_tok(wd[:, 3072 + c * 512:3072 + (c + 1) * 512], hs,
                       lambda qt, s, ps, t: act(VD[:, qt, c * 512:(c + 1) * 512], ps, ACT.Copy, t))
        tv = [(AE.sem, AE.n), (DV.sem, DV.n), (PE.sem, PE.n)]
        HF = H[:, :, :].rearrange("p a b -> p (a b)")
        BI = [HF[:, 0:1280], BI2]
        LB = [HF[:, 1280:2560], HF[:, 2560:3840]]
        OTK = [arena(23552, 512), arena(24064, 512), SQ[0], SQ[1]]
        bt = {}

        def dil_bias(h, *after):
            t = None
            for g, (o0, o1) in enumerate(((0, 256), (256, 768), (768, 1280))):
                slope = float(2.0 ** (-8.0 * (g * 8 + h + 1) / 24))
                t = act(BI[h % 2][:, o0:o1], DI[:, o0:o1], ACT.Copy, tdi, tv, *after, scale=slope)
            bt[h] = t

        jobs, hooks = [], {}
        dil_bias(0)
        for h in range(8):
            if h < 7:
                hooks.setdefault(4 * h + 2, []).append(lambda h=h: dil_bias(h + 1, (DV.sem, DV.n)))
            pb_ = 64 * (h % 2)
            for qt in range(4):
                k0 = max(0, qt - 1)
                segs, vals = [], []
                for g, (lo, full) in enumerate(((k0, 256), (0, 512), (0, 512))):
                    tile = g * 4 + h // 2
                    w = (qt + 1 - lo) * 128
                    base = (0, 256, 768)[g] + full - w
                    segs.append((QD[pb_:pb_ + 64, tile, qt * 128:(qt + 1) * 128],
                                 KD[pb_:pb_ + 64, tile, lo * 128:(qt + 1) * 128],
                                 BI[h % 2][:, base:base + w]))
                    vals += [VD[:, kt, g * 512 + h * 64:g * 512 + (h + 1) * 64] for kt in range(lo, qt + 1)]
                jobs.append((segs, vals, OTK[qt][:, h * 64:(h + 1) * 64], lambda h=h: bt[h]))
        MR[0] = arena(24576, 512)[0:2, :]

        def mod_hooks(l, step, hooks=hooks):
            n = 0.0
            for c in range(12):
                for f in mod_piece(l, c):
                    hooks.setdefault(int(n), []).append(f)
                    n += step
        mod_hooks(0, 1.3)
        to = attention(jobs, LB, PB, tv, hooks)
        OF = arena(0, 4, 512)
        tf = None
        fr_ = (PE.sem, PE.n)
        for j in range(4):
            b, ps, fr = B.take()
            t = tp([(ps[:, q * 128:(q + 1) * 128], OTK[q][:, j * 128:(j + 1) * 128]) for q in range(4)], fr, to)
            tf = act(OF[:, j, :], ps[:, :], ACT.Copy, t, fr_)
            sqf[0] = sqf[1] = t
            B.done(b, tf)
        linear(a["dil_w_out"], 4, [(OF, S)], add_x, tf)
        if stop == "dil":
            finish((DV.sem, DV.n))
            return emit(nc, ctx, PE, DV, AE, PO, SP)
        ffn1(1)
        if stop == "ffn1":
            finish((DV.sem, DV.n))
            return emit(nc, ctx, PE, DV, AE, PO, SP)

        fence()
        tq = last()
        XC = view(U[:, UN - 2048:UN], (8, LC))
        HC = view(U[:, UN - 4096:UN - 2048], (8, LC))
        AMAX = UN - 4096 - 4096
        txc = AE.dma(lambda e: e.dma_start(XC, a["ctx"]), lane("xc"), tq)
        for k in range(8):
            tx1 = act(X[:, k, :], X[:, k, :], ACT.Copy, tq, scale=ALPHA)
        tx2 = act(XC, XC, ACT.Copy, txc, scale=ALPHA)
        tX, tXC = [tx1], [tx2]
        for l in range(2):
            MOD, tmod = MODS[l], (DV.sem, DV.n)
            mod = lambda g, s: (lambda k: MOD[:, 8 * g + k, s:s + 1])
            layernorm(X, H, S, ea2, mod(1, 0), mod(0, 0), tX, tmod)
            layernorm(XC, HC, LC, ea2, mod(1, 1), mod(0, 1), tXC, tmod)
            th = (AE.sem, AE.n)
            if stop == "H":
                finish(th, src=H)
                return emit(nc, ctx, PE, DV, AE, PO, SP)
            tq = fence()
            o = 0
            def take(*shape):
                nonlocal o
                v = arena(o, *shape)
                o += int(np.prod(shape))
                assert o <= AMAX, o
                return v
            QA, QAX, KA, KAX = take(3, S), take(3, LC), take(3, S), take(3, LC)
            VA, VAX = take(4, 384), take(2, 384)
            ZB, ZBX = take(4, 512), take(2, 512)
            QC, QCX, KCx, KCX = take(3, S), take(3, LC), take(1, S), take(1, LC)
            VC, VCX = take(4, 128), take(2, 128)
            EB = [take(14, 64), take(14, 64)]
            LB = [take(768), take(768)]
            PB = [take(768), take(768)]
            NM = take(N_NA)
            MR[0] = take(512)[0:2, :]
            WS = take(4, 128)
            GS = take(256)
            CO, SI, RM, FL = NM[:, 64:576], NM[:, 576:1088], NM[:, 1088:1216], NM[:, 1216:1344]
            tnm = AE.dma(lambda e: e.dma_start(NM, a["kc"][:, K_NA:K_NA + N_NA]), lane("nm"), tq)
            tws = AE.dma(lambda e, l=l: e.dma_start(WS, a["w_sT"][l]), lane("ws"))
            tgs = AE.dma(lambda e, l=l: e.dma_start(
                GS, a["g_sgu"][l:l + 1, :].broadcast_to([128, 256])), lane("gs"))
            w = a["w_in"][l]
            both = [(H, S), (HC, LC)]
            qs = both if l == 0 else both[:1]
            linear(w[:, 0:384], 8, qs,
                   lambda j, s, ps, t: act((QA, QAX)[s][:, j, :], ps, ACT.Copy, t, scale=0.125), th)
            if stop == "projW0":
                print("slot", slot_n[0]-1)
                finish(*last(), src=ring[(slot_n[0] - 1) % 4])
                return emit(nc, ctx, PE, DV, AE, PO, SP)
            linear(w[:, 384:768], 8, both, lambda j, s, ps, t: act((KA, KAX)[s][:, j, :], ps, ACT.Copy, t))
            linear_tok(w[:, 768:1152], both, lambda q, s, ps, t: act((VA, VAX)[s][:, q, :], ps, ACT.Copy, t))
            linear_tok(w[:, 1152:1664], qs, lambda q, s, ps, t: act((ZB, ZBX)[s][:, q, :], ps, ACT.Gelu_apprx_tanh, t))
            kp = lambda v: v.rearrange("(k p) n -> p k n", p=128)
            si, sl, tw = weights(*[
                (lambda r, j=j, g=g: r[:, :, j * 128 + g * 64:j * 128 + (g + 1) * 64],
                 kp(w[:, 1664 + g * 192 + j * 64:1664 + g * 192 + (j + 1) * 64]))
                for j in range(3) for g in range(2)], (lambda r: r[:, :, 384:512], kp(w[:, 2048:2176])))
            for j in range(4):
                for s, (h_, n) in enumerate(both):
                    if j < 3 and s == 1 and l == 1:
                        continue
                    b, ps, fr = B.take()
                    t = mm(b, [(ps[:, 0:n], [(sl[:, k, j * 128:(j + 1) * 128], h_[:, k, :]) for k in range(8)])],
                           fr, tw)
                    last_pe = t
                    dst = ((QC, QCX)[s][:, j, :] if j < 3 else (KCx, KCX)[s][:, 0, :])
                    g, sc, ep = (C_GQ + l, 1.0, e64) if j < 3 else (C_GK + l, 1.0 / 64, e1)
                    t = headnorm(dst, ps[:, 0:n], n, col(g), sc, ep, t)
                    B.done(b, t)
                    if s == 0:
                        b, ps, fr = B.take()
                        t = mm(b, [(ps[:, :], [(RM, dst)])], fr, t, tnm)
                        i = cnt["rr"] % 2
                        cnt["rr"] += 1
                        t = tt(RR[i][:, :], ps[:, :], SI, M, t, rrf[i])
                        B.done(b, t)
                        t2 = tt(dst, dst, CO, M, t)
                        t = tt(dst, dst, RR[i][:, :], A_, t2)
                        rrf[i] = t
            slot_free[si] = last_pe
            linear_tok(w[:, 2176:2304], both, lambda q, s, ps, t: act((VC, VCX)[s][:, q, :], ps, ACT.Copy, t))
            tv = last()
            if stop == "projH":
                finish(tv, src=H)
                return emit(nc, ctx, PE, DV, AE, PO, SP)
            if stop == "projW":
                finish(tv, src=ring[(slot_n[0] - 6) % 4])
                return emit(nc, ctx, PE, DV, AE, PO, SP)
            if stop == "proj":
                finish(tv, src=arena(0, 8, 512))
                return emit(nc, ctx, PE, DV, AE, PO, SP)
            if stop == "proj2":
                finish(tv, src=arena(4608, 8, 512))
                return emit(nc, ctx, PE, DV, AE, PO, SP)
            OT = H[:, :, :].rearrange("p a b -> p (a b)").rearrange("p (a b) -> p a b", a=4)
            OTX = HC.rearrange("p a b -> p (a b)").rearrange("p (a b) -> p a b", a=2)
            ST, MV = LB[0][:, 0:16], LB[0][:, 16:24]
            tl = tv
            for s, (zb, ot, nt) in enumerate(((ZB, OT, 4), (ZBX, OTX, 2))):
                if s and l:
                    continue
                for q in range(nt):
                    vv = zb[:, q, 256:512]
                    t = DV(lambda e, vv=vv: e.bn_stats(ST[:, 0:6], vv), tl)
                    t = DV(lambda e: e.bn_aggr(MV[:, 0:2], ST[:, 0:6]), t)
                    t1 = act(MV[:, 2:3], MV[:, 1:2], ACT.Ln, t, bias=e1)
                    t1 = act(MV[:, 2:3], MV[:, 2:3], ACT.Exp, t1, scale=-0.5)
                    t = ts(vv, vv, MV[:, 0:1], MV[:, 2:3], ALU.subtract, M, t1)
                    t = tt(vv, vv, GS, M, t, tgs)
                    b, ps, fr = B.take()
                    t = mm(b, [(ps[:, g * 64:(g + 1) * 64], [(WS[:, g, :], vv[:, g * 64:(g + 1) * 64])])
                               for g in range(4)], fr, t, tws)
                    for g in range(4):
                        t2 = stt(ot[:, q, 384 + g * 64:384 + (g + 1) * 64], ps[:, g * 64:(g + 1) * 64],
                                 col(C_BS + 4 * l + g), zb[:, q, g * 64:(g + 1) * 64], A_, M, t, tv)
                    B.done(b, t2)
                    tl = t2
            bl, bt = {}, {}

            def bias_load(h, fr):
                for r in range(2):
                    base = ((l * 6 + h) * 15 + (1 - r)) * 127
                    src = bass.AP(a["rpb"].tensor, base, [[1, 64], [127, 14], [1, 64]])
                    bl[h] = SP.dma(lambda e, src=src, r=r, h=h: e.dma_start(EB[h % 2][64 * r:64 * r + 64, :, :], src),
                                   lane(f"rpb{h % 2}"), fr)

            def bias_turn(h):
                pair = []
                for c in range(2):
                    b, ps, fr = B.take()
                    t = mm(b, [(ps[:, 0:448], [(FL, EB[h % 2][:, 7 * c:7 * c + 7, :])])], fr, bl[h], tnm)
                    pair.append((b, ps))
                for c, (b, ps) in enumerate(pair):
                    bt[h] = tt(EB[h % 2][:, 7 * c:7 * c + 7, :], ps[:, 0:448].rearrange("p (a b) -> p a b", a=7),
                               NM[:, 0:64].unsqueeze(1).broadcast_to([128, 7, 64]), A_, t)
                    B.done(b, bt[h])
            for h in range(2):
                bias_load(h, tv)
                bias_turn(h)
            jobs, hooks = [], {}
            for h in range(6):
                pb_, tile = 64 * (h % 2), h // 2
                E = EB[h % 2].rearrange("p a b -> p (a b)")
                kx = KAX[pb_:pb_ + 64, tile, :]
                hv = slice(h * 64, (h + 1) * 64)
                if 1 <= h < 5:
                    hooks[len(jobs) + 1] = [lambda h=h: bias_load(h + 1, (DV.sem, DV.n))]
                    hooks[len(jobs) + 3] = [lambda h=h: bias_turn(h + 1)]
                for q in range(4):
                    qv = QA[pb_:pb_ + 64, tile, q * 128:(q + 1) * 128]
                    jobs.append(([(qv, KA[pb_:pb_ + 64, tile, :], E[:, (6 - 2 * q) * 64:(14 - 2 * q) * 64]),
                                  (qv, kx, None)],
                                 [VA[:, t_, hv] for t_ in range(4)] + [VAX[:, t_, hv] for t_ in range(2)],
                                 OT[:, q, hv], lambda h=h: bt[h]))
                if l == 0:
                    for q in range(2):
                        jobs.append(([(QAX[pb_:pb_ + 64, tile, q * 128:(q + 1) * 128], kx, None)],
                                     [VAX[:, t_, hv] for t_ in range(2)], OTX[:, q, hv], None))
            for h in range(6):
                g, tile = h // 3, h % 3
                pb_ = 64 * g
                hv = slice(g * 64, (g + 1) * 64)
                ov = slice(640 + h * 64, 640 + (h + 1) * 64)
                kk, kx = KCx[pb_:pb_ + 64, 0, :], KCX[pb_:pb_ + 64, 0, :]
                for q in range(4):
                    qv = QC[pb_:pb_ + 64, tile, q * 128:(q + 1) * 128]
                    jobs.append(([(qv, kk, None), (qv, kx, None)],
                                 [VC[:, t_, hv] for t_ in range(4)] + [VCX[:, t_, hv] for t_ in range(2)],
                                 OT[:, q, ov], None))
                if l == 0:
                    for q in range(2):
                        jobs.append(([(QCX[pb_:pb_ + 64, tile, q * 128:(q + 1) * 128], kx, None)],
                                     [VCX[:, t_, hv] for t_ in range(2)], OTX[:, q, ov], None))
            if l == 0:
                mod_hooks(1, 2.5, hooks)
            to = attention(jobs, LB, PB, tv, hooks)
            if stop == "OT":
                finish(to, src=H)
                return emit(nc, ctx, PE, DV, AE, PO, SP)
            MG, MGX = arena(0, 8, S), arena(4096, 8, LC)
            tq = fence()
            SG = LB[0][:, 0:64]
            SCR = LB[1]
            groups = ((0, 384), (384, 640), (640, 1024))
            jj = 0
            tr = to
            for s, (ot, nt) in enumerate(((OT, 4), (OTX, 2))):
                if s and l:
                    continue
                for q in range(nt):
                    for g, (lo, hi) in enumerate(groups):
                        c_ = SG[:, jj:jj + 1]
                        jj += 1
                        t1 = act(SCR[:, 0:hi - lo], ot[:, q, lo:hi], ACT.Square, tr, (AE.sem, AE.n), accum_out=c_)
                        t1 = act(c_, c_, ACT.Ln, t1, scale=1.0 / (hi - lo), bias=e1)
                        t1 = act(c_, c_, ACT.Exp, t1, scale=-0.5)
                        tr_ = ts(ot[:, q, lo:hi], ot[:, q, lo:hi], c_, None, M, None, t1)
            for s, (ot, mg, nt) in enumerate(((OT, MG, 4), (OTX, MGX, 2))):
                if s and l:
                    continue
                for k in range(8):
                    b, ps, fr = B.take()
                    t = tp([(ps[:, q * 128:(q + 1) * 128], ot[:, q, k * 128:(k + 1) * 128]) for q in range(nt)],
                           fr, tr_)
                    t = act(mg[:, k, :], ps[:, 0:nt * 128], ACT.Copy, t, tq, scale=col(C_GOUT + 8 * l + k))
                    B.done(b, t)
            def gated(g):
                def evac(j, s, ps, t):
                    x = (X, XC)[s][:, j, :]
                    return stt(x, ps, MOD[:, 8 * g + j, s:s + 1], x, M, A_, t)
                return evac
            ms = [(MG, S), (MGX, LC)][:2 - l]
            linear(a["w_o"][l], 8, ms, gated(2), t)

            if stop == f"mix{l}":
                break

            def post(n_, fin=False):
                c0 = C_LN + 32 * l + 16 * n_
                tq = (DV.sem, DV.n)
                r = []
                for s, (x, n) in enumerate(((X, S), (XC, LC))):
                    if s and l:
                        continue
                    t = layernorm(x, x, n, e1, lambda k: col(c0 + k), lambda k: col(c0 + 8 + k), tq)
                    r.append(t)
                    if not fin:
                        for k in range(8):
                            t = ts(x[:, k, :], x[:, k, :], ALPHA, 1.0, M, M, (AE.sem, AE.n), e=PO)
                        r[-1] = t
                return r
            tt_ = post(0)
            if stop == f"post{l}":
                break
            fence()
            for s, x in enumerate((X, XC)[:2 - l]):
                t = layernorm(x, HT[s], (S, LC)[s], ea2, mod(4, s), mod(3, s), tt_)
                for k in range(8):
                    th = split(HR[s][0][:, k, :], HR[s][1][:, k, :], HT[s][:, k, :], t)
            ffn(a["w_ffn_in"][l], a["w_ffn_out"][l], [S, LC][:2 - l], gated(5), th)
            tt_ = post(1, fin=(l == 1))
            tX, tXC = [tt_], [tt_]
            if stop == f"b2_{l}":
                break
        finish((AE.sem, AE.n), (PO.sem, PO.n), (DV.sem, DV.n))
        return emit(nc, ctx, PE, DV, AE, PO, SP)


def emit(nc, ctx, PE, DV, AE, PO, SP):
    block = ctx.enter_context(nc.Block())

    @block.sync
    def _(eng):
        SP.emit(eng)

    @block.tensor
    def _(eng):
        PE.emit(eng)

    @block.vector
    def _(eng):
        DV.emit(eng)

    @block.scalar
    def _(eng):
        AE.emit(eng)

    @block.gpsimd
    def _(eng):
        PO.emit(eng)


def layout(i):
    f = np.float32
    A = {k: np.ascontiguousarray(v) for k, v in i.items()}

    def feat(v, n=8):
        return v.reshape(n, 128).T

    c = np.zeros((128, NCOL), f)
    for l in range(2):
        c[:, C_NMIX + 8 * l:C_NMIX + 8 * l + 8] = feat(A["norm_mix"][l])
        c[:, C_NFFN + 8 * l:C_NFFN + 8 * l + 8] = feat(A["norm_ffn"][l])
        c[:, C_BMOD + 48 * l:C_BMOD + 48 * l + 48] = feat(A["b_mod_2"][l], 48)
        for h in range(2):
            c[64 * h:64 * h + 64, C_GQ + l] = A["g_q_2"][l]
            c[64 * h:64 * h + 64, C_GK + l] = A["g_k_2"][l]
        c[:, C_GOUT + 8 * l:C_GOUT + 8 * l + 8] = feat(A["g_out_2"][l])
        for n, k in enumerate(("ln1_g_2", "ln1_b_2", "ln2_g_2", "ln2_b_2")):
            o = C_LN + 32 * l + 8 * n
            c[:, o:o + 8] = feat(A[k][l])
        c[:, C_BS + 4 * l:C_BS + 4 * l + 4] = A["b_s_2"][l].T
    c[:, C_GNW] = A["gdn_norm_w"][0]
    c[:, C_CONV:C_CONV + 96] = A["gdn_conv_w"][0].reshape(4, 24, 128).transpose(2, 1, 0).reshape(128, 96)
    for h in range(2):
        c[64 * h:64 * h + 64, C_DQ] = A["dil_q_norm"][0]
        c[64 * h:64 * h + 64, C_DK] = A["dil_k_norm"][0]
    c[0:8, C_ALOG] = A["gdn_a_log"][0]
    c[0:8, C_DT] = A["gdn_dt_bias"][0]
    cc = np.stack([feat(A["c_2"][0]), feat(A["c_ctx_2"])], axis=2)
    c[:, C_C:C_C + 16] = cc.reshape(128, 16)
    rpb = np.zeros((2, 6, 15, 127), f)
    rpb[:, :, :, 48:79] = A["rpb_2"]
    return {
        "x": np.ascontiguousarray(A["x"][0].T.reshape(8, 128, S).transpose(1, 0, 2)),
        "ctx": np.ascontiguousarray(A["ctx_2"][0].T.reshape(8, 128, LC).transpose(1, 0, 2)),
        "cols": c, "kc": constants(), "rpb": rpb,
        "gdn_w_in": A["gdn_w_in"][0], "gdn_w_out": A["gdn_w_out"][0],
        "dil_w_in": A["dil_w_in"][0], "dil_w_out": A["dil_w_out"][0],
        "ffn_w_in": A["ffn_w_in"], "ffn_w_out": A["ffn_w_out"],
        "w_mod": A["w_mod_2"], "w_in": A["w_in_2"], "w_o": A["w_o_2"],
        "w_ffn_in": A["w_ffn_in_2"], "w_ffn_out": A["w_ffn_out_2"],
        "w_sT": np.ascontiguousarray(A["w_s_2"].transpose(0, 3, 1, 2)),
        "g_sgu": A["g_sgu_2"],
    }


def kernel(**inputs):
    import concourse.bacc as bacc
    from concourse.bass_utils import run_bass_kernel_spmd

    arrays = layout({k: np.asarray(v) for k, v in inputs.items()})
    nc = bacc.Bacc("TRN2", target_bir_lowering=False, num_devices=1)
    aps = {k: nc.dram_tensor("in_" + k, v.shape, F32, kind="ExternalInput").ap() for k, v in arrays.items()}
    out = nc.dram_tensor("out_0", (128, 8, S), F32, kind="ExternalOutput").ap()
    build(nc, aps, out)
    r = run_bass_kernel_spmd(nc, [{"in_" + k: v for k, v in arrays.items()}], core_ids=[0])
    y = np.asarray(r.results[0]["out_0"])
    return y.transpose(2, 1, 0).reshape(1, S, D)
```

```python
from contextlib import ExitStack

import numpy as np

import concourse.bass as bass
from concourse import mybir

F32 = mybir.dt.float32
F32R = mybir.dt.float32r
ALU = mybir.AluOpType
ACT = mybir.ActivationFunctionType
AX = mybir.AxisListType.X

S, LC, D = 512, 256, 1024
FF = 2816
ALPHA = 4.0 ** 0.25
EPS = 1e-6
BIG = 1e30
NS = 3
UN = 33792

C_NMIX, C_NFFN, C_GNW, C_CONV, C_DQ, C_DK, C_ALOG, C_DT = 0, 16, 32, 33, 129, 130, 131, 132
C_C, C_BMOD, C_GQ, C_GK, C_GOUT, C_LN, C_BS = 133, 149, 245, 247, 249, 265, 329
NCOL = 337
K_ID, K_ONE, K_BONE, K_EPS, K_RES = 0, 128, 256, 384, 392
K_GDN = K_RES
N_GDN = 7 * 128 + 128 + 512
K_DIL = K_GDN + N_GDN
N_DIL = 1280
K_NA = K_DIL + N_DIL
N_NA = 64 + 1024 + 128 + 128
NK = K_NA + N_NA


def constants():
    f = np.float32
    k = np.zeros((128, NK), f)
    i = np.arange(128)[:, None]
    j = np.arange(128)[None, :]
    k[:, K_ID:K_ID + 128] = i == j
    k[:, K_ONE:K_ONE + 128] = 1
    k[:, K_BONE:K_BONE + 128] = i // 64 == j // 64
    for n, e in enumerate((EPS, 64 * EPS, ALPHA * ALPHA * EPS, 1.0, 128 * EPS)):
        k[:, K_EPS + n] = e
    g = K_GDN
    for n in range(7):
        b = 1 << n
        k[:, g:g + 128] = (i // (2 * b) == j // (2 * b)) & (i % (2 * b) >= b) & (j % (2 * b) < b)
        g += 128
    k[:, g:g + 128] = i <= j
    g += 128
    k[:, g:g + 512] = np.arange(512) % 128 != 0
    g = K_DIL
    d0 = 128 + i - np.arange(256)[None, :]
    k[:, g:g + 256] = np.where((d0 >= 0) & (d0 <= 128), -d0, -BIG)
    d = 384 + i - np.arange(512)[None, :]
    k[:, g + 256:g + 768] = np.where((d >= 0) & (d % 4 == 0), -d, -BIG)
    k[:, g + 768:g + 1280] = np.where((d >= 0) & (d % 16 == 0), -d, -BIG)
    g = K_NA
    c, cc = i % 64, np.arange(64)[None, :]
    st = np.clip(c - 8, 0, 48)
    k[:, g:g + 64] = np.where((cc >= st) & (cc < st + 16), 0, -BIG)
    g += 64
    t = np.arange(512)
    inv = (f(1.0) / (f(10000.0) ** (np.arange(16, dtype=f) / f(16)))).astype(f)
    p = np.arange(128) % 64
    pos = np.where((p // 32 == 0)[:, None], (t // 64)[None, :], (t % 64)[None, :]).astype(f)
    ang = (pos * inv[p % 16][:, None]).astype(f)
    k[:, g:g + 512] = np.cos(ang)
    k[:, g + 512:g + 1024] = np.sin(ang)
    g += 1024
    first = (np.arange(128) % 32) < 16
    k[:, g:g + 128] = np.where(first[None, :], -1.0 * (i == j + 16), 1.0 * (i == j - 16))
    k[:, g + 128:g + 256] = (i // 64 == j // 64) & (i % 64 == 63 - j % 64)
    return k


class Engine:

    def __init__(self, sem):
        self.sem, self.n, self.queue, self.seen = sem, 0, [], {}

    def wait(self, *after):
        for t in after:
            if t is None:
                continue
            if isinstance(t, list):
                self.wait(*t)
            elif self.seen.get(id(t[0]), 0) < t[1]:
                self.seen[id(t[0])] = t[1]
                self.queue.append((None, t[0], t[1]))

    def __call__(self, fn, *after):
        self.wait(*after)
        self.n += 1
        self.queue.append((fn, self.sem, 1))
        return (self.sem, self.n)

    def quiet(self, fn, *after):
        self.wait(*after)
        self.queue.append((fn, None, 0))

    def dma(self, fn, lane, *after):
        self.wait(*after)
        lane[1] += 16
        self.queue.append((fn, lane[0], 16))
        return (lane[0], lane[1])

    def emit(self, eng):
        for fn, sem, n in self.queue:
            if fn is None:
                eng.wait_ge(sem, n)
            elif sem is None:
                fn(eng)
            else:
                fn(eng).then_inc(sem, n)


class Pair:

    def __init__(self, x, y):
        self.x, self.y = x, y

    def __getitem__(self, i):
        return (self.x, self.y)[i[1] // 4][i[0], i[1] % 4, i[2]]


class Banks:

    def __init__(self, tiles):
        self.tiles, self.free, self.i = tiles, [None] * len(tiles), 0

    def take(self):
        b = self.i % len(self.tiles)
        self.i += 1
        return b, self.tiles[b], self.free[b]

    def done(self, b, token):
        self.free[b] = token


def build(nc, a, out):
    ctx = ExitStack()
    with ctx:
        def sb(name, shape):
            return ctx.enter_context(nc.sbuf_tensor(name, shape, F32))

        def sem(name):
            return ctx.enter_context(nc.semaphore(name))

        def view(v, shape):
            if len(shape) == 2:
                v = v.rearrange("p (a b) -> p a b", a=shape[0])
            elif len(shape) == 3:
                v = v.rearrange("p (a b c) -> p a b c", a=shape[0], b=shape[1])
            return v

        X = sb("X", [128, 8, S])
        KC = sb("KC", [128, K_RES])
        COL = sb("COL", [128, NCOL])
        MODS = [sb(f"MOD{l}", [128, 48, 2]) for l in range(2)]
        SCT = sb("SCT", [128, 8, 2])
        AC = sb("AC", [128, 32])
        SQ = [sb(f"SQ{i}", [128, 512]) for i in range(2)]
        RR = [sb(f"RR{i}", [128, 512]) for i in range(2)]
        at = -(-nc.sbuf_base // 64) * 64
        ring, ring_lo = ([view(nc.alloc_sbuf_tensor_at(f"ring{n}{i}", [128, 4096], ty, offset=at + 16384 * i)[:, :],
                               (8, 512)) for i in range(NS)] for n, ty in (("", F32), ("lo", F32R)))
        at += 16384 * NS
        U = nc.alloc_sbuf_tensor_at("U", [128, UN], F32, offset=at)
        H = U[:, 0:4096].rearrange("p (a b) -> p a b", a=8)
        psum = [ctx.enter_context(nc.psum_tensor(f"ps{i}", [128, 512], F32))[:, :] for i in range(8)]

        PE, DV, AC_, PO, SP = (Engine(sem(n)) for n in ("s_pe", "s_dve", "s_act", "s_pool", "s_sp"))
        AE = AC_
        wl = [[sem(f"w{i}"), 0] for i in range(NS)]
        misc = {}

        def lane(name):
            if name not in misc:
                misc[name] = [sem("d_" + name), 0]
            return misc[name]

        B = Banks(psum)
        ident = KC[:, K_ID:K_ID + 128]
        ones = KC[:, K_ONE:K_ONE + 128]
        bones = KC[:, K_BONE:K_BONE + 128]
        e1, e64, ea2, one1, e128 = (KC[:, K_EPS + n:K_EPS + n + 1] for n in range(5))

        def col(n):
            return COL[:, n:n + 1]

        def arena(off, *shape):
            off += 4096
            assert off + int(np.prod(shape)) <= UN
            return view(U[:, off:off + int(np.prod(shape))], shape)

        def last():
            return [(e.sem, e.n) for e in (PE, DV, AE, PO) if e.n]

        def fence():
            t = last()
            for e in (DV, AE, PO):
                e.wait(t)
            return t

        slot_free = [None] * NS
        slot_n = [0]

        def weights(*parts):
            i = slot_n[0] % NS
            slot_n[0] += 1
            SP.wait(slot_free[i])
            for view, src in parts:
                t = SP.dma(lambda e, v=view(ring[i]), s=src: e.dma_start(v, s), wl[i])
            return i, ring[i], t

        def wtile(src, k, n):
            return weights((lambda r: r[:, 0:k, 0:n], src.rearrange("(k p) n -> p k n", p=128)))

        def mm(bank, groups, *after):
            PE.wait(*after)
            n = len(groups)
            t = None
            for g, (o, prs) in enumerate(groups):
                for i, (l, r, *tok) in enumerate(prs):
                    PE.wait(*tok)
                    f = (lambda e, o=o, l=l, r=r, st=(i == 0), sp=(i == len(prs) - 1):
                         e.matmul(o, l, r, start=st, stop=sp))
                    if g == n - 1 and i == len(prs) - 1:
                        t = PE(f)
                    else:
                        PE.quiet(f)
            return t

        def tp(outs, *after):
            PE.wait(*after)
            t = None
            for o, i in outs:
                k = i.shape[0]
                f = lambda e, o=o, i=i, k=k: e.transpose(o, i, ident[0:k, 0:k])
                t = PE(f) if i is outs[-1][1] else PE.quiet(f)
            return t

        table = [None]

        def act(o, i, fn, *after, **kw):
            if fn in (ACT.Exp, ACT.Ln) and table[0] != "log":
                AE.quiet(lambda e: e.preload_act_table_set("natural_log_exp_and_others"))
                table[0] = "log"
            elif fn in (ACT.Silu, ACT.Gelu_apprx_tanh, ACT.Sigmoid):
                table[0] = "other"
            return AE(lambda e: e.activation(o, i, fn, **kw), *after)

        def tt(o, x, y, op, *after, e=None):
            return (e or DV)(lambda q: q.tensor_tensor(o, x, y, op), *after)

        def ts(o, x, s1, s2, o0, o1, *after, e=None):
            if s2 is None:
                return (e or DV)(lambda q: q.tensor_scalar(o, x, s1, None, o0), *after)
            return (e or DV)(lambda q: q.tensor_scalar(o, x, s1, s2, o0, o1), *after)

        def stt(o, x, s, y, o0, o1, *after):
            return DV(lambda q: q.scalar_tensor_tensor(o, x, s, y, o0, o1), *after)

        def cp(o, x, *after):
            return DV(lambda q: q.tensor_copy(o, x), *after)

        M, A_ = ALU.mult, ALU.add

        sqf, rrf = [None, None], [None, None]
        cnt = {"sq": 0, "rr": 0}

        def sq_of(src, n, *after):
            i = cnt["sq"] % 2
            cnt["sq"] += 1
            t = act(SQ[i][:, 0:n], src, ACT.Square, sqf[i], *after)
            return i, SQ[i][:, 0:n], t

        def rstd(ps, bank, n, scale, eps, t):
            i = cnt["rr"] % 2
            cnt["rr"] += 1
            r = RR[i][:, 0:n]
            t = act(r, ps, ACT.Ln, t, rrf[i], scale=scale, bias=eps)
            B.done(bank, t)
            t = act(r, r, ACT.Exp, t, scale=-0.5)
            return i, r, t

        def sumsq(srcs, n, mat, *after):
            b, ps, fr = B.take()
            PE.wait(fr)
            for k, s in enumerate(srcs):
                i, q, t = sq_of(s, n, *after)
                f = (lambda e, q=q, k=k: e.matmul(ps[:, 0:n], mat, q, start=(k == 0),
                                                  stop=(k == len(srcs) - 1)))
                t = PE(f, t)
                sqf[i] = t
            return b, ps[:, 0:n], t

        def rms(x, h, w, *after):
            b, ps, t = sumsq([x[:, k, :] for k in range(8)], S, ones, *after)
            i, r, t = rstd(ps, b, S, 1.0 / D, e1, t)
            hold = last()
            for k in range(8):
                t = stt(h[:, k, :], x[:, k, :], col(w + k), r, M, M, t, hold)
            rrf[i] = t
            return t

        def layernorm(streams, eps, mid=None, each=None):
            hold = last()
            bank, toks, read = [], [], []
            for x, h, n, g, b_, after in streams:
                bk, ps, fr = B.take()
                t = mm(bk, [(ps[:, 0:n], [(ones, x[:, k, :]) for k in range(8)])], fr, after)
                bank.append((bk, ps, t))
            for (x, h, n, g, b_, _), (bk, ps, t) in zip(streams, bank):
                toks.append([stt(h[:, k, :], ps[:, 0:n], -1.0 / D, x[:, k, :], M, A_, t, hold) for k in range(8)])
                B.done(bk, toks[-1][-1])
                read.append(toks[-1][-1])
            bank = []
            for s, (x, h, n, g, b_, _) in enumerate(streams):
                b, ps, fr = B.take()
                PE.wait(fr)
                for k in range(8):
                    i, q, tq = sq_of(h[:, k, :], n, toks[s][k])
                    t = PE(lambda e, q=q, k=k, o=ps[:, 0:n]: e.matmul(o, ones, q, start=(k == 0), stop=(k == 7)), tq)
                    sqf[i] = t
                bank.append((b, ps, t))
            if mid:
                mid()
            out_, late = [], []
            for s, ((x, h, n, g, b_, _), (b, ps, t)) in enumerate(zip(streams, bank)):
                i, r, t = rstd(ps[:, 0:n], b, n, 1.0 / D, eps, t)
                out_.append([])
                for k in range(8):
                    tk = tt(h[:, k, :], h[:, k, :], r, M, t)
                    rrf[i] = tk
                    to = act(h[:, k, :], h[:, k, :], ACT.Identity, tk, scale=g(k), bias=b_(k))
                    late.append((s, k, to))
                    if not each:
                        out_[-1].append(to)
                while each and late:
                    out_[s].append(each(*late.pop(0)))
            return out_, read

        named = {}

        def ru(off, n):
            if (off, n) not in named:
                named[off, n] = nc.alloc_sbuf_tensor_at(f"R{off}_{n}", [128, n], F32R, offset=at + 4 * off)[:, :]
            return named[off, n]

        def split(hi, lo, src, *after, e=None):
            t = (e or PO)(lambda q: q.tensor_copy(hi, src), *after)
            return tt(lo, src, hi, ALU.subtract, t)

        def split_act(hi, lo, src, *after):
            t = act(hi, src, ACT.Copy, *after)
            return tt(lo, src, hi, ALU.subtract, t)

        def three(ws, xs, ks, tk=None):
            out = []
            for k in ks:
                t = tk[k] if tk else None
                out += [(ws(0, k), xs(0, k), t), (ws(0, k), xs(1, k), t), (ws(1, k), xs(0, k), t)]
            return out

        def parts(off, hi_off, kt, n, tiles, *after):
            hi, lo = view(ru(hi_off, kt * n), (kt, n)), view(ru(off, kt * n), (kt, n))
            src = view(U[:, off:off + kt * n], (kt, n))
            tk = [(split_act if k % 2 else split)(hi[:, k, :], lo[:, k, :], src[:, k, :], tiles and tiles[k], *after)
                  for k in range(kt)]
            return hi, lo, n, tk

        WH, whf = [None] * 3, [None] * 3

        def wh_at(off, *after):
            for i in range(3):
                WH[i] = ru(off + 1024 * i, 1024)
                whf[i] = list(after)
            cnt["wh"] = 0

        def piece(si, tw, sel, shape):
            i = cnt["wh"] % 3
            cnt["wh"] += 1
            n = int(np.prod(shape))
            hi, lo = view(WH[i][:, 0:n], shape), sel(ring_lo[si])
            t = act(hi, sel(ring[si]), ACT.Copy, tw, whf[i])
            return i, (hi, lo), tt(lo, sel(ring[si]), hi, ALU.subtract, t)

        class Products:

            def __init__(self, plan, kt, evac):
                self.plan, self.kt, self.evac = plan, kt, evac
                self.todo = [(g, j) for g, (_, st) in enumerate(plan) for j in range(len(st))]
                self.slot, self.ready = {}, {}

            def prep(self, n):
                if n < len(self.todo) and n not in self.ready:
                    g, j = self.todo[n]
                    if j == 0:
                        self.slot[g] = self.plan[g][0]()
                    si, _, tw = self.slot[g]
                    self.ready[n] = piece(si, tw, lambda r: r[:, 0:self.kt, j * 128:(j + 1) * 128], (self.kt, 128))

            def run(self, after, then=None):
                PE.wait(*after)
                self.prep(0)
                self.prep(1)
                late = []
                for n, (g, j) in enumerate(self.todo):
                    self.prep(n + 2)
                    if then and n + 2 >= len(self.todo):
                        then.prep(n + 2 - len(self.todo))
                    i, w, tp_ = self.ready[n]
                    for s, x in enumerate(self.plan[g][1][j]):
                        if x is None:
                            continue
                        b, ps, fr = B.take()
                        o = ps[:, 0:x[2]]
                        t = mm(b, [(o, three(lambda p, k: w[p][:, k, :], lambda p, k: x[p][:, k, :],
                                             range(self.kt), x[3]))], fr, tp_)
                        if late:
                            late.pop()()
                        late.append(lambda b=b, n=n, s=s, o=o, t=t: B.done(b, self.evac(n, s, o, t)))
                    whf[i] = t
                    if j == len(self.plan[g][1]) - 1:
                        slot_free[self.slot[g][0]] = t
                late.pop()()

        def linear3(w, kt, streams, evac):
            return Products([(lambda c=c: wtile(w[:, c:min(c + 512, w.shape[1])], kt, min(512, w.shape[1] - c)),
                              [streams] * (min(512, w.shape[1] - c) // 128)) for c in range(0, w.shape[1], 512)],
                            kt, evac)

        class linear_tok3:

            def __init__(self, w, streams, evac):
                self.w, self.streams, self.evac, self.ready = w, streams, evac, {}

            def prep(self, c):
                if c < 4 and c not in self.ready:
                    n = self.w.shape[1]
                    if c == 0:
                        self.slot = wtile(self.w, 8, n)
                    self.ready[c] = piece(self.slot[0], self.slot[2], lambda r: r[:, 2 * c:2 * c + 2, 0:n], (2, n))

            def run(self, after, then=None):
                n = self.w.shape[1]
                PE.wait(*after)
                self.prep(0)
                self.prep(1)
                tiles = [(s, q, x) + B.take() for s, x in enumerate(self.streams) for q in range(x[2] // 128)]
                for c in range(4):
                    self.prep(c + 2)
                    if then and c >= 2:
                        then.prep(c - 2)
                    i, w_, tp_ = self.ready[c]
                    for m, (s, q, x, b, ps, fr) in enumerate(tiles):
                        PE.wait(fr, tp_)
                        for k in range(2):
                            PE.wait(x[3][2 * c + k])
                            for u, (p, r) in enumerate(((0, 0), (1, 0), (0, 1))):
                                f = (lambda e, o=ps[:, 0:n], l=x[p][:, 2 * c + k, q * 128:(q + 1) * 128],
                                     r=w_[r][:, k, :], st=(c + k + u == 0), sp=(c == 3 and k == 1 and u == 2):
                                     e.matmul(o, l, r, start=st, stop=sp))
                                if k == 1 and u == 2 and (c == 3 or m == len(tiles) - 1):
                                    t = PE(f)
                                else:
                                    PE.quiet(f)
                        if c == 3:
                            B.done(b, self.evac(q, s, ps[:, 0:n], t))
                    whf[i] = t
                slot_free[self.slot[0]] = t

        def chain(calls, *after):
            for n, c in enumerate(calls):
                c.run(after if n == 0 else (), calls[n + 1] if n + 1 < len(calls) else None)

        HR = [[view(ru(o, 4096), (8, S)) for o in (0, 4096)],
              [view(ru(o, 2048), (8, LC)) for o in (8192, 10240)]]
        WR = [[ru(12288 + 4096 * i + 2048 * p, 2048) for p in range(2)] for i in range(3)]
        GR_ = [[[view(ru(24576 + 2048 * b + 1024 * p, 1024), (2, S)) for p in range(2)] for b in range(2)],
               [[view(ru(28672 + 1024 * b + 512 * p, 512), (2, LC)) for p in range(2)] for b in range(2)]]
        HT = [view(U[:, 24576:28672], (8, S)), view(U[:, 28672:30720], (8, LC))]
        TG = [U[:, 30720 + 512 * i:31232 + 512 * i] for i in range(2)]

        def to_parts(s, k, t):
            return (split_act if k % 2 else split)(HR[s][0][:, k, :], HR[s][1][:, k, :], HT[s][:, k, :], t)

        def ffn(wi, wo, ns, evac, prelude):
            tw = [None] * 3
            wfree = [None] * 3
            gfree = [[None] * 2, [None] * 2]
            gtok = [[None] * 2, [None] * 2]
            tgf = [None, None]
            qn = [0]
            outs = {}

            def w_in(c):
                si, sl, t = weights(
                    (lambda r: r[:, :, 0:256], wi[:, c * 256:(c + 1) * 256].rearrange("(k p) n -> p k n", p=128)),
                    (lambda r: r[:, :, 256:512],
                     wi[:, FF + c * 256:FF + (c + 1) * 256].rearrange("(k p) n -> p k n", p=128)))
                for p in range(2):
                    hi, lo = (view(z, (8, 256)) for z in WR[p])
                    tw[p] = split_act(hi, lo, sl[:, :, p * 256:(p + 1) * 256], t, wfree[p])
                slot_free[si] = [tw[0], tw[1]]

            def w_out(c):
                if c % 2 == 0:
                    k = min(4, 22 - 2 * c)
                    outs["w"] = weights((lambda r: r.rearrange("p a b -> p (a b)")[:, 0:1024 * k].rearrange(
                        "p (k n) -> p k n", k=k), wo[256 * c:256 * c + 128 * k, :].rearrange("(k p) n -> p k n", p=128)))
                si, sl, t = outs["w"]
                src = sl.rearrange("p a b -> p (a b)")[:, 2048 * (c % 2):2048 * (c % 2) + 2048]
                hi, lo = WR[2]
                tw[2] = split_act(hi, lo, src, t, wfree[2])
                slot_free[si] = tw[2]

            def inner(c):
                late = []
                for j in range(2):
                    for s, n in enumerate(ns):
                        bk = []
                        for p in range(2):
                            b, ps, fr = B.take()
                            w = lambda part, k: view(WR[p][part], (8, 256))[:, k, j * 128:(j + 1) * 128]
                            x = lambda part, k: HR[s][part][:, k, :]
                            t = mm(b, [(ps[:, 0:n], three(w, x, range(8), hk[s]))], fr, tw[p])
                            bk.append((b, ps, t))
                            if p == 0 and late:
                                late.pop()()
                        wfree[0] = wfree[1] = t

                        def ev(bk=bk, s=s, n=n, j=j):
                            (ba, pa, ta), (bb, pb, tb) = bk
                            i = qn[0] % 2
                            qn[0] += 1
                            t = act(SQ[i][:, 0:n], pa[:, 0:n], ACT.Silu, ta, sqf[i])
                            B.done(ba, t)
                            tg = tt(TG[i][:, 0:n], SQ[i][:, 0:n], pb[:, 0:n], M, t, tb, tgf[i])
                            sqf[i] = tg
                            B.done(bb, tg)
                            hi, lo = (GR_[s][c % 2][p][:, j, :] for p in range(2))
                            t = split(hi, lo, TG[i][:, 0:n], tg, gfree[s][c % 2])
                            tgf[i] = t
                            gtok[s][c % 2] = t
                        late.append(ev)
                return late.pop()

            def outer(c):
                for s, n in enumerate(ns):
                    late = []
                    for m in range(8):
                        b, ps, fr = B.take()
                        w = lambda part, k: view(WR[2][part], (2, 1024))[:, k, m * 128:(m + 1) * 128]
                        x = lambda part, k: GR_[s][c % 2][part][:, k, :]
                        t = mm(b, [(ps[:, 0:n], three(w, x, range(2)))], fr, tw[2], gtok[s][c % 2])
                        if late:
                            late.pop()()
                        late.append(lambda m=m, s=s, o=ps[:, 0:n], t=t, b=b: B.done(b, evac(m, s, o, t)))
                    gfree[s][c % 2] = t
                    late.pop()()
                wfree[2] = t

            hk = prelude(lambda: w_in(0))
            for c in range(12):
                tail = inner(c) if c < 11 else None
                if c == 0:
                    w_out(0)
                if c < 10:
                    w_in(c + 1)
                if c:
                    if tail:
                        tail()
                        tail = None
                    outer(c - 1)
                    if c < 11:
                        w_out(c)
                if tail:
                    tail()

        lfree, pfree, rfree = [None] * 2, [None] * 2, [None] * 4

        def attention(jobs, Lb, Pb, ready, hooks={}):
            state, turned = [], []

            def scores(n):
                segs, _, _, note = jobs[n]
                tn = note() if note else None
                L = Lb[n % 2]
                m = AC[:, 8 * (n % 4):8 * (n % 4) + 8]
                off, info = 0, []
                for g, (q, k, bias) in enumerate(segs):
                    w = k.shape[1]
                    b, ps, fr = B.take()
                    t = mm(b, [(ps[:, 0:w], [(q, k)])], fr, ready)
                    if bias is None:
                        t = DV(lambda e, ps=ps, w=w, g=g: e.reduce_max(m[:, g:g + 1], ps[:, 0:w], AX),
                               t, rfree[n % 4])
                        info.append((ps[:, 0:w], off, w, b))
                    else:
                        t = DV(lambda e, ps=ps, w=w, g=g, off=off, bias=bias: e.tensor_tensor_reduce(
                            L[:, off:off + w], ps[:, 0:w], bias, 1.0, 0.0 - 3e38, A_, ALU.max,
                            m[:, g:g + 1]), t, lfree[n % 2], rfree[n % 4], tn)
                        B.done(b, t)
                        info.append((L[:, off:off + w], off, w, None))
                    off += w
                t = DV(lambda e: e.tensor_reduce(m[:, 3:4], m[:, 0:len(segs)], AX, ALU.max, negate=True), t)
                for g, (src, f, w, b) in enumerate(info):
                    te = act(L[:, f:f + w], src, ACT.Exp, t, lfree[n % 2], bias=m[:, 3:4], accum_out=m[:, 4 + g:5 + g])
                    if b is not None:
                        B.done(b, te)
                state.append((te, off))

            def turn(n):
                te, width = state[n]
                L, P = Lb[n % 2], Pb[n % 2]
                nb = width // 128
                tc = []
                for c in range(0, nb, 4):
                    k = min(4, nb - c)
                    b, ps, fr = B.take()
                    t = tp([(ps[:, i * 128:(i + 1) * 128], L[:, (c + i) * 128:(c + i + 1) * 128])
                            for i in range(k)], fr, te)
                    o_, i_ = P[:, c * 128:(c + k) * 128], ps[:, 0:k * 128]
                    if (c // 4) % 2:
                        t2 = cp(o_, i_, t, pfree[n % 2])
                    else:
                        t2 = act(o_, i_, ACT.Copy, t, pfree[n % 2])
                    B.done(b, t2)
                    tc.append(t2)
                lfree[n % 2] = t
                turned.append(tc)

            def values(n):
                _, vals, o, _ = jobs[n]
                P = Pb[n % 2]
                b, ps, fr = B.take()
                t = mm(b, [(ps[:, 0:64], [(P[:, i * 128:(i + 1) * 128], v) for i, v in enumerate(vals)])],
                       fr, turned[n])
                pfree[n % 2] = t
                m = AC[:, 8 * (n % 4):8 * (n % 4) + 8]
                tr = state[n][0]
                if len(jobs[n][0]) > 1:
                    tr = DV(lambda e: e.reduce_sum(m[:, 4:5], m[:, 4:4 + len(jobs[n][0])], AX), tr)
                tr = DV(lambda e: e.reciprocal(m[:, 3:4], m[:, 4:5]), tr)
                t = ts(o, ps[:, 0:64], m[:, 3:4], None, M, None, t, tr)
                B.done(b, t)
                rfree[n % 4] = t
                return t

            t = None
            for n in range(len(jobs) + 2):
                for h in hooks.get(n, ()):
                    h()
                if n < len(jobs):
                    scores(n)
                if 0 <= n - 1 < len(jobs):
                    turn(n - 1)
                if n >= 2:
                    t = values(n - 2)
            return t

        mrf, MR = [None], [None]

        def mod_piece(l, c):
            w = []

            def half(g):
                si, sl, tw = w[0]
                b, ps, fr = B.take()
                t = mm(b, [(ps[0:2, :], [(SCT[:, k, :], sl[:, k, :]) for k in range(4 * g, 4 * g + 4)])], fr, tw, tsc)
                return si, b, ps[0:2, :], t

            def first():
                w.append(wtile(a["w_mod"][l][:, c * 512:(c + 1) * 512], 8, 512))
                si, b, ps, t = half(0)
                B.done(b, cp(MR[0], ps, t, mrf[0]))

            def second():
                si, b, ps, t = half(1)
                slot_free[si] = t
                t = tt(MR[0], MR[0], ps, A_, t)
                B.done(b, t)
                b, ps, fr = B.take()
                t = tp([(ps[:, 2 * j:2 * j + 2], MR[0][:, j * 128:(j + 1) * 128]) for j in range(4)], fr, t)
                mrf[0] = t
                o = C_BMOD + 48 * l + 4 * c
                t = tt(MODS[l][:, 4 * c:4 * c + 4, :], ps[:, 0:8].rearrange("p (a b) -> p a b", b=2),
                       COL[:, o:o + 4].unsqueeze(2).broadcast_to([128, 4, 2]), A_, t)
                B.done(b, t)
                if c in (2, 3, 8, 9):
                    z = MODS[l][:, 4 * c:4 * c + 4, :]
                    t = ts(z, z, 1.0, None, A_, None, t)
            return first, second

        def finish(*after):
            AE.wait(*after)
            t = AE.dma(lambda e: e.dma_start(out, X[:, :, :]), lane("out"))
            AE.wait(t)

        tk0 = AE.dma(lambda e: e.dma_start(KC[:, :], a["kc"][:, 0:K_RES]), lane("kc"))
        tcol = AE.dma(lambda e: e.dma_start(COL[:, :], a["cols"]), lane("col"))
        tx = AE.dma(lambda e: e.dma_start(X[:, :, :], a["x"]), lane("x"))
        boot = [tk0, tcol, tx]
        for e in (PE, DV, AE, PO):
            e.wait(boot)

        tsc = act(SCT[:, :, :], COL[:, C_C:C_C + 16].rearrange("p (k s) -> p k s", s=2), ACT.Silu)

        GM = arena(0, 8, 128)
        tgm = AE.dma(lambda e: e.dma_start(arena(0, 1024), a["kc"][:, K_GDN:K_GDN + 1024]), lane("gm"))
        o_ = 1024
        rows = [arena(o_ + 512 * n, 512) for n in range(2)]
        o_ += 2 * 512
        GC = arena(o_, 4, 8); o_ += 32
        BT = arena(o_, 4, 8); o_ += 32
        EG = arena(o_, 4, 8); o_ += 32
        KB = arena(o_, 4, 8); o_ += 32
        GL = arena(o_, 4, 8); o_ += 32
        TL = arena(o_, 4, 8); o_ += 32
        CD = arena(o_, 4, 8); o_ += 32
        NE = arena(o_, 8); o_ += 8
        bufs = [o_ + 2048 * n for n in range(10)]
        SO = o_ + 20480
        assert SO + 2048 <= 24960
        rs, res = (arena(bufs[9] + 512 * n, 512)[0:8, :] for n in range(2))
        tres = AE.dma(lambda e: e.dma_start(res, a["kc"][0:8, K_GDN + 1024:K_GDN + 1536]), lane("res"))
        cv = [arena(bufs[8], 516), arena(bufs[8] + 516, 516)]
        th = rms(X, H, C_NMIX, boot)
        wg = a["gdn_w_in"]
        si, sl, tw = weights((lambda r: r[:, :, 0:16],
                              wg[:, 4096:4112].rearrange("(k p) n -> p k n", p=128)))
        ba, pa, fa = B.take()
        bb, pb, fb = B.take()
        ta = mm(ba, [(pa[0:8, :], [(sl[:, k, 0:8], H[:, k, :]) for k in range(8)])], fa, tw, th)
        tb = mm(bb, [(pb[0:8, :], [(sl[:, k, 8:16], H[:, k, :]) for k in range(8)])], fb)
        slot_free[si] = tb
        hr = parts(0, 4096 + SO + 2048, 8, S, None, tb)
        rg, rb = (r[0:8, :] for r in rows)
        dt = COL[0:8, C_DT:C_DT + 1]
        t1 = act(NE[0:8, 0:1], COL[0:8, C_ALOG:C_ALOG + 1], ACT.Exp)
        t2 = act(rs, pa[0:8, :], ACT.Abs, ta, bias=dt)
        t3 = ts(rg, pa[0:8, :], dt, 0.0, A_, ALU.max, t2)
        B.done(ba, t3)
        t2 = act(rs, rs, ACT.Exp, t2, scale=-1.0)
        t2 = act(rs, rs, ACT.Ln, t2, bias=one1[0:8, :])
        t3 = tt(rg, rg, rs, A_, t2, t3)
        t3 = ts(rg, rg, NE[0:8, 0:1], -1.0, M, M, t3, t1)
        t3 = DV(lambda e: e.tensor_tensor_scan(rs, res, rg, 0.0, M, A_), t3, tres)
        tgr = cp(rg, rs, t3)
        t2 = act(rb, pb[0:8, :], ACT.Sigmoid, tb)
        B.done(bb, t2)
        b, ps, fr = B.take()
        t = tp([(ps[:, c * 8:c * 8 + 8], rg[:, c * 128:(c + 1) * 128]) for c in range(4)]
               + [(ps[:, 32 + c * 8:40 + c * 8], rb[:, c * 128:(c + 1) * 128]) for c in range(4)],
               fr, tgr, t2)
        t3 = cp(GC.rearrange("p a b -> p (a b)"), ps[:, 0:32], t)
        t4 = cp(BT.rearrange("p a b -> p (a b)"), ps[:, 32:64], t)
        B.done(b, t4)
        teg = act(EG, GC, ACT.Exp, t3)
        tkb = tt(KB, EG, BT, M, teg, t4)
        tsetup = [t4, tkb]

        def conv(j, dst, ps, t):
            i = cnt.setdefault("cv", 0) % 2
            cnt["cv"] += 1
            c = cv[i]
            w = C_CONV + 4 * j
            fr = cvf[i]
            t0 = PO(lambda e, c=c: e.memset(c[:, 0:3], 0.0), fr, tgr, hold)
            tc = act(c[:, 3:515], ps, ACT.Copy, t, fr, tgr, hold)
            tv = ts(dst, c[:, 3:515], col(w + 3), None, M, None, tc, t0, hold)
            for n in (2, 1, 0):
                tv = stt(dst, c[:, n:n + 512], col(w + n), dst, M, A_, tv)
            cvf[i] = tv
            act(dst, dst, ACT.Silu, tv)
            return tc

        cvf = [None, None]
        for hg in range(2):
            hold = last() if hg else None
            wh_at(4096 + bufs[3], *last())
            bf = [arena(o, 4, 512) for o in bufs]
            q, k, v, vb, kbe, ktl, DT, Xb, AT, qk = bf
            T, TT = v, k
            tp_ = None
            chain([linear3(wg[:, which * 1024 + hg * 512:which * 1024 + (hg + 1) * 512], 8, [hr],
                           lambda j, s, ps, t, which=which, dst=dst: conv(which * 8 + hg * 4 + j, dst[:, j, :], ps, t))
                   for which, dst in ((0, q), (1, k), (2, v))])
            tsil = (AE.sem, AE.n)
            ends = []
            for h in range(4):
                hh = hg * 4 + h
                for x_, scale, eps in ((q, 128.0, None), (k, 1.0, e1)):
                    b, ps, t = sumsq([x_[:, h, :]], 512, ones, tsil)
                    if eps is None:
                        i, r, t = rstd(ps, b, 512, 128.0, e128, t)
                    else:
                        i, r, t = rstd(ps, b, 512, 1.0, e1, t)
                    t = tt(x_[:, h, :], x_[:, h, :], r, M, t)
                    rrf[i] = t
                tn = t
                b, ps, fr = B.take()
                t = mm(b, [(ps[:, :], [(ident[0:8, hh:hh + 1].broadcast_to([8, 128]), rb)])], fr, tsetup)
                t = tt(Xb[:, h, :], k[:, h, :], ps[:, :], M, t, tn)
                B.done(b, t)
                b, ps, fr = B.take()
                t = mm(b, [(ps[:, :], [(ident[0:8, hh:hh + 1].broadcast_to([8, 128]), rg)])], fr)
                t4 = cp(GL[:, :, hh], ps.rearrange("p (a b) -> p a b", a=4)[:, :, 127], t)
                for c in range(4):
                    t4 = ts(DT[:, h, c * 128:(c + 1) * 128], ps[:, c * 128:(c + 1) * 128], GC[:, c, hh:hh + 1],
                            0.0, ALU.subtract, ALU.min, t)
                i = cnt["rr"] % 2
                cnt["rr"] += 1
                te = act(RR[i][:, :], ps[:, :], ACT.Exp, t4, rrf[i])
                B.done(b, te)
                td = act(DT[:, h, :], DT[:, h, :], ACT.Exp, t4)
                td = tt(DT[:, h, :].rearrange("p (a b) -> p a b", a=4), DT[:, h, :].rearrange("p (a b) -> p a b", a=4),
                        GM[:, 7:8, :].broadcast_to([128, 4, 128]), M, td, tgm)
                b, ps, fr = B.take()
                t = mm(b, [(ps[:, c * 128:(c + 1) * 128], [(k[:, h, c * 128:(c + 1) * 128],
                                                            Xb[:, h, c * 128:(c + 1) * 128])])
                           for c in range(4)], fr, (DV.sem, DV.n))
                ta_ = tt(AT[:, h, :], ps[:, :], DT[:, h, :], M, t, td)
                B.done(b, ta_)
                b, ps, fr = B.take()
                t = mm(b, [(ps[:, c * 128:(c + 1) * 128], [(k[:, h, c * 128:(c + 1) * 128],
                                                            q[:, h, c * 128:(c + 1) * 128])])
                           for c in range(4)], fr)
                t5 = tt(qk[:, h, :], ps[:, :], DT[:, h, :], M, t)
                B.done(b, t5)
                t6 = tt(q[:, h, :], q[:, h, :], RR[i][:, :], M, t, te)
                rrf[i] = t6
                ends += [t5, t6, ta_]
            h0 = hg * 4
            t = tt(TL[:, :, h0:h0 + 4], GL[:, :, h0:h0 + 4], GC[:, :, h0:h0 + 4], ALU.subtract, t4)
            t1 = act(TL[:, :, h0:h0 + 4], TL[:, :, h0:h0 + 4], ACT.Exp, t)
            t2 = act(CD[:, :, h0:h0 + 4], GL[:, :, h0:h0 + 4], ACT.Exp, t)
            kv = []
            for c in range(4):
                b, ps, fr = B.take()
                t = tp([(ps[:, h * 128:(h + 1) * 128], v[:, h, c * 128:(c + 1) * 128]) for h in range(4)], fr)
                p4 = ps[:, :].rearrange("p (a b) -> p a b", a=4)
                as4 = lambda z: z[:, c, :].rearrange("p (a b) -> p a b", a=4)
                bc = lambda z: z[:, c, h0:h0 + 4].unsqueeze(2).broadcast_to([128, 4, 128])
                t = tt(as4(vb), p4, bc(BT), M, t)
                B.done(b, t)
                kv.append(t)
                b, ps, fr = B.take()
                t = tp([(ps[:, h * 128:(h + 1) * 128], k[:, h, c * 128:(c + 1) * 128]) for h in range(4)], fr)
                p4 = ps[:, :].rearrange("p (a b) -> p a b", a=4)
                t_ = tt(as4(kbe), p4, bc(KB), M, t)
                t = tt(as4(ktl), p4, bc(TL), M, t, t1)
                B.done(b, t)
                kv.append(t)
            free3 = [(PE.sem, PE.n)]
            tT = [kv] * 4
            c4 = lambda z, h: z[:, h, :].rearrange("p (a b) -> p a b", a=4)
            p4 = lambda ps: ps[:, :].rearrange("p (a b) -> p a b", a=4)
            at_ = lambda z, h, c: z[:, h, c * 128:(c + 1) * 128]
            idb = ident.unsqueeze(1).broadcast_to([128, 4, 128])

            def masked(n, h):
                b, ps, fr = B.take()
                t = mm(b, [(ps[:, c * 128:(c + 1) * 128], [(at_(AT, h, c), at_(T, h, c) if n else ident)])
                           for c in range(4)], fr, tT[h], ends)
                t = tt(c4(Xb, h), p4(ps), GM[:, n:n + 1, :].broadcast_to([128, 4, 128]), M, t, tT[h])
                B.done(b, t)
                return t

            def level(n, h, tx_):
                tt_ = lambda c: at_(TT, h, c) if n else ident
                b2, ps2, fr2 = B.take()
                t = mm(b2, [(ps2[:, c * 128:(c + 1) * 128], [(at_(Xb, h, c), tt_(c))]) for c in range(4)], fr2, tx_)
                res_ = []
                if n < 6:
                    b1, ps1, fr1 = B.take()
                    t = mm(b1, [(ps1[:, c * 128:(c + 1) * 128], [(tt_(c), at_(Xb, h, c))]) for c in range(4)], fr1)
                    t1_ = tt(c4(T, h), c4(T, h) if n else idb, p4(ps1), ALU.subtract, t, free3)
                    B.done(b1, t1_)
                    res_.append(t1_)
                t2_ = tt(c4(TT, h), c4(TT, h) if n else idb, p4(ps2), ALU.subtract, t, free3)
                B.done(b2, t2_)
                tT[h] = res_ + [t2_]
            steps = [(n, h) for n in range(7) for h in range(4)]
            nxt = masked(0, 0)
            for i, (n, h) in enumerate(steps):
                tm_ = nxt
                if i + 1 < len(steps):
                    nxt = masked(*steps[i + 1])
                level(n, h, tm_)
            W = DT
            tw_ = []
            for h in range(4):
                b, ps, fr = B.take()
                t = mm(b, [(ps[:, c * 128:(c + 1) * 128], [(kbe[:, c, h * 128:(h + 1) * 128],
                                                            TT[:, h, c * 128:(c + 1) * 128])])
                           for c in range(4)], fr, tT[h])
                t = act(W[:, h, :], ps[:, :], ACT.Copy, t, scale=-1.0)
                B.done(b, t)
                tw_.append(t)
            SS = [Xb[:, 0, :], Xb[:, 1, :]]
            VN = [Xb[:, 2, :], Xb[:, 3, :]]
            oraw = T
            ts_, tvn = None, None
            for c in range(4):
                Sc, Sn, vn = SS[c % 2], SS[(c + 1) % 2], VN[c % 2]
                hs4 = lambda z, h: z[:, h * 128:(h + 1) * 128]
                b, ps, fr = B.take()
                t = mm(b, [(hs4(ps, h), [(TT[:, h, c * 128:(c + 1) * 128], hs4(vb[:, c, :], h))]
                            + ([(W[:, h, c * 128:(c + 1) * 128], hs4(Sc, h))] if c else []))
                           for h in range(4)], fr, tw_, ts_, tT)
                tvn = act(vn, ps[:, :], ACT.Copy, t)
                B.done(b, tvn)
                if c < 3:
                    b, ps, fr = B.take()
                    t = mm(b, [(hs4(ps, h), [(hs4(ktl[:, c, :], h), hs4(vn, h))]) for h in range(4)], fr, tvn)
                    if c == 0:
                        ts_ = cp(Sn, ps, t)
                    else:
                        for h in range(4):
                            ts_ = stt(hs4(Sn, h), hs4(Sc, h), CD[:, c, h0 + h:h0 + h + 1], hs4(ps, h), M, A_, t, t2)
                    B.done(b, ts_)
                b, ps, fr = B.take()
                t = mm(b, [(hs4(ps, h), ([(hs4(Sc, h), q[:, h, c * 128:(c + 1) * 128])] if c else [])
                            + [(hs4(vn, h), qk[:, h, c * 128:(c + 1) * 128])])
                           for h in range(4)], fr, tvn)
                t = act(oraw[:, :, c * 128:(c + 1) * 128], ps[:, :].rearrange("p (a b) -> p a b", a=4), ACT.Copy, t)
                B.done(b, t)
            Z = AT

            def zev(j, s, ps, t):
                return act(Z[:, j, :], ps, ACT.Silu, t)
            wh_at(4096 + bufs[3], *last())
            chain([linear3(wg[:, 3072 + hg * 512:3072 + (hg + 1) * 512], 8, [hr], zev)])
            tz = (AE.sem, AE.n)
            O = arena((SO, bufs[0])[hg], 4, 512)
            for h in range(4):
                b, ps, t = sumsq([oraw[:, h, :]], 512, ones, tz)
                i, r, t = rstd(ps, b, 512, 1.0 / 128, e1, t)
                t = tt(oraw[:, h, :], oraw[:, h, :], r, M, t)
                rrf[i] = t
                t = stt(O[:, h, :], oraw[:, h, :], col(C_GNW), Z[:, h, :], M, M, t)

        def add_x(j, s, ps, t):
            return tt(X[:, j, :], X[:, j, :], ps, A_, t)

        after = last()
        p0, p1 = (parts(o, 4096 + bufs[5 + n], 4, S, None, after) for n, o in enumerate((4096 + SO, 4096 + bufs[0])))
        wh_at(4096 + bufs[7], *after)
        chain([linear3(a["gdn_w_out"], 8, [(Pair(p0[0], p1[0]), Pair(p0[1], p1[1]), S, p0[3] + p1[3])], add_x)])

        def ffn1(l):
            def prelude(mid):
                fence()
                b, ps, t = sumsq([X[:, k, :] for k in range(8)], S, ones, (DV.sem, DV.n))
                mid()
                i, r, t = rstd(ps, b, S, 1.0 / D, e1, t)
                tk = [stt(HT[0][:, k, :], X[:, k, :], col(C_NFFN + 8 * l + k), r, M, M, t) for k in range(8)]
                rrf[i] = tk[-1]
                return [[to_parts(0, k, t) for k, t in enumerate(tk)]]
            ffn(a["ffn_w_in"][l], a["ffn_w_out"][l], [S], add_x, prelude)

        ffn1(0)

        fence()
        tq = last()
        QD, KD, VD = arena(0, 12, 512), arena(6144, 12, 512), arena(12288, 4, 1536)
        DI = arena(18432, 1280)
        PB = [arena(19712, 1280), arena(20992, 1280)]
        BI2 = arena(22272, 1280)
        tdi = AE.dma(lambda e: e.dma_start(DI, a["kc"][:, K_DIL:K_DIL + N_DIL]), lane("di"), tq)
        th = rms(X, H, C_NMIX + 8, (DV.sem, DV.n))
        wd = a["dil_w_in"]

        def headnorm(dst, ps, n, g, scale, eps, t):
            b, p2, t = sumsq([ps], n, bones, t)
            i, r, t = rstd(p2, b, n, scale, eps, t)
            t = stt(dst, ps, g, r, M, M, t)
            rrf[i] = t
            return t

        hr = parts(0, 4096 + 19712, 8, S, None, th)
        hs = [hr]
        wh_at(4096 + 19712 + 4096, *tq)
        chain([linear3(wd[:, 0:1536], 8, hs,
                       lambda j, s, ps, t: headnorm(QD[:, j, :], ps, 512, col(C_DQ), 1.0, e64, t)),
               linear3(wd[:, 1536:3072], 8, hs,
                       lambda j, s, ps, t: headnorm(KD[:, j, :], ps, 512, col(C_DK), 1.0 / 64, e1, t))]
              + [linear_tok3(wd[:, 3072 + c * 512:3072 + (c + 1) * 512], hs,
                             lambda qt, s, ps, t, c=c: act(VD[:, qt, c * 512:(c + 1) * 512], ps, ACT.Copy, t))
                 for c in range(3)])
        tv = [(AE.sem, AE.n), (DV.sem, DV.n), (PE.sem, PE.n)]
        HF = H[:, :, :].rearrange("p a b -> p (a b)")
        BI = [HF[:, 0:1280], BI2]
        LB = [HF[:, 1280:2560], HF[:, 2560:3840]]
        OTK = [arena(23552, 512), arena(24064, 512), SQ[0], SQ[1]]
        bt = {}

        def dil_bias(h, *after):
            t = None
            for g, (o0, o1) in enumerate(((0, 256), (256, 768), (768, 1280))):
                slope = float(2.0 ** (-8.0 * (g * 8 + h + 1) / 24))
                t = act(BI[h % 2][:, o0:o1], DI[:, o0:o1], ACT.Copy, tdi, tv, *after, scale=slope)
            bt[h] = t

        jobs, hooks = [], {}
        dil_bias(0)
        for h in range(8):
            if h < 7:
                hooks.setdefault(4 * h + 2, []).append(lambda h=h: dil_bias(h + 1, (DV.sem, DV.n)))
            pb_ = 64 * (h % 2)
            for qt in range(4):
                k0 = max(0, qt - 1)
                segs, vals = [], []
                for g, (lo, full) in enumerate(((k0, 256), (0, 512), (0, 512))):
                    tile = g * 4 + h // 2
                    w = (qt + 1 - lo) * 128
                    base = (0, 256, 768)[g] + full - w
                    segs.append((QD[pb_:pb_ + 64, tile, qt * 128:(qt + 1) * 128],
                                 KD[pb_:pb_ + 64, tile, lo * 128:(qt + 1) * 128],
                                 BI[h % 2][:, base:base + w]))
                    vals += [VD[:, kt, g * 512 + h * 64:g * 512 + (h + 1) * 64] for kt in range(lo, qt + 1)]
                jobs.append((segs, vals, OTK[qt][:, h * 64:(h + 1) * 64], lambda h=h: bt[h]))
        MR[0] = arena(24576, 512)[0:2, :]

        def mod_hooks(l, step, hooks=hooks):
            n = 0.0
            for c in range(12):
                for f in mod_piece(l, c):
                    hooks.setdefault(int(n), []).append(f)
                    n += step
        mod_hooks(0, 1.3)
        to = attention(jobs, LB, PB, tv, hooks)
        OF = arena(0, 4, 512)
        tf = None
        fr_ = (PE.sem, PE.n)
        for j in range(4):
            b, ps, fr = B.take()
            t = tp([(ps[:, q * 128:(q + 1) * 128], OTK[q][:, j * 128:(j + 1) * 128]) for q in range(4)], fr, to)
            tf = act(OF[:, j, :], ps[:, :], ACT.Copy, t, fr_)
            sqf[0] = sqf[1] = t
            B.done(b, tf)
        tv = last()
        hr = parts(4096, 4096 + 2048, 4, S, None, tv)
        wh_at(4096 + 4096, *tv)
        chain([linear3(a["dil_w_out"], 4, [hr], add_x)])
        ffn1(1)

        fence()
        tq = last()
        XC = view(U[:, UN - 2048:UN], (8, LC))
        HC = view(U[:, UN - 4096:UN - 2048], (8, LC))
        AMAX = UN - 4096 - 4096
        txc = AE.dma(lambda e: e.dma_start(XC, a["ctx"]), lane("xc"), tq)
        tX, tXC = tq, txc

        def scaled(streams, read):
            for x, t in zip(streams, read):
                for k in range(8):
                    if k % 2:
                        ta = act(x[:, k, :], x[:, k, :], ACT.Copy, t, scale=ALPHA)
                    else:
                        tp_ = ts(x[:, k, :], x[:, k, :], ALPHA, 1.0, M, M, t, e=PO)
            return [ta, tp_]

        for l in range(2):
            MOD, tmod = MODS[l], (DV.sem, DV.n)
            mod = lambda g, s: (lambda k: MOD[:, 8 * g + k, s:s + 1])
            tq = fence()
            o = 0
            def take(*shape):
                nonlocal o
                v = arena(o, *shape)
                o += int(np.prod(shape))
                assert o <= AMAX, o
                return v
            QA, QAX, KA, KAX = take(3, S), take(3, LC), take(3, S), take(3, LC)
            VA, VAX = take(4, 384), take(2, 384)
            ZB, ZBX = take(4, 512), take(2, 512)
            QC, QCX, KCx, KCX = take(3, S), take(3, LC), take(1, S), take(1, LC)
            VC, VCX = take(4, 128), take(2, 128)
            NM = take(N_NA)
            WS = take(4, 128)
            GS = take(256)
            spare = 4096 + o
            EB = [take(14, 64), take(14, 64)]
            LB = [take(768), take(768)]
            PB = [take(768), take(768)]
            MR[0] = take(512)[0:2, :]
            STS, SG, SCR = take(6, 24), take(24), take(384)
            assert spare + 4096 + 2048 + 3072 <= 4096 + AMAX
            CO, SI, RM, FL = NM[:, 64:576], NM[:, 576:1088], NM[:, 1088:1216], NM[:, 1216:1344]
            tnm = AE.dma(lambda e: e.dma_start(NM, a["kc"][:, K_NA:K_NA + N_NA]), lane("nm"), tq)
            tws = AE.dma(lambda e, l=l: e.dma_start(WS, a["w_sT"][l]), lane("ws"))
            tgs = AE.dma(lambda e, l=l: e.dma_start(
                GS, a["g_sgu"][l:l + 1, :].broadcast_to([128, 256])), lane("gs"))
            w = a["w_in"][l]
            HP = [[view(ru(o, 8 * n), (8, n)) for o in (hi, lo)]
                  for hi, lo, n in ((spare, 0, S), (spare + 4096, UN - 4096, LC))]

            def halves(s, k, t):
                return (split_act if k % 2 else split)(HP[s][0][:, k, :], HP[s][1][:, k, :], (H, HC)[s][:, k, :], t)
            AE.wait(tmod)
            tk, read = layernorm([(X, H, S, mod(1, 0), mod(0, 0), tX), (XC, HC, LC, mod(1, 1), mod(0, 1), tXC)],
                                 e1, None, halves)
            hr, hx = ((*HP[s], (S, LC)[s], tk[s]) for s in range(2))
            held = [scaled((X, XC)[:2 - l], read)]
            wh_at(spare + 6144, *tq)
            both = [hr, hx]
            qs = both if l == 0 else both[:1]
            calls = [
                linear3(w[:, 0:384], 8, qs,
                        lambda j, s, ps, t: act((QA, QAX)[s][:, j, :], ps, ACT.Copy, t, scale=0.125)),
                linear3(w[:, 384:768], 8, both, lambda j, s, ps, t: act((KA, KAX)[s][:, j, :], ps, ACT.Copy, t)),
                linear_tok3(w[:, 768:1152], both, lambda q, s, ps, t: act((VA, VAX)[s][:, q, :], ps, ACT.Copy, t))]
            kp = lambda v: v.rearrange("(k p) n -> p k n", p=128)
            load = lambda: weights(*[
                (lambda r, j=j, g=g: r[:, :, j * 128 + g * 64:j * 128 + (g + 1) * 64],
                 kp(w[:, 1664 + g * 192 + j * 64:1664 + g * 192 + (j + 1) * 64]))
                for j in range(3) for g in range(2)], (lambda r: r[:, :, 384:512], kp(w[:, 2048:2176])))

            def turned(j, s, ps, t):
                n = (S, LC)[s]
                dst = ((QC, QCX)[s][:, j, :] if j < 3 else (KCx, KCX)[s][:, 0, :])
                g, sc, ep = (C_GQ + l, 1.0, e64) if j < 3 else (C_GK + l, 1.0 / 64, e1)
                tn = headnorm(dst, ps, n, col(g), sc, ep, t)
                if s == 0:
                    b, ps, fr = B.take()
                    t = mm(b, [(ps[:, :], [(RM, dst)])], fr, tn, tnm)
                    i = cnt["rr"] % 2
                    cnt["rr"] += 1
                    t = tt(RR[i][:, :], ps[:, :], SI, M, t, rrf[i])
                    B.done(b, t)
                    t2 = tt(dst, dst, CO, M, t)
                    rrf[i] = tt(dst, dst, RR[i][:, :], A_, t2)
                return tn
            calls += [
                Products([(load, [qs + [None]] * 3 + [both])], 8, turned),
                linear_tok3(w[:, 2176:2304], both, lambda q, s, ps, t: act((VC, VCX)[s][:, q, :], ps, ACT.Copy, t)),
                linear_tok3(w[:, 1152:1664], qs,
                            lambda q, s, ps, t: act((ZB, ZBX)[s][:, q, :], ps, ACT.Gelu_apprx_tanh, t))]
            chain(calls)
            tv = last()
            OT = H[:, :, :].rearrange("p a b -> p (a b)").rearrange("p (a b) -> p a b", a=4)
            OTX = HC.rearrange("p a b -> p (a b)").rearrange("p (a b) -> p a b", a=2)
            outs = [(0, OT, q) for q in range(4)] + ([(1, OTX, q) for q in range(2)] if l == 0 else [])

            def gating(n):
                s, ot, q = outs[n]
                zb = (ZB, ZBX)[s]
                ST, vv, st = STS[:, n, :], zb[:, q, 256:512], []

                def first():
                    t = DV(lambda e: e.bn_stats(ST[:, 0:6], vv), tv)
                    t = DV(lambda e: e.bn_aggr(ST[:, 16:18], ST[:, 0:6]), t)
                    t1 = act(ST[:, 18:19], ST[:, 17:18], ACT.Ln, t, tv, bias=e1)
                    t1 = act(ST[:, 18:19], ST[:, 18:19], ACT.Exp, t1, scale=-0.5)
                    st.append(t1)

                def second():
                    t = ts(vv, vv, ST[:, 16:17], ST[:, 18:19], ALU.subtract, M, st[0])
                    st.append(tt(vv, vv, GS, M, t, tgs))

                def third():
                    b, ps, fr = B.take()
                    t = mm(b, [(ps[:, g * 64:(g + 1) * 64], [(WS[:, g, :], vv[:, g * 64:(g + 1) * 64])])
                               for g in range(4)], fr, st[1], tws)
                    for g in range(4):
                        t2 = stt(ot[:, q, 384 + g * 64:384 + (g + 1) * 64], ps[:, g * 64:(g + 1) * 64],
                                 col(C_BS + 4 * l + g), zb[:, q, g * 64:(g + 1) * 64], A_, M, t, tv)
                    B.done(b, t2)
                return first, second, third

            def group_norm(lo, hi, c0):
                m = len(outs)
                cc, st = SG[:, c0:c0 + m], []

                def first():
                    for n, (s, ot, q) in enumerate(outs):
                        t = act(SCR[:, 0:hi - lo], ot[:, q, lo:hi], ACT.Square, (DV.sem, DV.n), (AE.sem, AE.n), tv,
                                accum_out=cc[:, n:n + 1])
                    t = act(cc, cc, ACT.Ln, t, scale=1.0 / (hi - lo), bias=e1)
                    st.append(act(cc, cc, ACT.Exp, t, scale=-0.5))

                def second():
                    for n, (s, ot, q) in enumerate(outs):
                        t = ts(ot[:, q, lo:hi], ot[:, q, lo:hi], cc[:, n:n + 1], None, M, None, st[0])
                    st.append(t)
                return first, second, lambda: st[1]

            MG, MGX = arena(0, 8, S), arena(4096, 8, LC)
            tmg = [[None] * 8, [None] * 8]

            def back(k, tn, *after):
                for s, (ot, mg, nt) in enumerate(((OT, MG, 4), (OTX, MGX, 2))[:2 - l]):
                    b, ps, fr = B.take()
                    t = tp([(ps[:, q * 128:(q + 1) * 128], ot[:, q, k * 128:(k + 1) * 128]) for q in range(nt)],
                           fr, tn())
                    t = act(mg[:, k, :], ps[:, 0:nt * 128], ACT.Copy, t, *after, scale=col(C_GOUT + 8 * l + k))
                    B.done(b, t)
                    tmg[s][k] = t
            bl, bt = {}, {}

            def bias_load(h, fr):
                for r in range(2):
                    base = ((l * 6 + h) * 15 + (1 - r)) * 127
                    src = bass.AP(a["rpb"].tensor, base, [[1, 64], [127, 14], [1, 64]])
                    bl[h] = SP.dma(lambda e, src=src, r=r, h=h: e.dma_start(EB[h % 2][64 * r:64 * r + 64, :, :], src),
                                   lane(f"rpb{h % 2}"), fr)

            def bias_turn(h):
                pair = []
                for c in range(2):
                    b, ps, fr = B.take()
                    t = mm(b, [(ps[:, 0:448], [(FL, EB[h % 2][:, 7 * c:7 * c + 7, :])])], fr, bl[h], tnm)
                    pair.append((b, ps))
                for c, (b, ps) in enumerate(pair):
                    bt[h] = tt(EB[h % 2][:, 7 * c:7 * c + 7, :], ps[:, 0:448].rearrange("p (a b) -> p a b", a=7),
                               NM[:, 0:64].unsqueeze(1).broadcast_to([128, 7, 64]), A_, t)
                    B.done(b, bt[h])
            for h in range(2):
                bias_load(h, tv)
                bias_turn(h)
            jobs, hooks = [], {}
            for h in range(6):
                pb_, tile = 64 * (h % 2), h // 2
                E = EB[h % 2].rearrange("p a b -> p (a b)")
                kx = KAX[pb_:pb_ + 64, tile, :]
                hv = slice(h * 64, (h + 1) * 64)
                if 1 <= h < 5:
                    hooks[len(jobs) + 1] = [lambda h=h: bias_load(h + 1, (DV.sem, DV.n))]
                    hooks[len(jobs) + 3] = [lambda h=h: bias_turn(h + 1)]
                for q in range(4):
                    qv = QA[pb_:pb_ + 64, tile, q * 128:(q + 1) * 128]
                    jobs.append(([(qv, KA[pb_:pb_ + 64, tile, :], E[:, (6 - 2 * q) * 64:(14 - 2 * q) * 64]),
                                  (qv, kx, None)],
                                 [VA[:, t_, hv] for t_ in range(4)] + [VAX[:, t_, hv] for t_ in range(2)],
                                 OT[:, q, hv], lambda h=h: bt[h]))
                if l == 0:
                    for q in range(2):
                        jobs.append(([(QAX[pb_:pb_ + 64, tile, q * 128:(q + 1) * 128], kx, None)],
                                     [VAX[:, t_, hv] for t_ in range(2)], OTX[:, q, hv], None))
            n1 = len(jobs) + 2
            for h in range(6):
                g, tile = h // 3, h % 3
                pb_ = 64 * g
                hv = slice(g * 64, (g + 1) * 64)
                ov = slice(640 + h * 64, 640 + (h + 1) * 64)
                kk, kx = KCx[pb_:pb_ + 64, 0, :], KCX[pb_:pb_ + 64, 0, :]
                for q in range(4):
                    qv = QC[pb_:pb_ + 64, tile, q * 128:(q + 1) * 128]
                    jobs.append(([(qv, kk, None), (qv, kx, None)],
                                 [VC[:, t_, hv] for t_ in range(4)] + [VCX[:, t_, hv] for t_ in range(2)],
                                 OT[:, q, ov], None))
                if l == 0:
                    for q in range(2):
                        jobs.append(([(QCX[pb_:pb_ + 64, tile, q * 128:(q + 1) * 128], kx, None)],
                                     [VCX[:, t_, hv] for t_ in range(2)], OTX[:, q, ov], None))
            add = lambda n, f: hooks.setdefault(n, []).append(f)
            for n in range(len(outs)):
                for i, f in enumerate(gating(n)):
                    add(2 + 3 * n + i, f)
            g1, g2, g3 = group_norm(384, 640, 0), group_norm(0, 384, 6), group_norm(640, 1024, 12)
            add(n1, g1[0])
            add(n1 + 1, g1[1])
            add(n1 + 1, g2[0])
            add(n1 + 2, g2[1])
            for k in range(5):
                add(n1 + 4 + 2 * k, lambda k=k: back(k, (g2, g1)[k > 2][2], read_[0]))
            read_ = []
            add(n1 + 3, lambda: read_.append((PE.sem, PE.n)))
            if l == 0:
                mod_hooks(1, 2.5, hooks)
            attention(jobs, LB, PB, tv, hooks)
            tq = tq_ = fence()
            g3[0]()
            g3[1]()
            for k in range(5, 8):
                back(k, g3[2], tq)
            def gated(g):
                def evac(j, s, ps, t):
                    x = (X, XC)[s][:, j, :]
                    return stt(x, ps, MOD[:, 8 * g + j, s:s + 1], x, M, A_, t, held[-1])
                return evac
            m1 = parts(4096, 4096 + 6144, 8, S, tmg[0], tq_)
            m2 = parts(8192, 4096 + 10240, 8, LC, tmg[1], tq_) if l == 0 else None
            wh_at(4096 + 12288, *tq_)
            chain([linear3(a["w_o"][l], 8, [m1, m2], gated(2))])


            def post(n_):
                c0 = C_LN + 32 * l + 16 * n_
                tq = (DV.sem, DV.n)
                gb = (lambda k: col(c0 + k)), (lambda k: col(c0 + 8 + k))
                r, _ = layernorm([(x, x, n) + gb + (tq,) for x, n in ((X, S), (XC, LC))[:2 - l]], e1)
                return [t[-1] for t in r]
            tt_ = post(0)

            def prelude(mid):
                fence()
                r, read = layernorm([(x, HT[s], (S, LC)[s], mod(4, s), mod(3, s), tt_[s])
                                     for s, x in enumerate((X, XC)[:2 - l])], e1, mid, to_parts)
                held.append(scaled((X, XC)[:2 - l], read))
                return r
            ffn(a["w_ffn_in"][l], a["w_ffn_out"][l], [S, LC][:2 - l], gated(5), prelude)
            tt_ = post(1)
            tX, tXC = tt_[0], tt_[-1]
        finish((AE.sem, AE.n), (PO.sem, PO.n), (DV.sem, DV.n))
        return emit(nc, ctx, PE, DV, AE, PO, SP)


def emit(nc, ctx, PE, DV, AE, PO, SP):
    block = ctx.enter_context(nc.Block())

    @block.sync
    def _(eng):
        SP.emit(eng)

    @block.tensor
    def _(eng):
        PE.emit(eng)

    @block.vector
    def _(eng):
        DV.emit(eng)

    @block.scalar
    def _(eng):
        AE.emit(eng)

    @block.gpsimd
    def _(eng):
        PO.emit(eng)


def layout(i):
    f = np.float32
    A = {k: np.ascontiguousarray(v) for k, v in i.items()}

    def feat(v, n=8):
        return v.reshape(n, 128).T

    c = np.zeros((128, NCOL), f)
    for l in range(2):
        c[:, C_NMIX + 8 * l:C_NMIX + 8 * l + 8] = feat(A["norm_mix"][l])
        c[:, C_NFFN + 8 * l:C_NFFN + 8 * l + 8] = feat(A["norm_ffn"][l])
        c[:, C_BMOD + 48 * l:C_BMOD + 48 * l + 48] = feat(A["b_mod_2"][l], 48)
        for h in range(2):
            c[64 * h:64 * h + 64, C_GQ + l] = A["g_q_2"][l]
            c[64 * h:64 * h + 64, C_GK + l] = A["g_k_2"][l]
        c[:, C_GOUT + 8 * l:C_GOUT + 8 * l + 8] = feat(A["g_out_2"][l])
        for n, k in enumerate(("ln1_g_2", "ln1_b_2", "ln2_g_2", "ln2_b_2")):
            o = C_LN + 32 * l + 8 * n
            c[:, o:o + 8] = feat(A[k][l])
        c[:, C_BS + 4 * l:C_BS + 4 * l + 4] = A["b_s_2"][l].T
    c[:, C_GNW] = A["gdn_norm_w"][0]
    c[:, C_CONV:C_CONV + 96] = A["gdn_conv_w"][0].reshape(4, 24, 128).transpose(2, 1, 0).reshape(128, 96)
    for h in range(2):
        c[64 * h:64 * h + 64, C_DQ] = A["dil_q_norm"][0]
        c[64 * h:64 * h + 64, C_DK] = A["dil_k_norm"][0]
    c[0:8, C_ALOG] = A["gdn_a_log"][0]
    c[0:8, C_DT] = A["gdn_dt_bias"][0]
    cc = np.stack([feat(A["c_2"][0]), feat(A["c_ctx_2"])], axis=2)
    c[:, C_C:C_C + 16] = cc.reshape(128, 16)
    rpb = np.zeros((2, 6, 15, 127), f)
    rpb[:, :, :, 48:79] = A["rpb_2"]
    return {
        "x": np.ascontiguousarray(A["x"][0].T.reshape(8, 128, S).transpose(1, 0, 2)),
        "ctx": np.ascontiguousarray(A["ctx_2"][0].T.reshape(8, 128, LC).transpose(1, 0, 2)),
        "cols": c, "kc": constants(), "rpb": rpb,
        "gdn_w_in": A["gdn_w_in"][0], "gdn_w_out": A["gdn_w_out"][0],
        "dil_w_in": A["dil_w_in"][0], "dil_w_out": A["dil_w_out"][0],
        "ffn_w_in": A["ffn_w_in"], "ffn_w_out": A["ffn_w_out"],
        "w_mod": A["w_mod_2"], "w_in": A["w_in_2"], "w_o": A["w_o_2"],
        "w_ffn_in": A["w_ffn_in_2"], "w_ffn_out": A["w_ffn_out_2"],
        "w_sT": np.ascontiguousarray(A["w_s_2"].transpose(0, 3, 1, 2)),
        "g_sgu": A["g_sgu_2"],
    }


def kernel(**inputs):
    import concourse.bacc as bacc
    from concourse.bass_utils import run_bass_kernel_spmd

    arrays = layout({k: np.asarray(v) for k, v in inputs.items()})
    nc = bacc.Bacc("TRN2", target_bir_lowering=False, num_devices=1)
    aps = {k: nc.dram_tensor("in_" + k, v.shape, F32, kind="ExternalInput").ap() for k, v in arrays.items()}
    out = nc.dram_tensor("out_0", (128, 8, S), F32, kind="ExternalOutput").ap()
    build(nc, aps, out)
    r = run_bass_kernel_spmd(nc, [{"in_" + k: v for k, v in arrays.items()}], core_ids=[0])
    y = np.asarray(r.results[0]["out_0"])
    return y.transpose(2, 1, 0).reshape(1, S, D)
```
